# Optimizing a Trainium2 kernel written in Bass

```python
import jax
import jax.numpy as jnp
from jax import lax
import numpy as np

D_MODEL = 1024
BATCH = 1
SEQ = 256
DEPTH = 1

CHUNK = 64
N_META = 16
Q_BLOCK = 128
ROPE_THETA = 10000.0
NORM_EPS = 1e-6
NEG_INF = -1e30

FOX_HEADS = 8
FOX_HEAD_DIM = 64
DSA_HEADS = 8
Q_RANK = 256
KV_RANK = 128
QK_NOPE_DIM = 64
QK_ROPE_DIM = 32
V_HEAD_DIM = 64
IDX_HEADS = 4
IDX_HEAD_DIM = 64
IDX_ROPE_DIM = 32
IDX_TOPK_MAX = 256
N_EXPERTS = 32
TOP_K = 4
D_EXPERT = D_MODEL
SWIGLU_ALPHA = 1.702
SWIGLU_LIMIT = 7.0
EXPERT_BLOCK = 128

FOX_WIDTH = FOX_HEADS * FOX_HEAD_DIM
DSA_WIDTH = DSA_HEADS * V_HEAD_DIM
IN_SPLITS = (FOX_WIDTH, FOX_WIDTH, FOX_WIDTH, FOX_HEADS, Q_RANK, KV_RANK, QK_ROPE_DIM, IDX_HEAD_DIM, IDX_HEADS, D_MODEL, D_MODEL)
D_IN = sum(IN_SPLITS)

kernel_name = 'hybrid_fox_dsa_moe_meta_layer'

def rms_norm(x, g):
    xf = x.astype(jnp.float32)
    y = xf * lax.rsqrt(jnp.mean(xf * xf, axis=-1, keepdims=True) + NORM_EPS)
    return (y * g.astype(jnp.float32)).astype(x.dtype)

def layer_norm(x, g, b):
    xf = x.astype(jnp.float32)
    mu = jnp.mean(xf, axis=-1, keepdims=True)
    xc = xf - mu
    var = jnp.mean(xc * xc, axis=-1, keepdims=True)
    return (xc * lax.rsqrt(var + NORM_EPS) * g.astype(jnp.float32) + b.astype(jnp.float32)).astype(x.dtype)

def rope(x, pos):
    d = x.shape[-1]
    half = d // 2
    inv = ROPE_THETA ** (-jnp.arange(half, dtype=jnp.float32) / half)
    ang = pos.astype(jnp.float32)[:, None] * inv[None, :]
    ang = ang.reshape(ang.shape[:1] + (1,) * (x.ndim - 3) + (half,))
    cos, sin = jnp.cos(ang), jnp.sin(ang)
    x1 = x[..., :half].astype(jnp.float32)
    x2 = x[..., half:].astype(jnp.float32)
    return jnp.concatenate([x1 * cos - x2 * sin, x1 * sin + x2 * cos], axis=-1).astype(x.dtype)

def rope_partial(x, pos, n_rot):
    return jnp.concatenate([rope(x[..., :n_rot], pos), x[..., n_rot:]], axis=-1)

def chunk_ids(pos):
    return jnp.where(pos < N_META, 0, 1 + (pos - N_META) // CHUNK)

def chunk_end(last):
    if last < N_META:
        return N_META
    return N_META + CHUNK * (1 + (last - N_META) // CHUNK)

def fox_attention(q, k, v, log_f_cum, pos, n_valid):
    Tp, Dh = q.shape[1], q.shape[-1]
    scale = Dh ** -0.5
    outs = []
    for start in range(0, Tp, Q_BLOCK):
        end = start + Q_BLOCK
        s = jnp.einsum('bqhd,bkhd->bhqk', q[:, start:end], k[:, :end]).astype(jnp.float32) * scale
        f_q = jnp.transpose(log_f_cum[:, start:end], (0, 2, 1))[..., None]
        f_k = jnp.transpose(log_f_cum[:, :end], (0, 2, 1))[:, :, None, :]
        qpos, kpos = pos[start:end], pos[:end]
        allowed = (kpos[None, :] <= qpos[:, None]) & (kpos[None, :] < n_valid)
        s = jnp.where(allowed, s + f_q - f_k, NEG_INF)
        p = jax.nn.softmax(s, axis=-1).astype(v.dtype)
        outs.append(jnp.einsum('bhqk,bkhd->bqhd', p, v[:, :end]))
    return jnp.concatenate(outs, axis=1)

def dsa_attention(q_lat, q_rope, c_kv, k_rope, q_idx, k_idx, idx_w, pos, n_valid, k_sel):
    Tp = q_lat.shape[1]
    chunk = chunk_ids(pos)
    scale = (QK_NOPE_DIM + QK_ROPE_DIM) ** -0.5
    gather = jax.vmap(lambda a, i: a[i])
    outs = []
    for start in range(0, Tp, Q_BLOCK):
        end = start + Q_BLOCK
        kend = min(Tp, max(chunk_end(end - 1), k_sel))
        dots = jnp.einsum('bqhd,bkd->bhqk', q_idx[:, start:end], k_idx[:, :kend]).astype(jnp.float32)
        iscore = jnp.einsum('bqh,bhqk->bqk', idx_w[:, start:end].astype(jnp.float32), jax.nn.relu(dots)) * (IDX_HEAD_DIM ** -0.5)
        admissible = (chunk[:kend][None, :] <= chunk[start:end][:, None]) & (pos[:kend][None, :] < n_valid)
        iscore = jnp.where(admissible[None], iscore, NEG_INF)
        top_score, top_idx = lax.top_k(iscore, k_sel)
        sel_ok = top_score > 0.5 * NEG_INF
        kv_sel = gather(c_kv, top_idx)
        kr_sel = gather(k_rope, top_idx)
        s = (jnp.einsum('bqhr,bqkr->bhqk', q_lat[:, start:end], kv_sel)
             + jnp.einsum('bqhd,bqkd->bhqk', q_rope[:, start:end], kr_sel)).astype(jnp.float32) * scale
        s = jnp.where(sel_ok[:, None], s, NEG_INF)
        p = jax.nn.softmax(s, axis=-1).astype(kv_sel.dtype)
        outs.append(jnp.einsum('bhqk,bqkr->bqhr', p, kv_sel))
    return jnp.concatenate(outs, axis=1)

def hybrid_mixer(xn, pos, n_valid, k_sel, w_in, b_forget, q_norm_g, w_uq, kv_norm_g, w_uk, w_uv,
                 w_qidx, kidx_ln_g, kidx_ln_b, w_branch_a, w_branch_b, w_out):
    B, Tp, _ = xn.shape
    proj = xn @ w_in
    offs = [int(o) for o in np.cumsum(IN_SPLITS)[:-1]]
    qa, ka, va, fa, cq, ckv, kr, kidx, iw, ga, gb = jnp.split(proj, offs, axis=-1)

    qa = qa.reshape(B, Tp, FOX_HEADS, FOX_HEAD_DIM)
    ka = ka.reshape(B, Tp, FOX_HEADS, FOX_HEAD_DIM)
    va = va.reshape(B, Tp, FOX_HEADS, FOX_HEAD_DIM)
    log_f = jax.nn.log_sigmoid((fa + b_forget).astype(jnp.float32))
    log_f_cum = jnp.cumsum(log_f, axis=1)
    o_a = fox_attention(qa, ka, va, log_f_cum, pos, n_valid).reshape(B, Tp, FOX_WIDTH)

    cq_n = rms_norm(cq, q_norm_g)
    q = (cq_n @ w_uq).reshape(B, Tp, DSA_HEADS, QK_NOPE_DIM + QK_ROPE_DIM)
    q_nope, q_rope = q[..., :QK_NOPE_DIM], rope(q[..., QK_NOPE_DIM:], pos)
    q_lat = jnp.einsum('bthn,hnr->bthr', q_nope, w_uk)
    c_kv = rms_norm(ckv, kv_norm_g)
    k_rope = rope(kr, pos)
    q_idx = rope_partial((cq_n @ w_qidx).reshape(B, Tp, IDX_HEADS, IDX_HEAD_DIM), pos, IDX_ROPE_DIM)
    k_idx = rope_partial(layer_norm(kidx, kidx_ln_g, kidx_ln_b), pos, IDX_ROPE_DIM)
    idx_w = iw * (IDX_HEADS ** -0.5)
    o_lat = dsa_attention(q_lat, q_rope, c_kv, k_rope, q_idx, k_idx, idx_w, pos, n_valid, k_sel)
    o_b = jnp.einsum('bthr,hrv->bthv', o_lat, w_uv).reshape(B, Tp, DSA_WIDTH)

    merged = jax.nn.sigmoid(ga) * (o_a @ w_branch_a) + jax.nn.sigmoid(gb) * (o_b @ w_branch_b)
    return merged @ w_out

def moe_ffn(h, w_router, b_router, w_gate_up, b_gate_up, w_down, b_down):
    N, D = h.shape
    logits = (h @ w_router + b_router).astype(jnp.float32)
    top_val, top_idx = lax.top_k(logits, TOP_K)
    gate = jax.nn.softmax(top_val, axis=-1)
    flat_e = top_idx.reshape(-1)
    flat_tok = jnp.repeat(jnp.arange(N, dtype=jnp.int32), TOP_K)
    flat_gate = gate.reshape(-1)
    order = jnp.argsort(flat_e, stable=True)
    se = flat_e[order]
    counts = jnp.bincount(flat_e, length=N_EXPERTS)
    padded = (counts + EXPERT_BLOCK - 1) // EXPERT_BLOCK * EXPERT_BLOCK
    start = jnp.cumsum(counts) - counts
    pstart = jnp.cumsum(padded) - padded
    dest = pstart[se] + jnp.arange(N * TOP_K, dtype=jnp.int32) - start[se]
    n_slots = (-(-(N * TOP_K) // EXPERT_BLOCK) + N_EXPERTS) * EXPERT_BLOCK
    n_blocks = n_slots // EXPERT_BLOCK
    slot_tok = jnp.full((n_slots,), N, jnp.int32).at[dest].set(flat_tok[order])
    slot_gate = jnp.zeros((n_slots,), jnp.float32).at[dest].set(flat_gate[order])
    block_start = jnp.arange(n_blocks, dtype=jnp.int32) * EXPERT_BLOCK
    block_expert = jnp.minimum(jnp.searchsorted(jnp.cumsum(padded), block_start, side='right'), N_EXPERTS - 1)
    h_pad = jnp.concatenate([h, jnp.zeros((1, D), h.dtype)], axis=0)

    def expert_block(args):
        tok, e, g = args
        xb = h_pad[tok]
        gu = xb @ w_gate_up[e] + b_gate_up[e]
        x_glu, x_lin = gu[:, :D_EXPERT], gu[:, D_EXPERT:]
        x_glu = jnp.minimum(x_glu, SWIGLU_LIMIT)
        x_lin = jnp.clip(x_lin, -SWIGLU_LIMIT, SWIGLU_LIMIT)
        act = x_glu * jax.nn.sigmoid(SWIGLU_ALPHA * x_glu) * (x_lin + 1)
        yb = act @ w_down[e] + b_down[e]
        return yb * g[:, None].astype(yb.dtype)

    y = lax.map(expert_block, (slot_tok.reshape(n_blocks, EXPERT_BLOCK), block_expert,
                               slot_gate.reshape(n_blocks, EXPERT_BLOCK)))
    out = jnp.zeros((N + 1, D), y.dtype).at[slot_tok].add(y.reshape(n_slots, D))
    return out[:N].astype(h.dtype)

def setup_inputs(seed: int = 0) -> dict:
    key = jax.random.key(seed)
    ks = jax.random.split(key, 24)
    f32 = jnp.float32
    L = DEPTH

    def nrm(k, shape, scale):
        return jax.random.normal(k, shape, f32) * scale

    def gain(k, shape):
        return 1.0 + 0.02 * jax.random.normal(k, shape, f32)

    return {
        'x': nrm(ks[0], (BATCH, SEQ, D_MODEL), 1.0),
        'meta_tokens': nrm(ks[1], (N_META, D_MODEL), 1.0),
        'norm_mix_g': gain(ks[2], (L, D_MODEL)),
        'w_in': nrm(ks[3], (L, D_MODEL, D_IN), D_MODEL ** -0.5),
        'b_forget': nrm(ks[4], (L, FOX_HEADS), 0.1),
        'q_norm_g': gain(ks[5], (L, Q_RANK)),
        'w_uq': nrm(ks[6], (L, Q_RANK, DSA_HEADS * (QK_NOPE_DIM + QK_ROPE_DIM)), Q_RANK ** -0.5),
        'kv_norm_g': gain(ks[7], (L, KV_RANK)),
        'w_uk': nrm(ks[8], (L, DSA_HEADS, QK_NOPE_DIM, KV_RANK), KV_RANK ** -0.5),
        'w_uv': nrm(ks[9], (L, DSA_HEADS, KV_RANK, V_HEAD_DIM), KV_RANK ** -0.5),
        'w_qidx': nrm(ks[10], (L, Q_RANK, IDX_HEADS * IDX_HEAD_DIM), Q_RANK ** -0.5),
        'kidx_ln_g': gain(ks[11], (L, IDX_HEAD_DIM)),
        'kidx_ln_b': nrm(ks[12], (L, IDX_HEAD_DIM), 0.02),
        'w_branch_a': nrm(ks[13], (L, FOX_WIDTH, D_MODEL), FOX_WIDTH ** -0.5),
        'w_branch_b': nrm(ks[14], (L, DSA_WIDTH, D_MODEL), DSA_WIDTH ** -0.5),
        'w_out': nrm(ks[15], (L, D_MODEL, D_MODEL), D_MODEL ** -0.5),
        'norm_ffn_g': gain(ks[16], (L, D_MODEL)),
        'w_router': nrm(ks[17], (L, D_MODEL, N_EXPERTS), D_MODEL ** -0.5),
        'b_router': nrm(ks[18], (L, N_EXPERTS), 0.01),
        'w_gate_up': nrm(ks[19], (L, N_EXPERTS, D_MODEL, 2 * D_EXPERT), D_MODEL ** -0.5),
        'b_gate_up': nrm(ks[20], (L, N_EXPERTS, 2 * D_EXPERT), 0.01),
        'w_down': nrm(ks[21], (L, N_EXPERTS, D_EXPERT, D_MODEL), D_EXPERT ** -0.5),
        'b_down': nrm(ks[22], (L, N_EXPERTS, D_MODEL), 0.01),
        'norm_final_g': gain(ks[23], (D_MODEL,)),
    }

def reference(x, meta_tokens, norm_mix_g, w_in, b_forget, q_norm_g, w_uq, kv_norm_g, w_uk, w_uv,
              w_qidx, kidx_ln_g, kidx_ln_b, w_branch_a, w_branch_b, w_out, norm_ffn_g, w_router,
              b_router, w_gate_up, b_gate_up, w_down, b_down, norm_final_g):
    B, S, D = x.shape
    T = S + N_META
    Tp = -(-T // Q_BLOCK) * Q_BLOCK
    k_sel = min(IDX_TOPK_MAX, S // 4)
    pos = jnp.arange(Tp, dtype=jnp.int32)
    h = jnp.concatenate([jnp.broadcast_to(meta_tokens.astype(x.dtype)[None], (B, N_META, D)), x], axis=1)
    for l in range(DEPTH):
        xn = jnp.pad(rms_norm(h, norm_mix_g[l]), ((0, 0), (0, Tp - T), (0, 0)))
        mix = hybrid_mixer(xn, pos, T, k_sel, w_in[l], b_forget[l], q_norm_g[l], w_uq[l], kv_norm_g[l],
                           w_uk[l], w_uv[l], w_qidx[l], kidx_ln_g[l], kidx_ln_b[l], w_branch_a[l],
                           w_branch_b[l], w_out[l])
        h = h + mix[:, :T]
        hn = rms_norm(h, norm_ffn_g[l]).reshape(B * T, D)
        h = h + moe_ffn(hn, w_router[l], b_router[l], w_gate_up[l], b_gate_up[l], w_down[l], b_down[l]).reshape(B, T, D)
    return rms_norm(h, norm_final_g)[:, N_META:]


_drawn_inputs = setup_inputs


def setup_inputs(seed=0):
    import zlib

    import numpy as np

    out = dict(_drawn_inputs(seed))
    spreads = {}
    factors = {'kv_norm_g': 3.241, 'b_gate_up': 8.0, 'b_down': 8.0, 'norm_final_g': 2.904}
    for name, (base, spread) in spreads.items():
        noise = np.random.default_rng([zlib.crc32(name.encode()), seed]).standard_normal(out[name].shape)
        drawn = base * np.exp(spread * noise) if base else spread * noise
        out[name] = jnp.asarray(drawn.astype(out[name].dtype))
    for name, factor in factors.items():
        out[name] = (out[name] * factor).astype(out[name].dtype)
    return out
```

```python
import concourse.bass as bass
from concourse import mybir
from contextlib import ExitStack

P = 128
D = 1024
SEQ = 256
META = 16
KEYS = META + SEQ
CH = D // P
HEADS = 8
HD = 64
NOPE, ROPE = 64, 32
QK = NOPE + ROPE
QRANK, KVRANK = 256, 128
IH, ID = 4, 64
TOPK_SEL = 64
EXPERTS, TOPK = 32, 4
ARENA = 31800
CAP = 64
PAIRS = EXPERTS // 2
RCOLS = EXPERTS + 2
EPS = 1e-6
NEG = -1e30
TAKEN = -3e38

C_QA, C_KA, C_VA, C_MID = 0, 512, 1024, 1536
MID = 8 + QRANK + KVRANK + ROPE + ID + IH
C_GA = C_MID + MID
C_GB = C_GA + D
D_IN = C_GB + D
M_F, M_CQ, M_CKV, M_KR, M_KI, M_IW = 0, 8, 264, 392, 424, 488

TILES = [(P, META), (P, META + P), (META, 0)]
WIDTH = [META + P, META + 2 * P]

K_ID, K_LT, K_ONE, K_FM, K_CM, K_IOTA, K_COS, K_SIN = 0, 128, 256, 384, 656, 928, 992, 1040
KCOLS = 1088

SLOT = 2048
NSLOT = 8
MIX_LOADS = 24
PAIR_LOADS = 24
USES = PAIR_LOADS // NSLOT
LAST_READ = [("mid", 2)] * 2 + [("ka", 1), ("ka", 3), ("qa", 1), ("qa", 3)] + [("va", 2)] * 2 \
    + [("ga", m) for m in range(4)] + [("gb", m) for m in range(4)] + [("ba", 3)] * 2 + [("bb", 3)] * 2 \
    + [("out", 1, 1)] * 4

V_MIX, V_FFN, V_Q, V_KV, V_ROWS = 0, 8, 16, 18, 19


def mixer_jobs():
    jobs = ["vec", "bias"]
    jobs += [("xT", 0, 0), ("xT", 0, 1), ("xT", 1, 0), ("xT", 1, 1), ("xT", 2, 0)]
    jobs += [("mid", 0), ("mid", 1), ("mid", 2)]
    jobs += ["ukT"]
    jobs += [("ka", k) for k in range(4)]
    jobs += [("cqT", 0), ("ckvT", 0)]
    jobs += [("qa", k) for k in range(4)]
    jobs += [("kkT", 0), "FT"]
    jobs += [("q", t, n) for t in range(2) for n in range(2)]
    jobs += [("kc", k) for k in range(4)]
    jobs += [("qiT", t) for t in range(2)]
    jobs += [("dots", t, h) for t in range(2) for h in range(IH)]
    jobs += [("va", t) for t in range(3)]
    jobs += [("qT", t, n) for t in range(2) for n in range(2)]
    jobs += [("vb", t) for t in range(3)]
    items = attention_items()
    for i in range(len(items) + 2):
        if i < len(items):
            jobs.append(("S", i))
        if i >= 2:
            jobs.append(("PT", i - 2))
        if i % 2 == 1 and i // 2 < 8:
            jobs.append(("ga", i // 2) if i // 2 < 4 else ("gb", i // 2 - 4))
    jobs += [("oT", b, t) for b in range(2) for t in range(2)]
    jobs += [("ba", m) for m in range(4)]
    jobs += [("bb", m) for m in range(4)]
    jobs += [("out", t, n) for t in range(2) for n in range(2)]
    jobs += [("hT", t, n) for t in range(2) for n in range(2)]
    jobs += ["router", "rank"]
    return jobs


def attention_items():
    return [(b, t, h) for b in range(2) for t in range(2) for h in range(HEADS)]


ROT = 6


def build(nc, x, meta, w_in, b_forget, w_uq, w_uk, w_uv, w_qidx, kln_g, kln_b, w_a, w_b, w_out,
          norm_mix_g, norm_ffn_g, q_norm_g, kv_norm_g, w_router, b_router, w_gu, b_gu, w_dn, b_dn,
          norm_final_g, consts, out):
    f32, i32 = mybir.dt.float32, mybir.dt.int32
    ALU, ACT, AX = mybir.AluOpType, mybir.ActivationFunctionType, mybir.AxisListType

    JOBS = mixer_jobs()
    JOB = {name: n for n, name in enumerate(JOBS)}
    ITEMS = attention_items()

    ctx = ExitStack()
    with ctx:
        def sb(name, cols, dt=f32):
            return ctx.enter_context(nc.sbuf_tensor(name, [P, cols], dt))

        def sem(name):
            return ctx.enter_context(nc.semaphore(name))

        ring = sb("ring", NSLOT * SLOT)
        kst = sb("kst", KCOLS)
        h1 = sb("h1", 2 * D)
        vraw = sb("vraw", P)
        vT = sb("vT", V_ROWS)
        biasT = sb("biasT", 16 * EXPERTS)
        wr = sb("wr", CH * EXPERTS)
        bfor = sb("bfor", HEADS)
        klng = sb("klng", ID)
        klnb = sb("klnb", ID)
        brt = sb("brt", EXPERTS)
        st = sb("st", 64)
        rk = sb("rk", 8 * EXPERTS)
        gates = sb("gates", 2 * RCOLS)
        rank = sb("rank", 2 * RCOLS)
        top8 = sb("top8", 16)
        npf = sb("npf", 4)
        npi = sb("npi", 1, i32)

        arena = sb("arena", ARENA)
        at = [0]

        def take(n):
            at[0] += n
            assert at[0] <= ARENA, at[0]
            return arena[:, at[0] - n:at[0]]

        xs = take(3 * D)
        xnT = take(CH * KEYS).rearrange("p (c k) -> p c k", c=CH)
        qaT = take(4 * SEQ).rearrange("p (c k) -> p c k", c=4)
        kaT = take(4 * KEYS).rearrange("p (c k) -> p c k", c=4)
        va = take(3 * 512).rearrange("p (t n) -> p t n", t=3)
        mid = take(3 * MID).rearrange("p (t n) -> p t n", t=3)
        gaS = take(CH * SEQ)
        gbS = take(CH * SEQ)
        qcat = take(HEADS * SEQ)
        kcat = take(HEADS * KEYS)
        vb = take(3 * 512).rearrange("p (t n) -> p t n", t=3)
        qiT = take(IH * SEQ).rearrange("p (h k) -> p h k", h=IH)
        kiT = take(KEYS)
        wuv = take(512)
        wuk = take(512)
        ukT = take(512)
        cqT = take(2 * SEQ).rearrange("p (c k) -> p c k", c=2)
        ckvT = take(KEYS)
        kk = take(3 * 96).rearrange("p (t n) -> p t n", t=3)
        sq = take(3 * 96)
        isc = take(2 * KEYS)
        wrk = take(2 * KEYS)
        selb = take(2 * KEYS)
        pr = take(3 * KEYS)
        sm = take(3 * KEYS)
        pT = take(2 * 384)
        oaT = take(4 * SEQ).rearrange("p (c k) -> p c k", c=4)
        obT = take(4 * SEQ).rearrange("p (c k) -> p c k", c=4)
        nF = take(KEYS)
        logf = take(4 * 24)
        rel = take(3 * KEYS)
        b0 = 3 * D + CH * KEYS + 4 * SEQ + 4 * KEYS + 3 * 512 + 3 * MID + 2 * CH * SEQ
        braw = arena[0:EXPERTS, b0:b0 + 2048]
        wq = gaS.rearrange("p (c n) -> p c n", c=2)
        qtok = gbS.rearrange("p (t n) -> p t n", t=2)
        rt = xs[:, 2048:2048 + 1024]
        o_tok = xs[:, 0:2048].rearrange("p (b t n) -> p b t n", b=2, t=2)
        gaS = gaS.rearrange("p (c k) -> p c k", c=CH)
        gbS = gbS.rearrange("p (c k) -> p c k", c=CH)
        qcat = qcat.rearrange("p (h k) -> p h k", h=HEADS)
        kcat = kcat.rearrange("p (h k) -> p h k", h=HEADS)
        isc = isc.rearrange("p (t k) -> p t k", t=2)
        wrk = wrk.rearrange("p (t k) -> p t k", t=2)
        selb = selb.rearrange("p (t k) -> p t k", t=2)
        pr = pr.rearrange("p (t k) -> p t k", t=3)
        sm = sm.rearrange("p (t k) -> p t k", t=3)
        rel = rel.rearrange("p (t k) -> p t k", t=3)
        pT = pT.rearrange("p (b t k) -> p b t k", b=2, t=3)
        logf = logf.rearrange("p (a n) -> p a n", a=4)

        at[0] = 0
        hs = take(2 * D).rearrange("p (t n) -> p t n", t=2)
        hT = take(CH * SEQ).rearrange("p (c k) -> p c k", c=CH)
        xg = take(CH * P).rearrange("p (c j) -> p c j", c=CH)
        gl = take(2 * D).rearrange("p (e n) -> p e n", e=2)
        glu = take(2 * 512).rearrange("p (e n) -> p e n", e=2)
        lin = take(2 * 512).rearrange("p (e n) -> p e n", e=2)
        sg = take(2 * 512).rearrange("p (e n) -> p e n", e=2)
        act = take(2 * 512).rearrange("p (e n) -> p e n", e=2)
        yr = take(D)
        pick = take(2 * P).rearrange("p (t j) -> p t j", t=2)
        pickg = take(2 * P).rearrange("p (t j) -> p t j", t=2)
        pickgT = take(2 * P)
        gfin = take(D)
        bdn = take(D)[0:EXPERTS, :]
        gatesT = take(2 * P)[0:EXPERTS, :]
        fin = take(2 * D).rearrange("p (t n) -> p t n", t=2)

        ident = kst[:, K_ID:K_ID + P]
        ltri = kst[:, K_LT:K_LT + P]
        ones = kst[:, K_ONE:K_ONE + P]
        fmask = kst[:, K_FM:K_FM + KEYS]
        cmask = kst[:, K_CM:K_CM + KEYS]
        iota = kst[:, K_IOTA:K_IOTA + CAP]
        cos = kst[:, K_COS:K_COS + 48].rearrange("p (t n) -> p t n", t=3)
        sin = kst[:, K_SIN:K_SIN + 48].rearrange("p (t n) -> p t n", t=3)

        psum = ctx.enter_context(nc.psum_tensor("psum", [P, 8 * 512], f32))
        bank = [psum[:, n * 512:(n + 1) * 512] for n in range(8)]

        def banks(a, b):
            return psum[:, a * 512:b * 512]

        s_x = sem("x_loaded")
        s_vec = sem("vectors_loaded")
        s_kst = sem("constants_loaded")
        s_bias = sem("biases_loaded")
        s_mixw = sem("small_mixer_weights_loaded")
        s_late = sem("late_vectors_loaded")
        s_gfin = sem("final_gain_loaded")
        slot_loaded = [sem(f"slot{n}_loaded") for n in range(NSLOT)]
        slot_used = [sem(f"slot{n}_used") for n in range(NSLOT)]
        filled = [sem(f"bank{n}_filled") for n in range(ROT)]
        emptied = [sem(f"bank{n}_emptied") for n in range(ROT)]
        s_clear = sem("pool_cleared")
        s_ss = sem("x_squares_summed")
        s_ms = sem("x_mean_square_ready")
        s_sd = sem("x_deviation_ready")
        s_xs = sem("x_scaled")
        s_mss = sem("mid_squares_summed")
        s_mms = sem("mid_mean_square_ready")
        s_msd = sem("mid_deviation_ready")
        s_fz = sem("forget_logit_ready")
        s_fl = sem("forget_softplus_ready")
        s_logf = sem("log_forget_ready")
        s_cqn = sem("cq_normed")
        s_ckn = sem("ckv_normed")
        s_kk = sem("index_and_rope_keys_ready")
        s_qr = sem("queries_roped")
        s_rel = sem("index_relu_ready")
        s_relu = sem("index_relu_used")
        s_sel = sem("selection_ready")
        s_exp = sem("probabilities_ready")
        s_pv = sem("head_summed_over_values")
        s_on = sem("attention_tile_normalised")
        s_mg = sem("merged_ready")
        s_hss = sem("h_squares_summed")
        s_hms = sem("h_mean_square_ready")
        s_hsd = sem("h_deviation_ready")
        s_hs = sem("h_scaled")
        s_rmx = sem("router_maximum_ready")
        s_rex = sem("router_exp_ready")
        s_mask = sem("router_mask_ready")
        s_np = sem("pass_count_ready")
        s_bdn = sem("down_biases_loaded")
        s_gtf = sem("gates_transposed")
        s_gt = sem("gates_in_sbuf")
        s_gates = sem("gates_ready")
        s_gl = sem("gate_up_rows_in_sbuf")
        s_tf = sem("gate_up_transposed")
        s_pick = sem("pick_ready")
        s_gath = sem("pair_gathered")
        s_xg = sem("gathered_in_sbuf")
        s_pgf = sem("gated_pick_transposed")
        s_pgt = sem("gated_pick_in_sbuf")
        s_glu = sem("glu_clamped")
        s_sig = sem("sigmoid_ready")
        s_act = sem("activation_ready")
        s_y = sem("down_rows_in_sbuf")
        s_sc = sem("rows_scattered")
        s_acc = sem("rows_added")
        s_fss = sem("final_squares_summed")
        s_fms = sem("final_mean_square_ready")
        s_fsd = sem("final_deviation_ready")
        s_fin = sem("output_rows_ready")
        s_out = sem("output_stored")
        s_dch = sem("vector_step")
        s_ach = sem("scalar_step")
        s_moe = sem("vector_expert_step")

        block = ctx.enter_context(nc.Block())

        def job_bank(name):
            return bank[JOB[name] % ROT]

        def fill_begin(pe, name):
            n = JOB[name]
            if n >= ROT:
                pe.wait_ge(emptied[n % ROT], n // ROT)

        def fill_end(last, name):
            last.then_inc(filled[JOB[name] % ROT], 1)

        def wait_filled(eng, name):
            eng.wait_ge(filled[JOB[name] % ROT], JOB[name] // ROT + 1)

        def empty_end(last, name):
            last.then_inc(emptied[JOB[name] % ROT], 1)

        def wait_emptied(eng, name):
            eng.wait_ge(emptied[JOB[name] % ROT], JOB[name] // ROT + 1)

        def gate_up_done(eng, g, e):
            k = 8 * e + 7
            eng.wait_ge(slot_used[k % NSLOT], g * USES + (k // NSLOT + 1))

        def down_done(eng, g):
            eng.wait_ge(slot_used[(PAIR_LOADS - 1) % NSLOT], g * USES + USES)

        def slot(n):
            return ring[:, (n % NSLOT) * SLOT:(n % NSLOT + 1) * SLOT]

        w_in_v = w_in[0].rearrange("(c p) n -> p c n", p=P)

        def load(sp, n, dst, src):
            if n >= NSLOT:
                wait_filled(sp, LAST_READ[n - NSLOT])
            sp.dma_start(dst, src).then_inc(slot_loaded[n % NSLOT], 16)

        def in_cols(sp, n, col, width):
            load(sp, n, slot(n)[:, 0:CH * width].rearrange("p (c n) -> p c n", c=CH),
                 w_in_v[:, :, col:col + width])

        def in_rows(sp, n, w, row):
            load(sp, n, slot(n).rearrange("p (k n) -> p k n", k=2),
                 w[0, row:row + 2 * P, :].rearrange("(k p) n -> p k n", p=P))

        @block.sync
        def _(sp):
            sp.dma_start(h1[:, 0:D], x[0, 0:P, :]).then_inc(s_x, 16)
            sp.dma_start(h1[:, D:2 * D], x[0, P:2 * P, :]).then_inc(s_x, 16)
            sp.dma_start(xs[0:META, 2 * D:3 * D], meta).then_inc(s_x, 16)
            in_cols(sp, 0, C_MID, MID // 2)
            in_cols(sp, 1, C_MID + MID // 2, MID // 2)
            for k in range(2):
                in_cols(sp, 2 + k, C_KA + 256 * k, 256)
            for k in range(2):
                in_cols(sp, 4 + k, C_QA + 256 * k, 256)
            for k in range(2):
                in_cols(sp, 6 + k, C_VA + 256 * k, 256)
            for k in range(4):
                in_cols(sp, 8 + k, C_GA + 256 * k, 256)
            for k in range(4):
                in_cols(sp, 12 + k, C_GB + 256 * k, 256)
            for k in range(2):
                in_rows(sp, 16 + k, w_a, 256 * k)
            for k in range(2):
                in_rows(sp, 18 + k, w_b, 256 * k)
            for k in range(4):
                in_rows(sp, 20 + k, w_out, 256 * k)

            def expert_load(i, k):
                if k < 16:
                    src = w_gu[0, bass.ds(i * 2 + k // 8, 1), (k % 8) * P:(k % 8 + 1) * P, :]
                    sp.dma_start(slot(k), src.rearrange("e p n -> p (e n)")).then_inc(slot_loaded[k % NSLOT], 16)
                else:
                    r = 2 * P * ((k - 16) // 2)
                    src = w_dn[0, bass.ds(i * 2 + k % 2, 1), r:r + 2 * P, :]
                    sp.dma_start(slot(k).rearrange("p (k n) -> p k n", k=2),
                                 src.rearrange("e (k p) n -> p (e k) n", p=P)).then_inc(slot_loaded[k % NSLOT], 16)

            def rest_of_pair(g, i):
                for k in range(NSLOT, PAIR_LOADS):
                    sp.wait_ge(slot_used[k % NSLOT], g * USES + k // NSLOT)
                    expert_load(i, k)

            def whole_pass(g0):
                with sp.Fori(0, PAIRS - 1) as i:
                    rest_of_pair(g0 + i, i)
                    for k in range(NSLOT):
                        sp.wait_ge(slot_used[k], (g0 + i) * USES + USES)
                        expert_load(i + 1, k)
                rest_of_pair(g0 + (PAIRS - 1), PAIRS - 1)

            for k in range(NSLOT):
                wait_filled(sp, LAST_READ[MIX_LOADS - NSLOT + k])
                expert_load(0, k)
            whole_pass(0)
            sp.wait_ge(s_np, 1)
            n_pass = sp.value_load(npi[0:1, 0:1], min_val=1, max_val=SEQ // CAP)
            with sp.If(n_pass > 1):
                with sp.Fori(1, n_pass) as b:
                    for k in range(NSLOT):
                        sp.wait_ge(slot_used[k], b * (PAIRS * USES))
                        expert_load(0, k)
                    whole_pass(b * PAIRS)
            for t in range(2):
                sp.wait_ge(s_fin, t + 1)
                sp.dma_start(out[0, t * P:(t + 1) * P, :], fin[:, t, :]).then_inc(s_out, 16)
            sp.wait_ge(s_out, 32)

        @block.gpsimd
        def _(pool):
            nc.gpsimd.memset(mid[:, 2, :], 0.0).then_inc(s_clear, 1)
            nc.gpsimd.memset(st[:], 1.0).then_inc(s_clear, 1)

        @block.scalar
        def _(sc):
            row = [0]

            def vec(dram, rows):
                sc.dma_start(vraw[row[0]:row[0] + rows, :],
                             dram.rearrange("a (c p) -> (a c) p", p=P)).then_inc(s_vec, 16)
                row[0] += rows

            sc.dma_start(kst[:], consts).then_inc(s_kst, 16)
            vec(norm_mix_g, CH)
            vec(norm_ffn_g, CH)
            vec(q_norm_g, 2)
            vec(kv_norm_g, 1)
            sc.dma_start(braw, b_gu[0]).then_inc(s_bias, 16)
            sc.dma_start(wuk.rearrange("p (k r) -> p k r", k=4),
                         w_uk[0].rearrange("(k a) n r -> (a n) k r", a=2)).then_inc(s_mixw, 16)
            sc.dma_start(wuv.rearrange("p (h v) -> p h v", h=HEADS),
                         w_uv[0].rearrange("h r v -> r h v")).then_inc(s_mixw, 16)
            sc.dma_start(wq[:, :, 0:768], w_uq[0].rearrange("(c p) n -> p c n", p=P)).then_inc(s_mixw, 16)
            sc.dma_start(wq[:, :, 768:1024], w_qidx[0].rearrange("(c p) n -> p c n", p=P)).then_inc(s_mixw, 16)
            for dst, src in ((bfor, b_forget), (klng, kln_g), (klnb, kln_b), (brt, b_router)):
                sc.dma_start(dst[:], src.broadcast_to([P, dst.shape[1]])).then_inc(s_late, 16)
            sc.dma_start(wr[:].rearrange("p (c e) -> p c e", c=CH),
                         w_router[0].rearrange("(c p) e -> p c e", p=P)).then_inc(s_late, 16)

            sc.wait_ge(s_x, 48)
            sc.wait_ge(s_clear, 2)
            for t, (rows, _) in enumerate(TILES):
                src = h1[:, t * D:(t + 1) * D] if t < 2 else xs[0:META, 2 * D:3 * D]
                junk = xs[:, t * D:(t + 1) * D] if t < 2 else qtok[0:META, 0, :]
                sc.activation(junk, src, ACT.Square, accum_out=st[0:rows, t:t + 1]).then_inc(s_ss, 1)
            sc.wait_ge(s_ms, 1)
            sc.activation(st[:, 3:6], st[:, 3:6], ACT.Sqrt).then_inc(s_sd, 1)

            def copy_out(name, dst, src):
                wait_filled(sc, name)
                empty_end(sc.activation(dst, src, ACT.Copy), name)

            for t, (rows, _) in enumerate(TILES):
                copy_out(("mid", t), mid[0:rows, t, :], job_bank(("mid", t))[0:rows, 0:MID])
            sc.wait_ge(s_fz, 1)
            z, e = logf[:, 0, :], logf[:, 1, :]
            sc.activation(e, z, ACT.Abs).then_inc(s_ach, 1)
            sc.wait_ge(s_ach, 1)
            sc.activation(e, e, ACT.Exp, scale=-1.0).then_inc(s_ach, 1)
            sc.wait_ge(s_ach, 2)
            sc.activation(e, e, ACT.Ln, bias=1.0).then_inc(s_fl, 1)
            for t in range(3):
                wait_emptied(sc, ("mid", t))
            for t in range(2):
                sc.activation(rel[:, 0, 0:QRANK], mid[:, t, M_CQ:M_CQ + QRANK], ACT.Square,
                              accum_out=st[:, 8 + t:9 + t]).then_inc(s_mss, 1)
                sc.wait_ge(s_mss, t + 1)
            for t in range(3):
                sc.activation(rel[:, 0, 0:KVRANK], mid[:, t, M_CKV:M_CKV + KVRANK], ACT.Square,
                              accum_out=st[:, 10 + t:11 + t]).then_inc(s_mss, 1)
                sc.wait_ge(s_mss, t + 3)
            sc.wait_ge(s_mms, 1)
            sc.activation(st[:, 8:16], st[:, 8:16], ACT.Sqrt).then_inc(s_msd, 1)

            copy_out("ukT", ukT, job_bank("ukT")[:])
            for k in range(4):
                copy_out(("ka", k), kaT[:, k, :], job_bank(("ka", k))[:, 0:KEYS])
            for k in range(4):
                copy_out(("qa", k), qaT[:, k, :], job_bank(("qa", k))[:, 0:SEQ])
            for t in range(2):
                for n in range(2):
                    copy_out(("q", t, n), qtok[:, t, n * 512:(n + 1) * 512], job_bank(("q", t, n))[:])
            for k in range(4):
                name = ("kc", k)
                wait_filled(sc, name)
                sc.activation(kcat[0:NOPE, 2 * k, :], job_bank(name)[0:64, 0:KEYS], ACT.Copy)
                empty_end(sc.activation(kcat[0:NOPE, 2 * k + 1, :], job_bank(name)[64:128, 0:KEYS],
                                        ACT.Copy), name)
            for t in range(2):
                copy_out(("qiT", t), qiT[0:ID, :, t * P:(t + 1) * P],
                         job_bank(("qiT", t))[0:ID, :].rearrange("p (h k) -> p h k", h=IH))
            for n in range(2 * IH):
                t, h = divmod(n, IH)
                name = ("dots", t, h)
                if n >= 3:
                    sc.wait_ge(s_relu, n - 2)
                wait_filled(sc, name)
                ins = sc.activation(rel[:, n % 3, 0:WIDTH[t]], job_bank(name)[:, 0:WIDTH[t]], ACT.Relu,
                                    scale=IH ** -0.5 * ID ** -0.5)
                empty_end(ins, name)
            for t, (rows, _) in enumerate(TILES):
                copy_out(("va", t), va[0:rows, t, :], job_bank(("va", t))[0:rows, :])
            for t in range(2):
                for n in range(2):
                    copy_out(("qT", t, n), qcat[0:QK, 4 * n:4 * n + 4, t * P:(t + 1) * P],
                             job_bank(("qT", t, n))[0:QK, :].rearrange("p (h k) -> p h k", h=4))
            for t, (rows, _) in enumerate(TILES):
                copy_out(("vb", t), vb[0:rows, t, :], job_bank(("vb", t))[0:rows, :])
            for i, (b, t, h) in enumerate(ITEMS):
                w = WIDTH[t]
                wait_emptied(sc, ("S", i))
                if i >= 3:
                    wait_filled(sc, ("PT", i - 3))
                sc.activation(pr[:, i % 3, 0:w], sm[:, i % 3, 0:w], ACT.Exp, scale=-1.0,
                              bias=st[:, 16 + i % 3:17 + i % 3],
                              accum_out=rk[:, i:i + 1]).then_inc(s_exp, 1)
                if i % 2 == 1 and i // 2 < 8:
                    name = ("ga", i // 2) if i // 2 < 4 else ("gb", i // 2 - 4)
                    dst = gaS if name[0] == "ga" else gbS
                    wait_filled(sc, name)
                    ins = sc.activation(dst[:, 2 * name[1]:2 * name[1] + 2, :].rearrange("p c k -> p (c k)"),
                                        job_bank(name)[:], ACT.Sigmoid)
                    empty_end(ins, name)
            for b in range(2):
                for t in range(2):
                    dst = oaT if b == 0 else obT
                    copy_out(("oT", b, t), dst[:, :, t * P:(t + 1) * P],
                             job_bank(("oT", b, t))[:].rearrange("p (c k) -> p c k", c=4))
            for t in range(2):
                for n in range(2):
                    wait_emptied(sc, ("out", t, n))
                sc.activation(hs[:, t, :], h1[:, t * D:(t + 1) * D], ACT.Square,
                              accum_out=st[:, 20 + t:21 + t]).then_inc(s_hss, 1)
            sc.wait_ge(s_hms, 1)
            sc.activation(st[:, 22:24], st[:, 22:24], ACT.Sqrt).then_inc(s_hsd, 1)
            sc.dma_start(bdn, b_dn[0]).then_inc(s_bdn, 16)
            sc.dma_start(gfin, norm_final_g.rearrange("(a n) -> a n", a=1).broadcast_to([P, D])).then_inc(s_gfin, 16)
            sc.wait_ge(s_rmx, 2)
            for t in range(2):
                sc.activation(rk[:, 64 + 32 * t:96 + 32 * t], rk[:, 32 * t:32 * t + 32], ACT.Exp,
                              bias=st[:, 24 + t:25 + t]).then_inc(s_rex, 1)

            sc.wait_ge(s_np, 1)
            n_pass = sc.value_load(npi[0:1, 0:1], min_val=1, max_val=SEQ // CAP)
            sc.wait_ge(s_gtf, 1)
            sc.activation(gatesT, bank[2][0:EXPERTS, 0:2 * P], ACT.Copy).then_inc(s_gt, 1)
            with sc.Fori(0, n_pass) as b:
                with sc.Fori(0, PAIRS) as i:
                    g = sc.snap(b * PAIRS + i)
                    sc.wait_ge(s_pgf, g + 1)
                    sc.activation(pickgT, bank[0][:, 0:2 * P], ACT.Copy).then_inc(s_pgt, 1)
                    for e in range(2):
                        gate_up_done(sc, g, e)
                        sc.activation(gl[:, e, :], banks(2 + 2 * e, 4 + 2 * e), ACT.Copy).then_inc(s_gl, 1)
                        sc.wait_ge(s_glu, g * 2 + (e + 1))
                        sc.activation(sg[:, e, :], glu[:, e, :], ACT.Sigmoid, scale=1.702).then_inc(s_sig, 1)
                    down_done(sc, g)
                    sc.activation(yr, banks(2, 4), ACT.Copy).then_inc(s_y, 1)
            sc.wait_ge(s_acc, n_pass * PAIRS + 1)
            for t in range(2):
                sc.activation(hs[:, t, :], h1[:, t * D:(t + 1) * D], ACT.Square,
                              accum_out=st[:, 28 + t:29 + t]).then_inc(s_fss, 1)
            sc.wait_ge(s_fms, 1)
            sc.activation(st[:, 30:32], st[:, 30:32], ACT.Sqrt).then_inc(s_fsd, 1)

        @block.vector
        def _(dve):
            v = nc.vector
            chain = [0]

            def link(ins):
                chain[0] += 1
                ins.then_inc(s_dch, 1)
                dve.wait_ge(s_dch, chain[0])

            def scaled(dst, src, vec, cols):
                return v.tensor_tensor(dst, src, vec.unsqueeze(2).broadcast_to([P] + cols), ALU.mult)

            def rope4(dst1, dst2, x1, x2, c, s, tmp):
                a, b_, c_, d_ = tmp
                v.tensor_tensor(a, x1, c, ALU.mult)
                v.tensor_tensor(b_, x2, s, ALU.mult)
                v.tensor_tensor(c_, x1, s, ALU.mult)
                link(v.tensor_tensor(d_, x2, c, ALU.mult))
                v.tensor_tensor(dst1, a, b_, ALU.subtract)
                return v.tensor_tensor(dst2, c_, d_, ALU.add)

            wait_filled(dve, "vec")
            empty_end(v.tensor_copy(vT[:], job_bank("vec")[:, 0:V_ROWS]), "vec")
            wait_filled(dve, "bias")
            empty_end(v.tensor_copy(biasT[:], job_bank("bias")), "bias")
            dve.wait_ge(s_ss, 3)
            v.tensor_scalar(st[:, 3:6], st[:, 0:3], 1.0 / D, EPS, ALU.mult, ALU.add).then_inc(s_ms, 1)
            dve.wait_ge(s_sd, 1)
            link(v.reciprocal(st[:, 3:6], st[:, 3:6]))
            for t, (rows, _) in enumerate(TILES):
                src = h1[:, t * D:(t + 1) * D] if t < 2 else xs[0:META, 2 * D:3 * D]
                v.tensor_scalar(xs[0:rows, t * D:(t + 1) * D], src, st[0:rows, 3 + t:4 + t], None,
                                ALU.mult).then_inc(s_xs, 1)
            for t, (rows, col) in enumerate(TILES):
                for n in range(2 if t < 2 else 1):
                    name = ("xT", t, n)
                    wait_filled(dve, name)
                    cs = 4 if t < 2 else CH
                    src = job_bank(name)[:, 0:cs * rows].rearrange("p (c k) -> p c k", c=cs)
                    empty_end(scaled(xnT[:, 4 * n:4 * n + cs, col:col + rows], src,
                                     vT[:, V_MIX + 4 * n:V_MIX + 4 * n + cs], [cs, rows]), name)
            dve.wait_ge(s_late, 80)
            for t in range(3):
                wait_emptied(dve, ("mid", t))
            z = logf[:, 0, :].rearrange("p (t h) -> p t h", t=3)
            v.tensor_tensor(z, mid[:, :, M_F:M_F + HEADS], bfor[:].unsqueeze(1).broadcast_to([P, 3, HEADS]),
                            ALU.add).then_inc(s_fz, 1)
            ki = mid[:, :, M_KI:M_KI + ID]
            kc = kk[:, :, 0:ID]
            link(v.tensor_reduce(st[:, 32:35], ki, AX.X, ALU.add))
            link(v.tensor_scalar(st[:, 32:35], st[:, 32:35], 1.0 / ID, None, ALU.mult))
            link(v.tensor_tensor(kc, ki, st[:, 32:35].unsqueeze(2).broadcast_to([P, 3, ID]), ALU.subtract))
            sqv = sq[:, 0:3 * ID].rearrange("p (t n) -> p t n", t=3)
            link(v.tensor_tensor(sqv, kc, kc, ALU.mult))
            link(v.tensor_reduce(st[:, 13:16], sqv, AX.X, ALU.add))
            dve.wait_ge(s_mss, 5)
            v.tensor_scalar(st[:, 8:10], st[:, 8:10], 1.0 / QRANK, EPS, ALU.mult, ALU.add)
            v.tensor_scalar(st[:, 10:13], st[:, 10:13], 1.0 / KVRANK, EPS, ALU.mult, ALU.add)
            v.tensor_scalar(st[:, 13:16], st[:, 13:16], 1.0 / ID, EPS, ALU.mult, ALU.add).then_inc(s_mms, 1)
            dve.wait_ge(s_fl, 1)
            v.scalar_tensor_tensor(logf[:, 2, :], logf[:, 0, :], 0.0, logf[:, 1, :], ALU.min,
                                   ALU.subtract).then_inc(s_logf, 1)
            dve.wait_ge(s_msd, 1)
            link(v.reciprocal(st[:, 8:16], st[:, 8:16]))
            for t in range(2):
                ins = v.tensor_scalar(mid[:, t, M_CQ:M_CQ + QRANK], mid[:, t, M_CQ:M_CQ + QRANK],
                                      st[:, 8 + t:9 + t], None, ALU.mult)
            ins.then_inc(s_cqn, 1)
            for t in range(3):
                ins = v.tensor_scalar(mid[:, t, M_CKV:M_CKV + KVRANK], mid[:, t, M_CKV:M_CKV + KVRANK],
                                      st[:, 10 + t:11 + t], None, ALU.mult)
            ins.then_inc(s_ckn, 1)
            link(v.tensor_tensor(kc, kc, st[:, 13:16].unsqueeze(2).broadcast_to([P, 3, ID]), ALU.mult))
            link(v.tensor_tensor(kc, kc, klng[:].unsqueeze(1).broadcast_to([P, 3, ID]), ALU.mult))
            link(v.tensor_tensor(kc, kc, klnb[:].unsqueeze(1).broadcast_to([P, 3, ID]), ALU.add))
            link(v.tensor_copy(kk[:, :, ID:ID + ROPE], mid[:, :, M_KR:M_KR + ROPE]))
            tmp3 = [rt[:, 48 * n:48 * n + 48].rearrange("p (t n) -> p t n", t=3) for n in range(8)]
            for n, o in enumerate((0, ID)):
                last = rope4(kk[:, :, o:o + 16], kk[:, :, o + 16:o + 32], kk[:, :, o:o + 16],
                             kk[:, :, o + 16:o + 32], cos, sin, tmp3[4 * n:4 * n + 4])
            last.then_inc(s_kk, 1)
            wait_filled(dve, ("cqT", 0))
            empty_end(scaled(cqT, job_bank(("cqT", 0))[:].rearrange("p (c k) -> p c k", c=2),
                             vT[:, V_Q:V_Q + 2], [2, SEQ]), ("cqT", 0))
            wait_filled(dve, ("ckvT", 0))
            empty_end(v.tensor_scalar(ckvT, job_bank(("ckvT", 0))[:, 0:KEYS], vT[:, V_KV:V_KV + 1], None,
                                      ALU.mult), ("ckvT", 0))
            wait_filled(dve, ("kkT", 0))
            v.tensor_copy(kiT[0:ID, :], job_bank(("kkT", 0))[0:ID, 0:KEYS])
            empty_end(v.tensor_copy(kcat[NOPE:QK, :, :],
                                    job_bank(("kkT", 0))[ID:ID + ROPE, 0:KEYS].unsqueeze(1)
                                    .broadcast_to([ROPE, HEADS, KEYS])), ("kkT", 0))
            wait_filled(dve, "FT")
            empty_end(v.tensor_scalar(nF[0:HEADS, :], job_bank("FT")[0:HEADS, 0:KEYS], -(HD ** 0.5), None,
                                      ALU.mult), "FT")
            for t in range(2):
                for n in range(2):
                    wait_emptied(dve, ("q", t, n))
                for n, (o, heads, per, off) in enumerate(((768, IH, ID, 0), (0, HEADS, QK, NOPE))):
                    grp = qtok[:, t, o:o + heads * per].rearrange("p (h n) -> p h n", h=heads)
                    x1, x2 = grp[:, :, off:off + 16], grp[:, :, off + 16:off + 32]
                    cs_ = cos[:, t, :].unsqueeze(1).broadcast_to([P, heads, 16])
                    sn_ = sin[:, t, :].unsqueeze(1).broadcast_to([P, heads, 16])
                    tmp = [rt[:, 512 * n + 128 * m:512 * n + 128 * m + 16 * heads]
                           .rearrange("p (h n) -> p h n", h=heads) for m in range(4)]
                    ins = rope4(x1, x2, x1, x2, cs_, sn_, tmp)
                    ins.then_inc(s_qr, 1)
                    dve.wait_ge(s_qr, 2 * t + n + 1)
            for n in range(2 * IH):
                t, h = divmod(n, IH)
                w = WIDTH[t]
                wait_emptied(dve, ("dots", t, h))
                base = cmask[:, KEYS - w:KEYS] if h == 0 else isc[:, t, 0:w]
                ins = v.scalar_tensor_tensor(isc[:, t, 0:w], rel[:, n % 3, 0:w],
                                             mid[:, t, M_IW + h:M_IW + h + 1], base, ALU.mult, ALU.add)
                ins.then_inc(s_relu, 1)
                dve.wait_ge(s_relu, n + 1)
            for t in range(2):
                w = WIDTH[t]
                for r in range(TOPK_SEL // 8):
                    src = isc[:, t, 0:w] if r == 0 else wrk[:, t, 0:w]
                    link(v.max(top8[:, 8 * t:8 * t + 8], src))
                    link(v.match_replace(wrk[:, t, 0:w], top8[:, 8 * t:8 * t + 8], src, TAKEN))
                v.tensor_scalar(selb[:, t, 0:w], wrk[:, t, 0:w], TAKEN / 2, NEG, ALU.is_gt,
                                ALU.mult).then_inc(s_sel, 1)
            dve.wait_ge(s_sel, 2)

            def normalise(i):
                b, t, _ = ITEMS[i]
                n = 2 * b + t
                dve.wait_ge(s_exp, 8 * n + 8)
                link(v.reciprocal(st[:, 40:48], rk[:, 8 * n:8 * n + 8]))
                dve.wait_ge(s_pv, 8 * n + 8)
                src = bank[6 + n % 2].rearrange("p (h d) -> p h d", h=HEADS)
                v.tensor_tensor(o_tok[:, b, t, :].rearrange("p (h d) -> p h d", h=HEADS), src,
                                st[:, 40:48].unsqueeze(2).broadcast_to([P, HEADS, HD]),
                                ALU.mult).then_inc(s_on, 1)
                dve.wait_ge(s_on, n + 1)

            for i in range(len(ITEMS) + 2):
                if i < len(ITEMS):
                    b, t, h = ITEMS[i]
                    w = WIDTH[t]
                    mask = selb[:, t, 0:w] if b else fmask[:, KEYS - w:KEYS]
                    scale = (QK if b else HD) ** -0.5
                    if i >= 3:
                        dve.wait_ge(s_exp, i - 2)
                    wait_filled(dve, ("S", i))
                    ins = v.tensor_tensor_reduce(out=sm[:, i % 3, 0:w], in0=job_bank(("S", i))[:, 0:w],
                                                 in1=mask, scale=-scale, scalar=3e38, op0=ALU.add,
                                                 op1=ALU.min, accum_out=st[:, 16 + i % 3:17 + i % 3])
                    empty_end(ins, ("S", i))
                if i >= 2:
                    k = i - 2
                    t = ITEMS[k][1]
                    if k >= 2:
                        dve.wait_ge(s_pv, k - 1)
                    wait_filled(dve, ("PT", k))
                    src = job_bank(("PT", k))
                    v.tensor_copy(pT[0:META, k % 2, 2, :], src[0:META, 256:384])
                    empty_end(v.tensor_copy(pT[:, k % 2, 0:t + 1, :],
                                            src[:, 0:(t + 1) * P].rearrange("p (t k) -> p t k", t=t + 1)),
                              ("PT", k))
                    if k % 8 == 7:
                        normalise(k)
            for m in range(4):
                name = ("ba", m)
                wait_filled(dve, name)
                wait_emptied(dve, ("ga", m))
                dst = gaS[:, 2 * m:2 * m + 2, :].rearrange("p c k -> p (c k)")
                empty_end(v.tensor_tensor(dst, dst, job_bank(name)[:], ALU.mult), name)
            for m in range(4):
                name = ("bb", m)
                wait_filled(dve, name)
                wait_emptied(dve, ("gb", m))
                a = gaS[:, 2 * m:2 * m + 2, :].rearrange("p c k -> p (c k)")
                b_ = gbS[:, 2 * m:2 * m + 2, :].rearrange("p c k -> p (c k)")
                ins = v.tensor_tensor(b_, b_, job_bank(name)[:], ALU.mult)
                empty_end(ins, name)
                wait_emptied(dve, name)
                v.tensor_tensor(a, a, b_, ALU.add).then_inc(s_mg, 1)
            for t in range(2):
                for n in range(2):
                    name = ("out", t, n)
                    wait_filled(dve, name)
                    dst = h1[:, t * D + 512 * n:t * D + 512 * (n + 1)]
                    empty_end(v.tensor_tensor(dst, dst, job_bank(name)[:], ALU.add), name)
            dve.wait_ge(s_hss, 2)
            v.tensor_scalar(st[:, 22:24], st[:, 20:22], 1.0 / D, EPS, ALU.mult, ALU.add).then_inc(s_hms, 1)
            dve.wait_ge(s_hsd, 1)
            link(v.reciprocal(st[:, 22:24], st[:, 22:24]))
            for t in range(2):
                v.tensor_scalar(hs[:, t, :], h1[:, t * D:(t + 1) * D], st[:, 22 + t:23 + t], None,
                                ALU.mult).then_inc(s_hs, 1)
            for t in range(2):
                for n in range(2):
                    name = ("hT", t, n)
                    wait_filled(dve, name)
                    src = job_bank(name)[:].rearrange("p (c k) -> p c k", c=4)
                    empty_end(scaled(hT[:, 4 * n:4 * n + 4, t * P:(t + 1) * P], src,
                                     vT[:, V_FFN + 4 * n:V_FFN + 4 * n + 4], [4, P]), name)
            wait_filled(dve, "router")
            lg = rk[:, 0:64].rearrange("p (t e) -> p t e", t=2)
            ex = rk[:, 64:128]
            wk = rk[:, 128:192]
            msk = rk[:, 192:256]
            ins = v.tensor_tensor(lg, job_bank("router")[:, 0:64].rearrange("p (t e) -> p t e", t=2),
                                  brt[:].unsqueeze(1).broadcast_to([P, 2, EXPERTS]), ALU.add)
            empty_end(ins, "router")
            wait_emptied(dve, "router")
            for t in range(2):
                m8 = top8[:, 8 * t:8 * t + 8]
                link(v.max(m8, lg[:, t, :]))
                v.tensor_scalar(st[:, 24 + t:25 + t], m8[:, 0:1], -1.0, None, ALU.mult).then_inc(s_rmx, 1)
                link(v.memset(m8[:, 4:8], 3e38))
                link(v.match_replace(wk[:, 32 * t:32 * t + 32], m8, lg[:, t, :], TAKEN))
            v.tensor_scalar(msk, wk, TAKEN / 2, None, ALU.is_lt).then_inc(s_mask, 1)
            dve.wait_ge(s_mask, 1)
            dve.wait_ge(s_rex, 2)
            link(v.tensor_tensor(ex, ex, msk, ALU.mult))
            link(v.tensor_reduce(st[:, 26:28], ex.rearrange("p (t e) -> p t e", t=2), AX.X, ALU.add))
            link(v.reciprocal(st[:, 26:28], st[:, 26:28]))
            rk3 = rank[:].rearrange("p (t e) -> p t e", t=2)
            gt3 = gates[:].rearrange("p (t e) -> p t e", t=2)
            link(v.tensor_tensor(gt3[:, :, 0:EXPERTS],
                                 ex.rearrange("p (t e) -> p t e", t=2),
                                 st[:, 26:28].unsqueeze(2).broadcast_to([P, 2, EXPERTS]), ALU.mult))
            wait_filled(dve, "rank")
            link(v.scalar_tensor_tensor(rk3[:, :, 0:EXPERTS],
                                        job_bank("rank")[:, 0:64].rearrange("p (t e) -> p t e", t=2), 1000.0,
                                        msk.rearrange("p (t e) -> p t e", t=2), ALU.add, ALU.mult))
            v.tensor_copy(gt3[:, :, EXPERTS:RCOLS], gt3[:, :, 0:2]).then_inc(s_gates, 1)
            link(v.tensor_scalar(rk3[:, :, EXPERTS:RCOLS], rk3[:, :, 0:2], -1000.0 - CAP, None, ALU.add))
            link(v.tensor_scalar(rk3[:, :, 0:EXPERTS], rk3[:, :, 0:EXPERTS], -1000.0, None, ALU.add))
            ins = v.tensor_reduce(npf[:, 3:4], job_bank("rank")[:, 64:96], AX.X, ALU.max)
            empty_end(ins, "rank")
            wait_emptied(dve, "rank")
            link(v.tensor_scalar(st[:, 48:49], npf[:, 3:4], float(CAP), 1.0, ALU.is_gt, ALU.add))
            for m in (2, 3):
                link(v.tensor_scalar(st[:, 49:50], npf[:, 3:4], float(m * CAP), None, ALU.is_gt))
                link(v.tensor_tensor(st[:, 48:49], st[:, 48:49], st[:, 49:50], ALU.add))
            v.tensor_copy(npi[:], st[:, 48:49]).then_inc(s_np, 1)
            dve.wait_ge(s_np, 1)

            n_pass = dve.value_load(npi[0:1, 0:1], min_val=1, max_val=SEQ // CAP)
            bias = biasT[:].rearrange("p (m e) -> p m e", e=EXPERTS)

            def pick_pair(col):
                for t in range(2):
                    ins = v.tensor_tensor(pick[:, t, :].rearrange("p (e j) -> p e j", e=2),
                                          iota.unsqueeze(1).broadcast_to([P, 2, CAP]),
                                          rk3[:, t, col].unsqueeze(2).broadcast_to([P, 2, CAP]), ALU.is_equal)
                return ins

            def gate_pair(col):
                for t in range(2):
                    ins = v.tensor_tensor(pickg[:, t, :].rearrange("p (e j) -> p e j", e=2),
                                          pick[:, t, :].rearrange("p (e j) -> p e j", e=2),
                                          gt3[:, t, col].unsqueeze(2).broadcast_to([P, 2, CAP]), ALU.mult)
                return ins

            def gathered():
                scaled(xg, banks(0, 2).rearrange("p (c j) -> p c j", c=CH), vT[:, V_FFN:V_FFN + CH],
                       [CH, P]).then_inc(s_xg, 1)

            def add_rows():
                v.tensor_tensor(h1[:], h1[:], banks(4, 8), ALU.add).then_inc(s_acc, 1)

            link(pick_pair(slice(0, 2)))
            gate_pair(slice(0, 2)).then_inc(s_pick, 1)
            dve.wait_ge(s_gath, 1)
            gathered()
            dve.wait_ge(s_sc, 1)
            add_rows()
            dve.wait_ge(s_acc, 1)
            STEPS = 9
            with dve.Fori(0, n_pass) as b:
                with dve.Fori(0, PAIRS) as i:
                    g = dve.snap(b * PAIRS + i)
                    first = dve.snap(g * STEPS + b)
                    step = [0]

                    def mlink(ins):
                        step[0] += 1
                        ins.then_inc(s_moe, 1)
                        dve.wait_ge(s_moe, first + step[0])

                    dve.wait_ge(s_pgf, g + 1)
                    mlink(pick_pair(bass.ds(i * 2 + 2, 2)))
                    gate_pair(bass.ds(i * 2 + 2, 2)).then_inc(s_pick, 1)
                    for e in range(2):
                        rows = banks(6, 8).rearrange("p (m j) -> p m j", m=8)

                        def with_bias(dst, src, m):
                            return v.tensor_tensor(
                                dst.rearrange("p (m j) -> p m j", m=8), src,
                                bias[:, m:m + 8, bass.ds(i * 2 + e, 1)].broadcast_to([P, 8, CAP]), ALU.add)
                        dve.wait_ge(s_tf, g * 2 + (e + 1))
                        mlink(with_bias(glu[:, e, :], rows[:, :, 0:CAP], 0))
                        v.tensor_scalar(glu[:, e, :], glu[:, e, :], 7.0, None, ALU.min).then_inc(s_glu, 1)
                        mlink(with_bias(lin[:, e, :], rows[:, :, CAP:2 * CAP], 8))
                        mlink(v.tensor_scalar(lin[:, e, :], lin[:, e, :], 7.0, -7.0, ALU.min, ALU.max))
                        dve.wait_ge(s_sig, g * 2 + (e + 1))
                        mlink(v.scalar_tensor_tensor(lin[:, e, :], lin[:, e, :], 1.0, glu[:, e, :],
                                                     ALU.add, ALU.mult))
                        v.tensor_tensor(act[:, e, :], lin[:, e, :], sg[:, e, :], ALU.mult).then_inc(s_act, 1)
                    dve.wait_ge(s_gath, g + 2)
                    gathered()
                    dve.wait_ge(s_sc, g + 2)
                    add_rows()
                    dve.wait_ge(s_acc, g + 2)
                    assert step[0] == STEPS
                v.tensor_scalar(rank[:], rank[:], -float(CAP), None, ALU.add).then_inc(s_moe, 1)
                dve.wait_ge(s_moe, (b * PAIRS + PAIRS) * STEPS + (b + 1))

            dve.wait_ge(s_fss, 2)
            v.tensor_scalar(st[:, 30:32], st[:, 28:30], 1.0 / D, EPS, ALU.mult, ALU.add).then_inc(s_fms, 1)
            dve.wait_ge(s_fsd, 1)
            link(v.reciprocal(st[:, 30:32], st[:, 30:32]))
            dve.wait_ge(s_gfin, 16)
            for t in range(2):
                v.scalar_tensor_tensor(fin[:, t, :], h1[:, t * D:(t + 1) * D], st[:, 30 + t:31 + t], gfin,
                                       ALU.mult, ALU.mult).then_inc(s_fin, 1)

        @block.tensor
        def _(pe):
            mm = nc.tensor.matmul
            tr = nc.tensor.transpose
            def loaded(n):
                pe.wait_ge(slot_loaded[n % NSLOT], 16 * (n // NSLOT + 1))

            def used(last, n):
                last.then_inc(slot_used[n % NSLOT], 1)

            def win(n, width=256):
                return slot(n)[:, 0:CH * width].rearrange("p (c n) -> p c n", c=CH)

            pe.wait_ge(s_kst, 16)
            pe.wait_ge(s_vec, 64)
            fill_end(tr(job_bank("vec")[:, 0:V_ROWS], vraw[0:V_ROWS, :], ident[0:V_ROWS, 0:V_ROWS]), "vec")
            pe.wait_ge(s_bias, 16)
            for m in range(16):
                ins = tr(job_bank("bias")[:, m * EXPERTS:(m + 1) * EXPERTS], braw[:, m * P:(m + 1) * P],
                         ident[0:EXPERTS, 0:EXPERTS])
            fill_end(ins, "bias")
            for t, (rows, col) in enumerate(TILES):
                pe.wait_ge(s_xs, t + 1)
                for n in range(2 if t < 2 else 1):
                    name = ("xT", t, n)
                    fill_begin(pe, name)
                    for c in range(4 if t < 2 else CH):
                        ins = tr(job_bank(name)[:, c * rows:(c + 1) * rows],
                                 xs[0:rows, t * D + (4 * n + c) * P:t * D + (4 * n + c + 1) * P],
                                 ident[0:rows, 0:rows])
                    fill_end(ins, name)
            for t in range(3):
                wait_emptied(pe, ("xT", t, 0))
                if t < 2:
                    wait_emptied(pe, ("xT", t, 1))
            for t, (rows, col) in enumerate(TILES):
                name = ("mid", t)
                fill_begin(pe, name)
                for s in range(2):
                    loaded(s)
                    half = MID // 2
                    for c in range(CH):
                        ins = mm(job_bank(name)[0:rows, s * half:(s + 1) * half], xnT[:, c, col:col + rows],
                                 win(s, half)[:, c, :], start=c == 0, stop=c == CH - 1)
                fill_end(ins, name)
            pe.wait_ge(s_mixw, 64)
            fill_begin(pe, "ukT")
            for k in range(4):
                ins = tr(job_bank("ukT")[:, k * P:(k + 1) * P], wuk[:, k * P:(k + 1) * P], ident)
            fill_end(ins, "ukT")

            def feature_major(name, s, k, cols, width):
                fill_begin(pe, name)
                loaded(s)
                for c in range(CH):
                    ins = mm(job_bank(name)[:, 0:width], win(s)[:, c, k * P:(k + 1) * P],
                             xnT[:, c, cols:cols + width], start=c == 0, stop=c == CH - 1)
                fill_end(ins, name)

            for k in range(4):
                feature_major(("ka", k), 2 + k // 2, k % 2, 0, KEYS)
            name = ("cqT", 0)
            fill_begin(pe, name)
            pe.wait_ge(s_cqn, 1)
            for c in range(2):
                for t in range(2):
                    ins = tr(job_bank(name)[:, c * SEQ + t * P:c * SEQ + (t + 1) * P],
                             mid[:, t, M_CQ + c * P:M_CQ + (c + 1) * P], ident)
            fill_end(ins, name)
            name = ("ckvT", 0)
            fill_begin(pe, name)
            pe.wait_ge(s_ckn, 1)
            for t, (rows, col) in enumerate(TILES):
                ins = tr(job_bank(name)[:, col:col + rows], mid[0:rows, t, M_CKV:M_CKV + KVRANK],
                         ident[0:rows, 0:rows])
            fill_end(ins, name)
            for k in range(4):
                feature_major(("qa", k), 4 + k // 2, k % 2, META, SEQ)
            name = ("kkT", 0)
            fill_begin(pe, name)
            pe.wait_ge(s_kk, 1)
            for t, (rows, col) in enumerate(TILES):
                ins = tr(job_bank(name)[0:QK, col:col + rows], kk[0:rows, t, :], ident[0:rows, 0:rows])
            fill_end(ins, name)
            fill_begin(pe, "FT")
            pe.wait_ge(s_logf, 1)
            lf = logf[:, 2, :].rearrange("p (t h) -> p t h", t=3)
            FT = job_bank("FT")
            for t, (rows, col) in ((2, TILES[2]), (0, TILES[0]), (1, TILES[1])):
                terms = [(lf[0:rows, t, :], ltri[0:rows, 0:rows]), (lf[0:rows, t, :], ident[0:rows, 0:rows])]
                if t < 2:
                    terms.append((lf[0:META, 2, :], ones[0:META, 0:rows]))
                if t == 1:
                    terms.append((lf[:, 0, :], ones[:, 0:rows]))
                for n, (a, b_) in enumerate(terms):
                    ins = mm(FT[0:HEADS, col:col + rows], a, b_, start=n == 0, stop=n == len(terms) - 1)
            fill_end(ins, "FT")
            wait_emptied(pe, ("cqT", 0))
            for t in range(2):
                for n in range(2):
                    name = ("q", t, n)
                    fill_begin(pe, name)
                    for c in range(2):
                        ins = mm(job_bank(name)[:], cqT[:, c, t * P:(t + 1) * P],
                                 wq[:, c, n * 512:(n + 1) * 512], start=c == 0, stop=c == 1)
                    fill_end(ins, name)
            wait_emptied(pe, ("ckvT", 0))
            wait_emptied(pe, "ukT")
            for k in range(4):
                name = ("kc", k)
                fill_begin(pe, name)
                fill_end(mm(job_bank(name)[:, 0:KEYS], ukT[:, k * P:(k + 1) * P], ckvT, start=True,
                            stop=True), name)
            pe.wait_ge(s_qr, 4)
            for t in range(2):
                name = ("qiT", t)
                fill_begin(pe, name)
                for h in range(IH):
                    ins = tr(job_bank(name)[0:ID, h * P:(h + 1) * P],
                             qtok[:, t, 768 + h * ID:768 + (h + 1) * ID], ident)
                fill_end(ins, name)
            wait_emptied(pe, ("kkT", 0))
            for t in range(2):
                wait_emptied(pe, ("qiT", t))
                for h in range(IH):
                    name = ("dots", t, h)
                    fill_begin(pe, name)
                    fill_end(mm(job_bank(name)[:, 0:WIDTH[t]], qiT[0:ID, h, t * P:(t + 1) * P],
                                kiT[0:ID, 0:WIDTH[t]], start=True, stop=True), name)
            for t, (rows, col) in enumerate(TILES):
                name = ("va", t)
                fill_begin(pe, name)
                for s in range(2):
                    loaded(6 + s)
                    for c in range(CH):
                        ins = mm(job_bank(name)[0:rows, s * 256:(s + 1) * 256], xnT[:, c, col:col + rows],
                                 win(6 + s)[:, c, :], start=c == 0, stop=c == CH - 1)
                fill_end(ins, name)
            for t in range(2):
                for n in range(2):
                    name = ("qT", t, n)
                    fill_begin(pe, name)
                    for h in range(4):
                        ins = tr(job_bank(name)[0:QK, h * P:(h + 1) * P],
                                 qtok[:, t, (4 * n + h) * QK:(4 * n + h + 1) * QK], ident)
                    fill_end(ins, name)
            for t, (rows, col) in enumerate(TILES):
                name = ("vb", t)
                fill_begin(pe, name)
                fill_end(mm(job_bank(name)[0:rows, :], ckvT[:, col:col + rows], wuv, start=True, stop=True),
                         name)
            for name in [("ka", 3), ("qa", 3), "FT"] + [("kc", k) for k in range(4)] \
                    + [("va", t) for t in range(3)]:
                wait_emptied(pe, name)

            def scores(i):
                b, t, h = ITEMS[i]
                w = WIDTH[t]
                name = ("S", i)
                fill_begin(pe, name)
                dst = job_bank(name)[:, 0:w]
                if b == 0:
                    r = (h % 2) * HD
                    mm(dst, qaT[r:r + HD, h // 2, t * P:(t + 1) * P], kaT[r:r + HD, h // 2, 0:w],
                       start=True, stop=False)
                    ins = mm(dst, ident[0:HEADS, h:h + 1].broadcast_to([HEADS, P]), nF[0:HEADS, 0:w],
                             start=False, stop=True)
                else:
                    if h == 0:
                        for n in range(2):
                            wait_emptied(pe, ("qT", t, n))
                    ins = mm(dst, qcat[0:QK, h, t * P:(t + 1) * P], kcat[0:QK, h, 0:w], start=True,
                             stop=True)
                fill_end(ins, name)

            def transposed(i):
                b, t, h = ITEMS[i]
                name = ("PT", i)
                fill_begin(pe, name)
                pe.wait_ge(s_exp, i + 1)
                for k in range(t + 1):
                    tr(job_bank(name)[:, k * P:(k + 1) * P], pr[:, i % 3, META + k * P:META + (k + 1) * P],
                       ident)
                fill_end(tr(job_bank(name)[0:META, 256:384], pr[:, i % 3, 0:META], ident), name)

            def values(i):
                b, t, h = ITEMS[i]
                n = 2 * b + t
                if h == 0 and n >= 2:
                    pe.wait_ge(s_on, n - 1)
                if i == 16:
                    for m in range(3):
                        wait_emptied(pe, ("vb", m))
                wait_emptied(pe, ("PT", i))
                vv = vb if b else va
                dst = bank[6 + n % 2][:, h * HD:(h + 1) * HD]
                for k in range(t + 1):
                    mm(dst, pT[:, i % 2, k, :], vv[:, k, h * HD:(h + 1) * HD], start=k == 0, stop=False)
                ins = mm(dst, pT[0:META, i % 2, 2, :], vv[0:META, 2, h * HD:(h + 1) * HD], start=False,
                         stop=True)
                ins.then_inc(s_pv, 1)

            for i in range(len(ITEMS) + 2):
                if i < len(ITEMS):
                    scores(i)
                if i >= 3:
                    values(i - 3)
                if i >= 2:
                    transposed(i - 2)
                if i % 2 == 1 and i // 2 < 8:
                    m = i // 2 % 4
                    name = ("ga", m) if i // 2 < 4 else ("gb", m)
                    s = (8 if i // 2 < 4 else 12) + m
                    fill_begin(pe, name)
                    loaded(s)
                    for k in range(2):
                        for c in range(CH):
                            ins = mm(job_bank(name)[:, k * SEQ:(k + 1) * SEQ], win(s)[:, c, k * P:(k + 1) * P],
                                     xnT[:, c, META:KEYS], start=c == 0, stop=c == CH - 1)
                    fill_end(ins, name)
            values(len(ITEMS) - 1)
            for b in range(2):
                for t in range(2):
                    name = ("oT", b, t)
                    fill_begin(pe, name)
                    pe.wait_ge(s_on, 2 * b + t + 1)
                    for c in range(4):
                        ins = tr(job_bank(name)[:, c * P:(c + 1) * P], o_tok[:, b, t, c * P:(c + 1) * P],
                                 ident)
                    fill_end(ins, name)
            for b, (kind, src, s0) in enumerate((("ba", oaT, 16), ("bb", obT, 18))):
                for t in range(2):
                    wait_emptied(pe, ("oT", b, t))
                loaded(s0)
                loaded(s0 + 1)
                for m in range(4):
                    name = (kind, m)
                    fill_begin(pe, name)
                    for k in range(2):
                        for c in range(4):
                            w = slot(s0 + c // 2).rearrange("p (k n) -> p k n", k=2)[:, c % 2, :]
                            ins = mm(job_bank(name)[:, k * SEQ:(k + 1) * SEQ],
                                     w[:, (2 * m + k) * P:(2 * m + k + 1) * P], src[:, c, :],
                                     start=c == 0, stop=c == 3)
                    fill_end(ins, name)
            pe.wait_ge(s_mg, 4)
            for n in range(20, 24):
                loaded(n)
            for t in range(2):
                for n in range(2):
                    name = ("out", t, n)
                    fill_begin(pe, name)
                    for c in range(CH):
                        w = slot(20 + c // 2).rearrange("p (k n) -> p k n", k=2)[:, c % 2, :]
                        ins = mm(job_bank(name)[:], gaS[:, c, t * P:(t + 1) * P],
                                 w[:, n * 512:(n + 1) * 512], start=c == 0, stop=c == CH - 1)
                    fill_end(ins, name)
            for t in range(2):
                pe.wait_ge(s_hs, t + 1)
                for n in range(2):
                    name = ("hT", t, n)
                    fill_begin(pe, name)
                    for c in range(4):
                        ins = tr(job_bank(name)[:, c * P:(c + 1) * P],
                                 hs[:, t, (4 * n + c) * P:(4 * n + c + 1) * P], ident)
                    fill_end(ins, name)
            fill_begin(pe, "router")
            for t in range(2):
                for n in range(2):
                    wait_emptied(pe, ("hT", t, n))
            pe.wait_ge(s_late, 80)
            wrv = wr[:].rearrange("p (c e) -> p c e", c=CH)
            for t in range(2):
                for c in range(CH):
                    ins = mm(job_bank("router")[:, t * EXPERTS:(t + 1) * EXPERTS],
                             hT[:, c, t * P:(t + 1) * P], wrv[:, c, :], start=c == 0, stop=c == CH - 1)
            fill_end(ins, "router")
            fill_begin(pe, "rank")
            pe.wait_ge(s_mask, 1)
            mk = [rk[:, 192 + 32 * t:224 + 32 * t] for t in range(2)]
            rb = job_bank("rank")
            mm(rb[:, 0:32], ltri, mk[0], start=True, stop=True)
            mm(rb[:, 32:64], ones, mk[0], start=True, stop=False)
            mm(rb[:, 32:64], ltri, mk[1], start=False, stop=True)
            mm(rb[:, 64:96], ones, mk[0], start=True, stop=False)
            fill_end(mm(rb[:, 64:96], ones, mk[1], start=False, stop=True), "rank")
            for name in JOBS[-ROT:]:
                wait_emptied(pe, name)

            def gather():
                for c in range(CH):
                    for t in range(2):
                        ins = mm(bank[c // 4][:, (c % 4) * P:(c % 4 + 1) * P],
                                 hs[:, t, c * P:(c + 1) * P], pick[:, t, :], start=t == 0, stop=t == 1)
                ins.then_inc(s_gath, 1)

            pe.wait_ge(s_pick, 1)
            gather()
            pe.wait_ge(s_gates, 1)
            gt3 = gates[:].rearrange("p (t e) -> p t e", t=2)
            for t in range(2):
                ins = tr(bank[2][0:EXPERTS, t * P:(t + 1) * P], gt3[:, t, 0:EXPERTS], ident)
            ins.then_inc(s_gtf, 1)
            pe.wait_ge(s_gt, 1)
            pe.wait_ge(s_bdn, 16)
            for t in range(2):
                for n in range(2):
                    ins = mm(bank[4 + 2 * t + n], gatesT[:, t * P:(t + 1) * P], bdn[:, n * 512:(n + 1) * 512],
                             start=True, stop=True)
            ins.then_inc(s_sc, 1)
            pe.wait_ge(s_np, 1)
            n_pass = pe.value_load(npi[0:1, 0:1], min_val=1, max_val=SEQ // CAP)
            with pe.Fori(0, n_pass) as b:
                with pe.Fori(0, PAIRS) as i:
                    g = pe.snap(b * PAIRS + i)

                    def arrived(k):
                        pe.wait_ge(slot_loaded[k % NSLOT], g * (16 * USES) + 16 * ((MIX_LOADS + k) // NSLOT + 1))

                    def features(e):
                        pe.wait_ge(s_gl, g * 2 + (e + 1))
                        for m in range(CH):
                            ins = tr(bank[6 + m // 4][:, (m % 4) * P:(m % 4 + 1) * P],
                                     gl[:, e, m * P:(m + 1) * P], ident)
                        ins.then_inc(s_tf, 1)

                    pe.wait_ge(s_xg, g + 1)
                    for t in range(2):
                        ins = tr(bank[0][:, t * P:(t + 1) * P], pickg[:, t, :], ident)
                    ins.then_inc(s_pgf, 1)
                    for e in range(2):
                        if e == 1:
                            pe.wait_ge(s_acc, g + 1)
                        for c in range(CH):
                            k = 8 * e + c
                            arrived(k)
                            for n in range(2):
                                for u in range(2):
                                    ins = mm(bank[2 + 2 * e + n][u * CAP:(u + 1) * CAP, :],
                                             xg[:, c, e * CAP:(e + 1) * CAP],
                                             slot(k)[:, u * D + n * 512:u * D + (n + 1) * 512],
                                             start=c == 0, stop=c == CH - 1)
                            used(ins, k)
                            if e == 1 and c == 1:
                                features(0)
                    pe.wait_ge(s_pick, g + 2)
                    pe.wait_ge(s_pgt, g + 1)
                    gather()
                    pe.wait_ge(s_act, g * 2 + 1)
                    features(1)
                    pe.wait_ge(s_act, g * 2 + 2)
                    for c in range(CH):
                        for e in range(2):
                            if c % 2 == 0:
                                arrived(16 + 2 * (c // 2) + e)
                        for n in range(2):
                            for e in range(2):
                                k = 16 + 2 * (c // 2) + e
                                ins = mm(bank[2 + n][e * CAP:(e + 1) * CAP, :],
                                         act[:, e, c * CAP:(c + 1) * CAP],
                                         slot(k)[:, (c % 2) * D + n * 512:(c % 2) * D + (n + 1) * 512],
                                         start=c == 0, stop=c == CH - 1)
                                if c % 2 and n:
                                    used(ins, k)
                    pe.wait_ge(s_y, g + 1)
                    for t in range(2):
                        for n in range(2):
                            ins = mm(bank[4 + 2 * t + n], pickgT[:, t * P:(t + 1) * P],
                                     yr[:, n * 512:(n + 1) * 512], start=True, stop=True)
                    ins.then_inc(s_sc, 1)


_INS = ['x', 'meta_tokens', 'w_in', 'b_forget', 'w_uq', 'w_uk', 'w_uv', 'w_qidx', 'kidx_ln_g', 'kidx_ln_b',
        'w_branch_a', 'w_branch_b', 'w_out', 'norm_mix_g', 'norm_ffn_g', 'q_norm_g', 'kv_norm_g',
        'w_router', 'b_router', 'w_gate_up', 'b_gate_up', 'w_down', 'b_down', 'norm_final_g']


def _constants(np):
    k = np.zeros((P, KCOLS), np.float32)
    r = np.arange(P)
    k[:, K_ID:K_ID + P] = np.eye(P)
    k[:, K_LT:K_LT + P] = r[:, None] < r[None, :]
    k[:, K_ONE:K_ONE + P] = 1.0
    k[:, K_FM + KEYS - P:K_FM + KEYS] = np.where(r[None, :] > r[:, None], NEG, 0.0)
    k[0:64, K_CM + KEYS - 64:K_CM + KEYS] = NEG
    k[:, K_IOTA:K_IOTA + CAP] = np.arange(CAP)
    half = ROPE // 2
    inv = (np.float32(10000.0) ** (-np.arange(half, dtype=np.float32) / np.float32(half))).astype(np.float32)
    for t, (rows, col) in enumerate(TILES):
        ang = ((col + r).astype(np.float32)[:, None] * inv[None, :]).astype(np.float32)
        k[:, K_COS + half * t:K_COS + half * (t + 1)] = np.cos(ang.astype(np.float64))
        k[:, K_SIN + half * t:K_SIN + half * (t + 1)] = np.sin(ang.astype(np.float64))
    return k


def kernel(**inputs):
    import numpy as _np
    import concourse.bacc as _bacc
    from concourse import mybir as _mybir
    from concourse.bass_utils import run_bass_kernel_spmd as _run

    nc = _bacc.Bacc("TRN2", target_bir_lowering=False, num_devices=1)
    arrays, aps = {}, {}
    for name in _INS:
        a = _np.ascontiguousarray(inputs[name])
        arrays[f"in_{name}"] = a
        aps[name] = nc.dram_tensor(f"in_{name}", a.shape, _mybir.dt.from_np(a.dtype), kind="ExternalInput").ap()
    consts = _constants(_np)
    arrays["consts"] = consts
    aps["consts"] = nc.dram_tensor("consts", consts.shape, _mybir.dt.float32, kind="ExternalInput").ap()
    out = nc.dram_tensor("out", (1, SEQ, D), _mybir.dt.float32, kind="ExternalOutput").ap()
    a = aps
    build(nc, a['x'], a['meta_tokens'], a['w_in'], a['b_forget'], a['w_uq'], a['w_uk'], a['w_uv'],
          a['w_qidx'], a['kidx_ln_g'], a['kidx_ln_b'], a['w_branch_a'], a['w_branch_b'], a['w_out'],
          a['norm_mix_g'], a['norm_ffn_g'], a['q_norm_g'], a['kv_norm_g'], a['w_router'], a['b_router'],
          a['w_gate_up'], a['b_gate_up'], a['w_down'], a['b_down'], a['norm_final_g'], a['consts'], out)
    r = _run(nc, [arrays], core_ids=[0])
    return r.results[0]["out"]
```

```python
import concourse.bass as bass
from concourse import mybir
from contextlib import ExitStack

P = 128
D = 1024
SEQ = 256
META = 16
KEYS = META + SEQ
CH = D // P
HEADS = 8
HD = 64
NOPE, ROPE = 64, 32
QK = NOPE + ROPE
QRANK, KVRANK = 256, 128
IH, ID = 4, 64
TOPK_SEL = 64
EXPERTS, TOPK = 32, 4
ARENA = 31800
CAP = 64
PAIRS = EXPERTS // 2
RCOLS = EXPERTS + 2
EPS = 1e-6
NEG = -1e30
RANK0 = 1000.0
TAKEN = -3e38

C_QA, C_KA, C_VA, C_MID = 0, 512, 1024, 1536
MID = 8 + QRANK + KVRANK + ROPE + ID + IH
C_GA = C_MID + MID
C_GB = C_GA + D
D_IN = C_GB + D
M_F, M_CQ, M_CKV, M_KR, M_KI, M_IW = 0, 8, 264, 392, 424, 488

TILES = [(P, META), (P, META + P), (META, 0)]
WIDTH = [META + P, META + 2 * P]

K_ID, K_LT, K_ONE, K_FM, K_CM, K_IOTA, K_COS, K_SIN = 0, 128, 256, 384, 656, 928, 992, 1040
KCOLS = 1088

SLOT = 2048
NSLOT = 8
ESLOT = 16
MIX_LOADS = 24
PAIR_LOADS = 24
UNROLL = 2
TURNS = PAIRS // UNROLL
USES = UNROLL * PAIR_LOADS // ESLOT
LAST_READ = [("mid", 2)] * 2 + [("ka", 1), ("ka", 3), ("qa", 1), ("qa", 3)] + [("va", 2)] * 2 \
    + [("gate", 2 * m + 1) for m in range(8)] + [("ba", 3)] * 2 + [("bb", 3)] * 2 \
    + [("out", 1, 1)] * 4

V_MIX, V_FFN, V_Q, V_KV, V_ROWS = 0, 8, 16, 18, 19


def mixer_jobs():
    jobs = ["vec"]
    jobs += [("xT", 0, 0), ("xT", 0, 1), ("xT", 1, 0), ("xT", 1, 1), ("xT", 2, 0)]
    jobs += ["bias", ("mid", 0), ("mid", 1), ("mid", 2)]
    jobs += ["ukT"]
    jobs += [("ka", k) for k in range(4)]
    jobs += [("cqT", 0), ("ckvT", 0)]
    jobs += [("qa", k) for k in range(4)]
    jobs += [("kkT", 0), "FT"]
    jobs += [("q", t, n) for t in range(2) for n in range(2)]
    jobs += [("kc", k) for k in range(4)]
    jobs += [("va", 0)]
    jobs += [("qiT", t) for t in range(2)]
    jobs += [("dots", t, h) for t in range(2) for h in range(IH)]
    jobs += [("va", 1), ("va", 2)]
    jobs += [("qT", t, n) for t in range(2) for n in range(2)]
    jobs += [("vb", t) for t in range(3)]
    items = attention_items()
    for i in range(len(items) + 2):
        if i < len(items):
            jobs.append(("S", i))
        if i >= 2:
            jobs.append(("PT", i - 2))
        if i % 2 == 1 and i < len(items):
            jobs.append(("gate", i // 2))
    jobs += [("ba", m) for m in range(4)]
    jobs += [("bb", m) for m in range(4)]
    jobs += [("out", 0, 0), ("out", 0, 1), ("out", 1, 0), ("hT", 0, 0), ("hT", 0, 1), ("out", 1, 1),
             ("router", 0), ("hT", 1, 0), ("hT", 1, 1), ("router", 1), "rank"]
    return jobs


def attention_items():
    return [(b, t, h) for b in range(2) for t in range(2) for h in range(HEADS)]


ROT = 6


def build(nc, x, meta, w_in, b_forget, w_uq, w_uk, w_uv, w_qidx, kln_g, kln_b, w_a, w_b, w_out,
          norm_mix_g, norm_ffn_g, q_norm_g, kv_norm_g, w_router, b_router, w_gu, b_gu, w_dn, b_dn,
          norm_final_g, consts, out):
    f32, i32 = mybir.dt.float32, mybir.dt.int32
    ALU, ACT, AX = mybir.AluOpType, mybir.ActivationFunctionType, mybir.AxisListType

    JOBS = mixer_jobs()
    JOB = {name: n for n, name in enumerate(JOBS)}
    ITEMS = attention_items()

    ctx = ExitStack()
    with ctx:
        def sb(name, cols, dt=f32):
            return ctx.enter_context(nc.sbuf_tensor(name, [P, cols], dt))

        def sem(name):
            return ctx.enter_context(nc.semaphore(name))

        ring = sb("ring", NSLOT * SLOT)
        kst = sb("kst", KCOLS)
        h1 = sb("h1", 2 * D)
        vraw = sb("vraw", P)
        vT = sb("vT", V_ROWS)
        biasT = sb("biasT", 16 * EXPERTS)
        wr = sb("wr", CH * EXPERTS)
        bfor = sb("bfor", HEADS)
        klng = sb("klng", ID)
        klnb = sb("klnb", ID)
        brt = sb("brt", EXPERTS)
        st = sb("st", 64)
        rk = sb("rk", 8 * EXPERTS)
        gates = sb("gates", 2 * RCOLS)
        rank = sb("rank", 2 * RCOLS)
        top8 = sb("top8", 16)
        npf = sb("npf", 4)
        npi = sb("npi", 1, i32)

        arena = sb("arena", ARENA)
        at = [0]

        def take(n):
            at[0] += n
            assert at[0] <= ARENA, at[0]
            return arena[:, at[0] - n:at[0]]

        xs = take(3 * D)
        qaT = take(4 * SEQ).rearrange("p (c k) -> p c k", c=4)
        mid = take(3 * MID).rearrange("p (t n) -> p t n", t=3)
        qiT = take(IH * SEQ).rearrange("p (h k) -> p h k", h=IH)
        wuv = take(512)
        wuk = take(512)
        cqT = take(2 * SEQ).rearrange("p (c k) -> p c k", c=2)
        ckvT = take(KEYS)
        kk = take(3 * 96).rearrange("p (t n) -> p t n", t=3)
        sq = take(3 * 96)
        logf = take(4 * 24)
        gaS = take(CH * SEQ)
        gbS = take(CH * SEQ)
        oaT = take(4 * SEQ).rearrange("p (c k) -> p c k", c=4)
        obT = take(4 * SEQ).rearrange("p (c k) -> p c k", c=4)
        at[0] = tail = 15 * D
        xnT = take(CH * KEYS).rearrange("p (c k) -> p c k", c=CH)
        qcat = take(HEADS * SEQ)
        kcat = take(HEADS * KEYS)
        va = take(3 * 512).rearrange("p (t n) -> p t n", t=3)
        vb = take(3 * 512).rearrange("p (t n) -> p t n", t=3)
        kaT = take(4 * KEYS).rearrange("p (c k) -> p c k", c=4)
        nF = take(KEYS)
        pT = take(4 * 384)
        pr = take(3 * KEYS)
        sm = take(3 * KEYS)
        selb = take(2 * KEYS)
        isc = take(2 * KEYS)
        wrk = take(2 * KEYS)
        ukT = take(512)
        kiT = take(KEYS)
        assert at[0] - tail >= (ESLOT - NSLOT) * SLOT
        more = arena[:, tail:tail + (ESLOT - NSLOT) * SLOT]
        rel = oaT.rearrange("p c k -> p (c k)")[:, 0:3 * KEYS]
        braw = qcat[0:EXPERTS, :]
        wq = gaS.rearrange("p (c n) -> p c n", c=2)
        qtok = gbS.rearrange("p (t n) -> p t n", t=2)
        rt = xs[:, 2048:2048 + 1024]
        gaS = gaS.rearrange("p (c k) -> p c k", c=CH)
        gbS = gbS.rearrange("p (c k) -> p c k", c=CH)
        qcat = qcat.rearrange("p (h k) -> p h k", h=HEADS)
        kcat = kcat.rearrange("p (h k) -> p h k", h=HEADS)
        isc = isc.rearrange("p (t k) -> p t k", t=2)
        wrk = wrk.rearrange("p (t k) -> p t k", t=2)
        selb = selb.rearrange("p (t k) -> p t k", t=2)
        pr = pr.rearrange("p (t k) -> p t k", t=3)
        sm = sm.rearrange("p (t k) -> p t k", t=3)
        rel = rel.rearrange("p (t k) -> p t k", t=3)
        pT = pT.rearrange("p (b t k) -> p b t k", b=4, t=3)
        logf = logf.rearrange("p (a n) -> p a n", a=4)

        at[0] = 0
        hs = take(2 * D).rearrange("p (t n) -> p t n", t=2)
        hT = take(CH * SEQ).rearrange("p (c k) -> p c k", c=CH)
        xg = take(CH * P).rearrange("p (c j) -> p c j", c=CH)
        gl = take(2 * D).rearrange("p (e n) -> p e n", e=2)
        glu = take(2 * 512).rearrange("p (e n) -> p e n", e=2)
        lin = take(2 * 512).rearrange("p (e n) -> p e n", e=2)
        sg = take(2 * 512).rearrange("p (e n) -> p e n", e=2)
        act = take(2 * 512).rearrange("p (e n) -> p e n", e=2)
        yr = take(D)
        pick = take(2 * P).rearrange("p (t j) -> p t j", t=2)
        pickg = take(2 * P).rearrange("p (t j) -> p t j", t=2)
        pickgT = take(2 * P)
        gfin = take(D)
        bdn = take(D)[0:EXPERTS, :]
        gatesT = take(2 * P)[0:EXPERTS, :]
        fin = gl.rearrange("p e n -> p (e n)").rearrange("p (t n) -> p t n", t=2)
        assert at[0] <= tail

        ident = kst[:, K_ID:K_ID + P]
        ltri = kst[:, K_LT:K_LT + P]
        ones = kst[:, K_ONE:K_ONE + P]
        fmask = kst[:, K_FM:K_FM + KEYS]
        cmask = kst[:, K_CM:K_CM + KEYS]
        iota = kst[:, K_IOTA:K_IOTA + CAP]
        cos = kst[:, K_COS:K_COS + 48].rearrange("p (t n) -> p t n", t=3)
        sin = kst[:, K_SIN:K_SIN + 48].rearrange("p (t n) -> p t n", t=3)

        psum = ctx.enter_context(nc.psum_tensor("psum", [P, 8 * 512], f32))
        bank = [psum[:, n * 512:(n + 1) * 512] for n in range(8)]

        def banks(a, b):
            return psum[:, a * 512:b * 512]

        s_x = sem("x_loaded")
        s_vec = sem("vectors_loaded")
        s_idn = sem("identity_loaded")
        s_kst = sem("constants_loaded")
        s_bias = sem("biases_loaded")
        s_mixw = sem("small_mixer_weights_loaded")
        s_late = sem("late_vectors_loaded")
        s_gfin = sem("final_gain_loaded")
        slot_loaded = [sem(f"slot{n}_loaded") for n in range(ESLOT)]
        slot_used = [sem(f"slot{n}_used") for n in range(ESLOT)]
        filled = [sem(f"bank{n}_filled") for n in range(ROT)]
        emptied = [sem(f"bank{n}_emptied") for n in range(ROT)]
        s_clear = sem("pool_cleared")
        s_ss = sem("x_squares_summed")
        s_ms = sem("x_mean_square_ready")
        s_sd = sem("x_deviation_ready")
        s_xs = sem("x_scaled")
        s_mss = sem("mid_squares_summed")
        s_mms = sem("mid_mean_square_ready")
        s_msd = sem("mid_deviation_ready")
        s_fz = sem("forget_logit_ready")
        s_fl = sem("forget_softplus_ready")
        s_logf = sem("log_forget_ready")
        s_cqn = sem("cq_normed")
        s_ckn = sem("ckv_normed")
        s_kk = sem("index_and_rope_keys_ready")
        s_qr = sem("queries_roped")
        s_rel = sem("index_relu_ready")
        s_relu = sem("index_relu_used")
        s_sel = sem("selection_ready")
        s_exp = sem("probabilities_ready")
        s_pv = sem("pair_of_heads_summed_over_values")
        s_pn = sem("probabilities_normalised")
        s_on = sem("attention_tile_in_sbuf")
        s_mg = sem("merged_ready")
        s_hss = sem("h_squares_summed")
        s_hms = sem("h_mean_square_ready")
        s_hsd = sem("h_deviation_ready")
        s_hs = sem("h_scaled")
        s_rmx = sem("router_maximum_ready")
        s_rex = sem("router_exp_ready")
        s_mask = sem("router_mask_ready")
        s_np = sem("pass_count_ready")
        s_bdn = sem("down_biases_loaded")
        s_gtf = sem("gates_transposed")
        s_gt = sem("gates_in_sbuf")
        s_gates = sem("gates_ready")
        s_gl = sem("gate_up_rows_in_sbuf")
        s_tf = sem("gate_up_transposed")
        s_pick0 = sem("first_pick_ready")
        s_pick = sem("gated_pick_ready")
        s_gath = sem("pair_gathered")
        s_xg = sem("gathered_in_sbuf")
        s_pgf = sem("gated_pick_transposed")
        s_pgt = sem("gated_pick_in_sbuf")
        s_glu = sem("glu_clamped")
        s_sig = sem("sigmoid_ready")
        s_act = sem("activation_ready")
        s_y = sem("down_rows_in_sbuf")
        s_sc = sem("rows_scattered")
        s_acc = sem("rows_added")
        s_fss = sem("final_squares_summed")
        s_fms = sem("final_mean_square_ready")
        s_fsd = sem("final_deviation_ready")
        s_fin = sem("output_rows_ready")
        s_out = sem("output_stored")
        s_dch = sem("vector_step")
        s_ach = sem("scalar_step")
        s_moe = sem("vector_expert_step")

        block = ctx.enter_context(nc.Block())

        def job_bank(name):
            return bank[JOB[name] % ROT]

        def fill_begin(pe, name):
            n = JOB[name]
            if n >= ROT:
                pe.wait_ge(emptied[n % ROT], n // ROT)

        def fill_end(last, name):
            last.then_inc(filled[JOB[name] % ROT], 1)

        def wait_filled(eng, name):
            eng.wait_ge(filled[JOB[name] % ROT], JOB[name] // ROT + 1)

        def empty_end(last, name):
            last.then_inc(emptied[JOB[name] % ROT], 1)

        def wait_emptied(eng, name):
            eng.wait_ge(emptied[JOB[name] % ROT], JOB[name] // ROT + 1)

        def gate_up_done(eng, turn, u, e):
            k = PAIR_LOADS * u + 8 * e + 7
            eng.wait_ge(slot_used[place(k)], turn * USES + (k // ESLOT + 1))

        def down_done(eng, turn, u):
            k = PAIR_LOADS * u + PAIR_LOADS - 1
            eng.wait_ge(slot_used[place(k)], turn * USES + (k // ESLOT + 1))

        def slot(n):
            return ring[:, (n % NSLOT) * SLOT:(n % NSLOT + 1) * SLOT]

        def place(k):
            return (k + NSLOT) % ESLOT

        def eslot(k):
            n = place(k)
            return ring[:, n * SLOT:(n + 1) * SLOT] if n < NSLOT else more[:, (n - NSLOT) * SLOT:(n - NSLOT + 1) * SLOT]

        w_in_v = w_in[0].rearrange("(c p) n -> p c n", p=P)

        def load(sp, n, dst, src):
            if n >= NSLOT:
                wait_filled(sp, LAST_READ[n - NSLOT])
            sp.dma_start(dst, src).then_inc(slot_loaded[n % NSLOT], 16)

        def in_cols(sp, n, col, width):
            load(sp, n, slot(n)[:, 0:CH * width].rearrange("p (c n) -> p c n", c=CH),
                 w_in_v[:, :, col:col + width])

        def in_rows(sp, n, w, row):
            load(sp, n, slot(n).rearrange("p (k n) -> p k n", k=2),
                 w[0, row:row + 2 * P, :].rearrange("(k p) n -> p k n", p=P))

        @block.sync
        def _(sp):
            sp.dma_start(h1[:, 0:D], x[0, 0:P, :]).then_inc(s_x, 16)
            sp.dma_start(h1[:, D:2 * D], x[0, P:2 * P, :]).then_inc(s_x, 16)
            sp.dma_start(xs[0:META, 2 * D:3 * D], meta).then_inc(s_x, 16)
            sp.dma_start(kst[:, 0:P], consts[:, 0:P]).then_inc(s_idn, 16)
            in_cols(sp, 0, C_MID, MID // 2)
            in_cols(sp, 1, C_MID + MID // 2, MID // 2)
            for k in range(2):
                in_cols(sp, 2 + k, C_KA + 256 * k, 256)
            for k in range(2):
                in_cols(sp, 4 + k, C_QA + 256 * k, 256)
            for k in range(2):
                in_cols(sp, 6 + k, C_VA + 256 * k, 256)
            for k in range(4):
                in_cols(sp, 8 + k, C_GA + 256 * k, 256)
            for k in range(4):
                in_cols(sp, 12 + k, C_GB + 256 * k, 256)
            for k in range(2):
                in_rows(sp, 16 + k, w_a, 256 * k)
            for k in range(2):
                in_rows(sp, 18 + k, w_b, 256 * k)
            for k in range(4):
                in_rows(sp, 20 + k, w_out, 256 * k)

            def expert_load(j, kk):
                u, k = divmod(kk, PAIR_LOADS)
                pair = j * (2 * UNROLL) + 2 * u
                if k < 16:
                    src = w_gu[0, bass.ds(pair + k // 8, 1), (k % 8) * P:(k % 8 + 1) * P, :]
                    sp.dma_start(eslot(kk), src.rearrange("e p n -> p (e n)")).then_inc(slot_loaded[place(kk)], 16)
                else:
                    r = 2 * P * ((k - 16) // 2)
                    src = w_dn[0, bass.ds(pair + k % 2, 1), r:r + 2 * P, :]
                    sp.dma_start(eslot(kk).rearrange("p (k n) -> p k n", k=2),
                                 src.rearrange("e (k p) n -> p (e k) n", p=P)).then_inc(slot_loaded[place(kk)], 16)

            def rest_of_turn(turn, j):
                for kk in range(ESLOT, UNROLL * PAIR_LOADS):
                    sp.wait_ge(slot_used[place(kk)], turn * USES + kk // ESLOT)
                    expert_load(j, kk)

            def whole_pass(turn0):
                with sp.Fori(0, TURNS - 1) as j:
                    rest_of_turn(turn0 + j, j)
                    for kk in range(ESLOT):
                        sp.wait_ge(slot_used[place(kk)], (turn0 + j) * USES + USES)
                        expert_load(j + 1, kk)
                rest_of_turn(turn0 + (TURNS - 1), TURNS - 1)

            sp.wait_ge(s_pv, len(ITEMS) // 2)
            for kk in range(ESLOT):
                if place(kk) < NSLOT:
                    wait_filled(sp, LAST_READ[MIX_LOADS - NSLOT + place(kk)])
                expert_load(0, kk)
            whole_pass(0)
            sp.wait_ge(s_np, 1)
            n_pass = sp.value_load(npi[0:1, 0:1], min_val=1, max_val=SEQ // CAP)
            with sp.If(n_pass > 1):
                with sp.Fori(1, n_pass) as b:
                    for kk in range(ESLOT):
                        sp.wait_ge(slot_used[place(kk)], b * (TURNS * USES))
                        expert_load(0, kk)
                    whole_pass(b * TURNS)
            for t in range(2):
                sp.wait_ge(s_fin, t + 1)
                sp.dma_start(out[0, t * P:(t + 1) * P, :], fin[:, t, :]).then_inc(s_out, 16)
            sp.wait_ge(s_out, 32)

        @block.gpsimd
        def _(pool):
            nc.gpsimd.memset(st[:], 1.0).then_inc(s_clear, 1)
            nc.gpsimd.memset(mid[:, 2, :], 0.0).then_inc(s_clear, 1)
            pool.dma_start(braw, b_gu[0]).then_inc(s_bias, 16)
            pool.dma_start(kst[:, P:KCOLS], consts[:, P:KCOLS]).then_inc(s_kst, 16)
            for dst, src in ((bfor, b_forget), (klng, kln_g), (klnb, kln_b), (brt, b_router)):
                pool.dma_start(dst[:], src.broadcast_to([P, dst.shape[1]])).then_inc(s_late, 16)
            pool.dma_start(wuk.rearrange("p (k r) -> p k r", k=4),
                           w_uk[0].rearrange("(k a) n r -> (a n) k r", a=2)).then_inc(s_mixw, 16)
            pool.dma_start(wuv.rearrange("p (h v) -> p h v", h=HEADS),
                           w_uv[0].rearrange("h r v -> r h v")).then_inc(s_mixw, 16)
            pool.dma_start(wq[:, :, 0:768], w_uq[0].rearrange("(c p) n -> p c n", p=P)).then_inc(s_mixw, 16)
            pool.dma_start(wq[:, :, 768:1024], w_qidx[0].rearrange("(c p) n -> p c n", p=P)).then_inc(s_mixw, 16)
            pool.dma_start(wr[:].rearrange("p (c e) -> p c e", c=CH),
                           w_router[0].rearrange("(c p) e -> p c e", p=P)).then_inc(s_late, 16)

        @block.scalar
        def _(sc):
            row = [0]

            def vec(dram, rows):
                sc.dma_start(vraw[row[0]:row[0] + rows, :],
                             dram.rearrange("a (c p) -> (a c) p", p=P)).then_inc(s_vec, 16)
                row[0] += rows

            vec(norm_mix_g, CH)
            vec(norm_ffn_g, CH)
            vec(q_norm_g, 2)
            vec(kv_norm_g, 1)
            sc.wait_ge(s_clear, 1)
            sc.activation(st[:, 60:61], st[:, 61:62], ACT.Sqrt)
            sc.wait_ge(s_x, 48)
            sc.activation(xs[:, 0:D], h1[:, 0:D], ACT.Square, accum_out=st[:, 0:1]).then_inc(s_ss, 1)
            sc.wait_ge(s_ms, 1)
            sc.activation(st[:, 3:5], st[:, 3:5], ACT.Sqrt).then_inc(s_sd, 1)
            sc.activation(qtok[0:META, 0, :], xs[0:META, 2 * D:3 * D], ACT.Square,
                          accum_out=st[0:META, 2:3]).then_inc(s_ss, 1)
            sc.wait_ge(s_ms, 2)
            sc.activation(st[:, 5:6], st[:, 5:6], ACT.Sqrt).then_inc(s_sd, 1)

            def copy_out(name, dst, src):
                wait_filled(sc, name)
                empty_end(sc.activation(dst, src, ACT.Copy), name)

            def strips_out(name, dst, width):
                wait_filled(sc, name)
                for j in range(4):
                    ins = sc.activation(dst[0:META, 2, j * width:(j + 1) * width],
                                        job_bank(name)[32 * j:32 * j + META, 0:width], ACT.Copy)
                empty_end(ins, name)

            for t in range(2):
                copy_out(("mid", t), mid[:, t, :], job_bank(("mid", t))[:, 0:MID])
            sc.wait_ge(s_clear, 2)
            strips_out(("mid", 2), mid, MID // 4)
            sc.wait_ge(s_fz, 1)
            z, e = logf[:, 0, :], logf[:, 1, :]
            sc.activation(e, z, ACT.Abs).then_inc(s_ach, 1)
            sc.wait_ge(s_ach, 1)
            sc.activation(e, e, ACT.Exp, scale=-1.0).then_inc(s_ach, 1)
            sc.wait_ge(s_ach, 2)
            sc.activation(e, e, ACT.Ln, bias=1.0).then_inc(s_fl, 1)
            for t in range(3):
                wait_emptied(sc, ("mid", t))
            for t in range(2):
                sc.activation(rel[:, 0, 0:QRANK], mid[:, t, M_CQ:M_CQ + QRANK], ACT.Square,
                              accum_out=st[:, 8 + t:9 + t]).then_inc(s_mss, 1)
                sc.wait_ge(s_mss, t + 1)
            for t in range(3):
                sc.activation(rel[:, 0, 0:KVRANK], mid[:, t, M_CKV:M_CKV + KVRANK], ACT.Square,
                              accum_out=st[:, 10 + t:11 + t]).then_inc(s_mss, 1)
                sc.wait_ge(s_mss, t + 3)
            sc.wait_ge(s_mms, 1)
            sc.activation(st[:, 8:16], st[:, 8:16], ACT.Sqrt).then_inc(s_msd, 1)

            copy_out("ukT", ukT, job_bank("ukT")[:])
            for k in range(4):
                copy_out(("ka", k), kaT[:, k, :], job_bank(("ka", k))[:, 0:KEYS])
            for k in range(4):
                copy_out(("qa", k), qaT[:, k, :], job_bank(("qa", k))[:, 0:SEQ])
            for t in range(2):
                for n in range(2):
                    copy_out(("q", t, n), qtok[:, t, n * 512:(n + 1) * 512], job_bank(("q", t, n))[:])
            for k in range(4):
                name = ("kc", k)
                wait_filled(sc, name)
                sc.activation(kcat[0:NOPE, 2 * k, :], job_bank(name)[0:64, 0:KEYS], ACT.Copy)
                empty_end(sc.activation(kcat[0:NOPE, 2 * k + 1, :], job_bank(name)[64:128, 0:KEYS],
                                        ACT.Copy), name)
            copy_out(("va", 0), va[:, 0, :], job_bank(("va", 0)))
            for t in range(2):
                copy_out(("qiT", t), qiT[0:ID, :, t * P:(t + 1) * P],
                         job_bank(("qiT", t))[0:ID, :].rearrange("p (h k) -> p h k", h=IH))
            for n in range(2 * IH):
                t, h = divmod(n, IH)
                name = ("dots", t, h)
                if n >= 3:
                    sc.wait_ge(s_relu, n - 2)
                wait_filled(sc, name)
                ins = sc.activation(rel[:, n % 3, 0:WIDTH[t]], job_bank(name)[:, 0:WIDTH[t]], ACT.Relu,
                                    scale=IH ** -0.5 * ID ** -0.5)
                empty_end(ins, name)
            copy_out(("va", 1), va[:, 1, :], job_bank(("va", 1)))
            strips_out(("va", 2), va, P)
            for t in range(2):
                for n in range(2):
                    copy_out(("qT", t, n), qcat[0:QK, 4 * n:4 * n + 4, t * P:(t + 1) * P],
                             job_bank(("qT", t, n))[0:QK, :].rearrange("p (h k) -> p h k", h=4))
            for t in range(2):
                copy_out(("vb", t), vb[:, t, :], job_bank(("vb", t)))
            strips_out(("vb", 2), vb, P)
            def output_tile(n):
                sc.wait_ge(s_pv, 4 * n + 4)
                dst = (oaT if n < 2 else obT)[:, :, (n % 2) * P:(n % 2 + 1) * P]
                sc.activation(dst, bank[6 + n % 2].rearrange("p (c k) -> p c k", c=4), ACT.Copy).then_inc(s_on, 1)

            for i, (b, t, h) in enumerate(ITEMS):
                w = WIDTH[t]
                wait_emptied(sc, ("S", i))
                if i >= 3:
                    wait_filled(sc, ("PT", i - 3))
                sc.activation(pr[:, i % 3, 0:w], sm[:, i % 3, 0:w], ACT.Exp, scale=-1.0,
                              bias=st[:, 16 + i % 3:17 + i % 3],
                              accum_out=rk[:, i:i + 1]).then_inc(s_exp, 1)
                if i % 2 == 1:
                    name = ("gate", i // 2)
                    dst = (gaS if i < 16 else gbS)[:, i // 2 % CH, :]
                    wait_filled(sc, name)
                    empty_end(sc.activation(dst, job_bank(name)[:, 0:SEQ], ACT.Sigmoid), name)
                if i % 8 == 3 and i > 8:
                    output_tile(i // 8 - 1)
            output_tile(3)
            sc.activation(st[:, 60:61], st[:, 61:62], ACT.Sqrt)
            for t in range(2):
                for n in range(2):
                    wait_emptied(sc, ("out", t, n))
                sc.activation(gl[:, 0, 0:D], h1[:, t * D:(t + 1) * D], ACT.Square,
                              accum_out=st[:, 20 + t:21 + t]).then_inc(s_hss, 1)
                sc.wait_ge(s_hms, t + 1)
                sc.activation(st[:, 22 + t:23 + t], st[:, 22 + t:23 + t], ACT.Sqrt).then_inc(s_hsd, 1)
            sc.dma_start(bdn, b_dn[0]).then_inc(s_bdn, 16)
            sc.dma_start(gfin, norm_final_g.rearrange("(a n) -> a n", a=1).broadcast_to([P, D])).then_inc(s_gfin, 16)
            for t in range(2):
                sc.wait_ge(s_rmx, t + 1)
                sc.activation(rk[:, 64 + 32 * t:96 + 32 * t], rk[:, 32 * t:32 * t + 32], ACT.Exp,
                              bias=st[:, 24 + t:25 + t]).then_inc(s_rex, 1)

            sc.wait_ge(s_np, 1)
            n_pass = sc.value_load(npi[0:1, 0:1], min_val=1, max_val=SEQ // CAP)
            sc.wait_ge(s_gtf, 1)
            sc.activation(gatesT, bank[2][0:EXPERTS, 0:2 * P], ACT.Copy).then_inc(s_gt, 1)
            with sc.Fori(0, n_pass) as b:
                with sc.Fori(0, TURNS) as j:
                    turn = sc.snap(b * TURNS + j)
                    for u in range(UNROLL):
                        g = turn * UNROLL + u
                        sc.wait_ge(s_pgf, g + 1)
                        sc.activation(pickgT, bank[0][:, 0:2 * P], ACT.Copy).then_inc(s_pgt, 1)
                        for e in range(2):
                            gate_up_done(sc, turn, u, e)
                            sc.activation(gl[:, e, :], banks(2 + 2 * e, 4 + 2 * e), ACT.Copy).then_inc(s_gl, 1)
                            sc.wait_ge(s_glu, g * 2 + (e + 1))
                            sc.activation(sg[:, e, :], glu[:, e, :], ACT.Sigmoid, scale=1.702).then_inc(s_sig, 1)
                        down_done(sc, turn, u)
                        sc.activation(yr, banks(2, 4), ACT.Copy).then_inc(s_y, 1)
            sc.activation(st[:, 60:61], st[:, 61:62], ACT.Sqrt)
            for t in range(2):
                sc.wait_ge(s_acc, n_pass * (2 * PAIRS) + (t + 1))
                sc.activation(hs[:, t, :], h1[:, t * D:(t + 1) * D], ACT.Square,
                              accum_out=st[:, 28 + t:29 + t]).then_inc(s_fss, 1)
                sc.wait_ge(s_fms, t + 1)
                sc.activation(st[:, 30 + t:31 + t], st[:, 30 + t:31 + t], ACT.Sqrt).then_inc(s_fsd, 1)

        @block.vector
        def _(dve):
            v = nc.vector
            chain = [0]

            def link(ins):
                chain[0] += 1
                ins.then_inc(s_dch, 1)
                dve.wait_ge(s_dch, chain[0])

            def scaled(dst, src, vec, cols):
                return v.tensor_tensor(dst, src, vec.unsqueeze(2).broadcast_to([P] + cols), ALU.mult)

            def rope4(dst1, dst2, x1, x2, c, s, tmp):
                a, b_, c_, d_ = tmp
                v.tensor_tensor(a, x1, c, ALU.mult)
                v.tensor_tensor(b_, x2, s, ALU.mult)
                v.tensor_tensor(c_, x1, s, ALU.mult)
                link(v.tensor_tensor(d_, x2, c, ALU.mult))
                v.tensor_tensor(dst1, a, b_, ALU.subtract)
                return v.tensor_tensor(dst2, c_, d_, ALU.add)

            dve.wait_ge(s_x, 48)
            dve.wait_ge(s_clear, 1)
            link(v.tensor_tensor_reduce(out=xs[:, D:2 * D], in0=h1[:, D:2 * D], in1=h1[:, D:2 * D], scale=1.0,
                                        scalar=0.0, op0=ALU.mult, op1=ALU.add, accum_out=st[:, 1:2]))
            for n, tiles in enumerate(((0, 1), (2,))):
                a, e = tiles[0], tiles[-1] + 1
                dve.wait_ge(s_ss, n + 1)
                v.tensor_scalar(st[:, 3 + a:3 + e], st[:, a:e], 1.0 / D, EPS, ALU.mult,
                                ALU.add).then_inc(s_ms, 1)
                dve.wait_ge(s_sd, n + 1)
                link(v.reciprocal(st[:, 3 + a:3 + e], st[:, 3 + a:3 + e]))
                for t in tiles:
                    rows = TILES[t][0]
                    src = h1[:, t * D:(t + 1) * D] if t < 2 else xs[0:META, 2 * D:3 * D]
                    v.tensor_scalar(xs[0:rows, t * D:(t + 1) * D], src, st[0:rows, 3 + t:4 + t], None,
                                    ALU.mult).then_inc(s_xs, 1)
            wait_filled(dve, "vec")
            empty_end(v.tensor_copy(vT[:], job_bank("vec")[:, 0:V_ROWS]), "vec")
            wait_emptied(dve, "vec")
            for t, (rows, col) in enumerate(TILES):
                for n in range(2 if t < 2 else 1):
                    name = ("xT", t, n)
                    wait_filled(dve, name)
                    cs = 4 if t < 2 else CH
                    src = job_bank(name)[:, 0:cs * rows].rearrange("p (c k) -> p c k", c=cs)
                    empty_end(scaled(xnT[:, 4 * n:4 * n + cs, col:col + rows], src,
                                     vT[:, V_MIX + 4 * n:V_MIX + 4 * n + cs], [cs, rows]), name)
            wait_filled(dve, "bias")
            empty_end(v.tensor_copy(biasT[:], job_bank("bias")), "bias")
            dve.wait_ge(s_late, 80)
            for t in range(3):
                wait_emptied(dve, ("mid", t))
            z = logf[:, 0, :].rearrange("p (t h) -> p t h", t=3)
            v.tensor_tensor(z, mid[:, :, M_F:M_F + HEADS], bfor[:].unsqueeze(1).broadcast_to([P, 3, HEADS]),
                            ALU.add).then_inc(s_fz, 1)
            ki = mid[:, :, M_KI:M_KI + ID]
            kc = kk[:, :, 0:ID]
            link(v.tensor_reduce(st[:, 32:35], ki, AX.X, ALU.add))
            link(v.tensor_scalar(st[:, 32:35], st[:, 32:35], 1.0 / ID, None, ALU.mult))
            link(v.tensor_tensor(kc, ki, st[:, 32:35].unsqueeze(2).broadcast_to([P, 3, ID]), ALU.subtract))
            sqv = sq[:, 0:3 * ID].rearrange("p (t n) -> p t n", t=3)
            link(v.tensor_tensor(sqv, kc, kc, ALU.mult))
            link(v.tensor_reduce(st[:, 13:16], sqv, AX.X, ALU.add))
            dve.wait_ge(s_mss, 5)
            v.tensor_scalar(st[:, 8:10], st[:, 8:10], 1.0 / QRANK, EPS, ALU.mult, ALU.add)
            v.tensor_scalar(st[:, 10:13], st[:, 10:13], 1.0 / KVRANK, EPS, ALU.mult, ALU.add)
            v.tensor_scalar(st[:, 13:16], st[:, 13:16], 1.0 / ID, EPS, ALU.mult, ALU.add).then_inc(s_mms, 1)
            dve.wait_ge(s_fl, 1)
            v.scalar_tensor_tensor(logf[:, 2, :], logf[:, 0, :], 0.0, logf[:, 1, :], ALU.min,
                                   ALU.subtract).then_inc(s_logf, 1)
            dve.wait_ge(s_msd, 1)
            link(v.reciprocal(st[:, 8:16], st[:, 8:16]))
            for t in range(2):
                ins = v.tensor_scalar(mid[:, t, M_CQ:M_CQ + QRANK], mid[:, t, M_CQ:M_CQ + QRANK],
                                      st[:, 8 + t:9 + t], None, ALU.mult)
            ins.then_inc(s_cqn, 1)
            for t in range(3):
                ins = v.tensor_scalar(mid[:, t, M_CKV:M_CKV + KVRANK], mid[:, t, M_CKV:M_CKV + KVRANK],
                                      st[:, 10 + t:11 + t], None, ALU.mult)
            ins.then_inc(s_ckn, 1)
            link(v.tensor_tensor(kc, kc, st[:, 13:16].unsqueeze(2).broadcast_to([P, 3, ID]), ALU.mult))
            link(v.tensor_tensor(kc, kc, klng[:].unsqueeze(1).broadcast_to([P, 3, ID]), ALU.mult))
            link(v.tensor_tensor(kc, kc, klnb[:].unsqueeze(1).broadcast_to([P, 3, ID]), ALU.add))
            link(v.tensor_copy(kk[:, :, ID:ID + ROPE], mid[:, :, M_KR:M_KR + ROPE]))
            tmp3 = [rt[:, 48 * n:48 * n + 48].rearrange("p (t n) -> p t n", t=3) for n in range(8)]
            for n, o in enumerate((0, ID)):
                last = rope4(kk[:, :, o:o + 16], kk[:, :, o + 16:o + 32], kk[:, :, o:o + 16],
                             kk[:, :, o + 16:o + 32], cos, sin, tmp3[4 * n:4 * n + 4])
            last.then_inc(s_kk, 1)
            wait_filled(dve, ("cqT", 0))
            empty_end(scaled(cqT, job_bank(("cqT", 0))[:].rearrange("p (c k) -> p c k", c=2),
                             vT[:, V_Q:V_Q + 2], [2, SEQ]), ("cqT", 0))
            wait_filled(dve, ("ckvT", 0))
            empty_end(v.tensor_scalar(ckvT, job_bank(("ckvT", 0))[:, 0:KEYS], vT[:, V_KV:V_KV + 1], None,
                                      ALU.mult), ("ckvT", 0))
            wait_filled(dve, ("kkT", 0))
            v.tensor_copy(kiT[0:ID, :], job_bank(("kkT", 0))[0:ID, 0:KEYS])
            empty_end(v.tensor_copy(kcat[NOPE:QK, :, :],
                                    job_bank(("kkT", 0))[ID:ID + ROPE, 0:KEYS].unsqueeze(1)
                                    .broadcast_to([ROPE, HEADS, KEYS])), ("kkT", 0))
            wait_filled(dve, "FT")
            empty_end(v.tensor_scalar(nF[0:HEADS, :], job_bank("FT")[0:HEADS, 0:KEYS], -(HD ** 0.5), None,
                                      ALU.mult), "FT")
            for t in range(2):
                for n in range(2):
                    wait_emptied(dve, ("q", t, n))
                for n, (o, heads, per, off) in enumerate(((768, IH, ID, 0), (0, HEADS, QK, NOPE))):
                    grp = qtok[:, t, o:o + heads * per].rearrange("p (h n) -> p h n", h=heads)
                    x1, x2 = grp[:, :, off:off + 16], grp[:, :, off + 16:off + 32]
                    cs_ = cos[:, t, :].unsqueeze(1).broadcast_to([P, heads, 16])
                    sn_ = sin[:, t, :].unsqueeze(1).broadcast_to([P, heads, 16])
                    tmp = [rt[:, 512 * n + 128 * m:512 * n + 128 * m + 16 * heads]
                           .rearrange("p (h n) -> p h n", h=heads) for m in range(4)]
                    ins = rope4(x1, x2, x1, x2, cs_, sn_, tmp)
                    ins.then_inc(s_qr, 1)
                    dve.wait_ge(s_qr, 2 * t + n + 1)
            for n in range(2 * IH):
                t, h = divmod(n, IH)
                w = WIDTH[t]
                wait_emptied(dve, ("dots", t, h))
                base = cmask[:, KEYS - w:KEYS] if h == 0 else isc[:, t, 0:w]
                ins = v.scalar_tensor_tensor(isc[:, t, 0:w], rel[:, n % 3, 0:w],
                                             mid[:, t, M_IW + h:M_IW + h + 1], base, ALU.mult, ALU.add)
                ins.then_inc(s_relu, 1)
                dve.wait_ge(s_relu, n + 1)
            for t in range(2):
                w = WIDTH[t]
                for r in range(TOPK_SEL // 8):
                    src = isc[:, t, 0:w] if r == 0 else wrk[:, t, 0:w]
                    link(v.max(top8[:, 8 * t:8 * t + 8], src))
                    link(v.match_replace(wrk[:, t, 0:w], top8[:, 8 * t:8 * t + 8], src, TAKEN))
                v.tensor_scalar(selb[:, t, 0:w], wrk[:, t, 0:w], TAKEN / 2, NEG, ALU.is_gt,
                                ALU.mult).then_inc(s_sel, 1)
            dve.wait_ge(s_sel, 2)
            for i in range(len(ITEMS) + 2):
                if i < len(ITEMS):
                    b, t, h = ITEMS[i]
                    w = WIDTH[t]
                    mask = selb[:, t, 0:w] if b else fmask[:, KEYS - w:KEYS]
                    scale = (QK if b else HD) ** -0.5
                    if i >= 3:
                        dve.wait_ge(s_exp, i - 2)
                    wait_filled(dve, ("S", i))
                    ins = v.tensor_tensor_reduce(out=sm[:, i % 3, 0:w], in0=job_bank(("S", i))[:, 0:w],
                                                 in1=mask, scale=-scale, scalar=3e38, op0=ALU.add,
                                                 op1=ALU.min, accum_out=st[:, 16 + i % 3:17 + i % 3])
                    empty_end(ins, ("S", i))
                if 1 <= i <= len(ITEMS):
                    k = i - 1
                    w = WIDTH[ITEMS[k][1]]
                    dve.wait_ge(s_exp, k + 1)
                    link(v.reciprocal(rk[:, 32 + k:33 + k], rk[:, k:k + 1]))
                    v.tensor_scalar(pr[:, k % 3, 0:w], pr[:, k % 3, 0:w], rk[:, 32 + k:33 + k], None,
                                    ALU.mult).then_inc(s_pn, 1)
                if i >= 2:
                    k = i - 2
                    t = ITEMS[k][1]
                    if k >= 4:
                        dve.wait_ge(s_pv, (k - 4) // 2 + 1)
                    wait_filled(dve, ("PT", k))
                    src = job_bank(("PT", k))
                    v.tensor_copy(pT[0:META, k % 4, 2, :], src[0:META, 256:384])
                    empty_end(v.tensor_copy(pT[:, k % 4, 0:t + 1, :],
                                            src[:, 0:(t + 1) * P].rearrange("p (t k) -> p t k", t=t + 1)),
                              ("PT", k))
            for m in range(4):
                name = ("ba", m)
                wait_filled(dve, name)
                for k in range(2):
                    wait_emptied(dve, ("gate", 2 * m + k))
                dst = gaS[:, 2 * m:2 * m + 2, :].rearrange("p c k -> p (c k)")
                empty_end(v.tensor_tensor(dst, dst, job_bank(name)[:], ALU.mult), name)
            for m in range(4):
                name = ("bb", m)
                wait_filled(dve, name)
                for k in range(2):
                    wait_emptied(dve, ("gate", CH + 2 * m + k))
                a = gaS[:, 2 * m:2 * m + 2, :].rearrange("p c k -> p (c k)")
                b_ = gbS[:, 2 * m:2 * m + 2, :].rearrange("p c k -> p (c k)")
                ins = v.tensor_tensor(b_, b_, job_bank(name)[:], ALU.mult)
                empty_end(ins, name)
                wait_emptied(dve, name)
                v.tensor_tensor(a, a, b_, ALU.add).then_inc(s_mg, 1)
            rk3 = rank[:].rearrange("p (t e) -> p t e", t=2)
            gt3 = gates[:].rearrange("p (t e) -> p t e", t=2)

            def pick_pair(col):
                for t in range(2):
                    ins = v.tensor_tensor(pick[:, t, :].rearrange("p (e j) -> p e j", e=2),
                                          iota.unsqueeze(1).broadcast_to([P, 2, CAP]),
                                          rk3[:, t, col].unsqueeze(2).broadcast_to([P, 2, CAP]), ALU.is_equal)
                return ins

            def gate_pair(col):
                for t in range(2):
                    ins = v.tensor_tensor(pickg[:, t, :].rearrange("p (e j) -> p e j", e=2),
                                          pick[:, t, :].rearrange("p (e j) -> p e j", e=2),
                                          gt3[:, t, col].unsqueeze(2).broadcast_to([P, 2, CAP]), ALU.mult)
                return ins

            def gathered():
                scaled(xg, banks(0, 2).rearrange("p (c j) -> p c j", c=CH), vT[:, V_FFN:V_FFN + CH],
                       [CH, P]).then_inc(s_xg, 1)

            def add_rows(n):
                for t in range(2):
                    dve.wait_ge(s_sc, n * 2 + (t + 1))
                    half = h1[:, t * D:(t + 1) * D]
                    v.tensor_tensor(half, half, banks(4 + 2 * t, 6 + 2 * t), ALU.add).then_inc(s_acc, 1)

            lg = rk[:, 0:64].rearrange("p (t e) -> p t e", t=2)
            ex = rk[:, 64:128]
            wk = rk[:, 128:192]
            msk = rk[:, 192:256]

            def add_projected(t, n):
                name = ("out", t, n)
                wait_filled(dve, name)
                dst = h1[:, t * D + 512 * n:t * D + 512 * (n + 1)]
                empty_end(v.tensor_tensor(dst, dst, job_bank(name), ALU.add), name)

            def features_out(t, n):
                name = ("hT", t, n)
                wait_filled(dve, name)
                src = job_bank(name).rearrange("p (c k) -> p c k", c=4)
                empty_end(scaled(hT[:, 4 * n:4 * n + 4, t * P:(t + 1) * P], src,
                                 vT[:, V_FFN + 4 * n:V_FFN + 4 * n + 4], [4, P]), name)

            def row_scale(t):
                dve.wait_ge(s_hss, t + 1)
                v.tensor_scalar(st[:, 22 + t:23 + t], st[:, 20 + t:21 + t], 1.0 / D, EPS, ALU.mult,
                                ALU.add).then_inc(s_hms, 1)
                dve.wait_ge(s_hsd, t + 1)
                link(v.reciprocal(st[:, 22 + t:23 + t], st[:, 22 + t:23 + t]))

            def scale_rows(t):
                v.tensor_scalar(hs[:, t, :], h1[:, t * D:(t + 1) * D], st[:, 22 + t:23 + t], None,
                                ALU.mult).then_inc(s_hs, 1)

            def choose(t):
                name = ("router", t)
                wait_filled(dve, name)
                ins = v.scalar_tensor_tensor(lg[:, t, :], job_bank(name)[:, 0:EXPERTS], st[:, 22 + t:23 + t],
                                             brt[:], ALU.mult, ALU.add)
                empty_end(ins, name)
                wait_emptied(dve, name)
                m8 = top8[:, 8 * t:8 * t + 8]
                link(v.max(m8, lg[:, t, :]))
                v.tensor_scalar(st[:, 24 + t:25 + t], m8[:, 0:1], -1.0, None, ALU.mult).then_inc(s_rmx, 1)
                link(v.memset(m8[:, 4:8], 3e38))
                link(v.match_replace(wk[:, 32 * t:32 * t + 32], m8, lg[:, t, :], TAKEN))
                v.tensor_scalar(msk[:, 32 * t:32 * t + 32], wk[:, 32 * t:32 * t + 32], TAKEN / 2, None,
                                ALU.is_lt).then_inc(s_mask, 1)

            add_projected(0, 0)
            add_projected(0, 1)
            add_projected(1, 0)
            features_out(0, 0)
            features_out(0, 1)
            row_scale(0)
            scale_rows(0)
            add_projected(1, 1)
            choose(0)
            features_out(1, 0)
            features_out(1, 1)
            row_scale(1)
            choose(1)
            scale_rows(1)
            dve.wait_ge(s_mask, 2)
            wait_filled(dve, "rank")
            link(v.scalar_tensor_tensor(rk3[:, :, 0:EXPERTS],
                                        job_bank("rank")[:, 0:64].rearrange("p (t e) -> p t e", t=2), RANK0,
                                        msk.rearrange("p (t e) -> p t e", t=2), ALU.add, ALU.mult))
            pick_pair(slice(0, 2)).then_inc(s_pick0, 1)
            empty_end(v.tensor_reduce(npf[:, 3:4], job_bank("rank")[:, 64:96], AX.X, ALU.max), "rank")
            wait_emptied(dve, "rank")
            link(v.tensor_scalar(st[:, 48:49], npf[:, 3:4], float(CAP), 1.0, ALU.is_gt, ALU.add))
            for m in (2, 3):
                link(v.tensor_scalar(st[:, 49:50], npf[:, 3:4], float(m * CAP), None, ALU.is_gt))
                link(v.tensor_tensor(st[:, 48:49], st[:, 48:49], st[:, 49:50], ALU.add))
            v.tensor_copy(npi[:], st[:, 48:49]).then_inc(s_np, 1)
            dve.wait_ge(s_rex, 2)
            link(v.tensor_tensor(ex, ex, msk, ALU.mult))
            link(v.tensor_reduce(st[:, 26:28], ex.rearrange("p (t e) -> p t e", t=2), AX.X, ALU.add))
            link(v.reciprocal(st[:, 26:28], st[:, 26:28]))
            link(v.tensor_tensor(gt3[:, :, 0:EXPERTS], ex.rearrange("p (t e) -> p t e", t=2),
                                 st[:, 26:28].unsqueeze(2).broadcast_to([P, 2, EXPERTS]), ALU.mult))
            v.tensor_copy(gt3[:, :, EXPERTS:RCOLS], gt3[:, :, 0:2]).then_inc(s_gates, 1)
            dve.wait_ge(s_pick0, 1)
            gate_pair(slice(0, 2)).then_inc(s_pick, 1)
            link(v.tensor_scalar(rk3[:, :, EXPERTS:RCOLS], rk3[:, :, 0:2], -float(CAP), None, ALU.add))
            dve.wait_ge(s_gates, 1)
            dve.wait_ge(s_np, 1)
            n_pass = dve.value_load(npi[0:1, 0:1], min_val=1, max_val=SEQ // CAP)
            bias = biasT[:].rearrange("p (m e) -> p m e", e=EXPERTS)

            dve.wait_ge(s_gath, 1)
            gathered()
            add_rows(0)
            dve.wait_ge(s_acc, 2)
            STEPS = 9
            with dve.Fori(0, n_pass) as b:
                with dve.Fori(0, TURNS) as j:
                    turn = dve.snap(b * TURNS + j)
                    first = dve.snap(turn * (UNROLL * STEPS) + b)
                    step = [0]

                    def mlink(ins):
                        step[0] += 1
                        ins.then_inc(s_moe, 1)
                        dve.wait_ge(s_moe, first + step[0])

                    for u in range(UNROLL):
                        g = turn * UNROLL + u
                        pair = j * (2 * UNROLL) + 2 * u
                        dve.wait_ge(s_pgf, g + 1)
                        mlink(pick_pair(bass.ds(pair + 2, 2)))
                        gate_pair(bass.ds(pair + 2, 2)).then_inc(s_pick, 1)
                        for e in range(2):
                            rows = banks(6, 8).rearrange("p (m j) -> p m j", m=8)

                            def with_bias(dst, src, m):
                                return v.tensor_tensor(
                                    dst.rearrange("p (m j) -> p m j", m=8), src,
                                    bias[:, m:m + 8, bass.ds(pair + e, 1)].broadcast_to([P, 8, CAP]), ALU.add)
                            dve.wait_ge(s_tf, g * 2 + (e + 1))
                            mlink(with_bias(glu[:, e, :], rows[:, :, 0:CAP], 0))
                            v.tensor_scalar(glu[:, e, :], glu[:, e, :], 7.0, None, ALU.min).then_inc(s_glu, 1)
                            mlink(with_bias(lin[:, e, :], rows[:, :, CAP:2 * CAP], 8))
                            mlink(v.tensor_scalar(lin[:, e, :], lin[:, e, :], 7.0, -7.0, ALU.min, ALU.max))
                            dve.wait_ge(s_sig, g * 2 + (e + 1))
                            mlink(v.scalar_tensor_tensor(lin[:, e, :], lin[:, e, :], 1.0, glu[:, e, :],
                                                         ALU.add, ALU.mult))
                            v.tensor_tensor(act[:, e, :], lin[:, e, :], sg[:, e, :], ALU.mult).then_inc(s_act, 1)
                        dve.wait_ge(s_gath, g + 2)
                        gathered()
                        add_rows(g + 1)
                        dve.wait_ge(s_acc, g * 2 + 4)
                    assert step[0] == UNROLL * STEPS
                v.tensor_scalar(rank[:], rank[:], -float(CAP), None, ALU.add).then_inc(s_moe, 1)
                dve.wait_ge(s_moe, (b * TURNS + TURNS) * (UNROLL * STEPS) + (b + 1))

            dve.wait_ge(s_gfin, 16)
            for t in range(2):
                dve.wait_ge(s_fss, t + 1)
                v.tensor_scalar(st[:, 30 + t:31 + t], st[:, 28 + t:29 + t], 1.0 / D, EPS, ALU.mult,
                                ALU.add).then_inc(s_fms, 1)
                dve.wait_ge(s_fsd, t + 1)
                link(v.reciprocal(st[:, 30 + t:31 + t], st[:, 30 + t:31 + t]))
                v.scalar_tensor_tensor(fin[:, t, :], h1[:, t * D:(t + 1) * D], st[:, 30 + t:31 + t], gfin,
                                       ALU.mult, ALU.mult).then_inc(s_fin, 1)

        @block.tensor
        def _(pe):
            mm = nc.tensor.matmul
            tr = nc.tensor.transpose
            def loaded(n):
                pe.wait_ge(slot_loaded[n % NSLOT], 16 * (n // NSLOT + 1))

            def used(last, n):
                last.then_inc(slot_used[place(n)], 1)

            def win(n, width=256):
                return slot(n)[:, 0:CH * width].rearrange("p (c n) -> p c n", c=CH)

            pe.wait_ge(s_idn, 16)
            pe.wait_ge(s_vec, 64)
            fill_end(tr(job_bank("vec")[:, 0:V_ROWS], vraw[0:V_ROWS, :], ident[0:V_ROWS, 0:V_ROWS]), "vec")
            for t, (rows, col) in enumerate(TILES):
                pe.wait_ge(s_xs, t + 1)
                for n in range(2 if t < 2 else 1):
                    name = ("xT", t, n)
                    fill_begin(pe, name)
                    for c in range(4 if t < 2 else CH):
                        ins = tr(job_bank(name)[:, c * rows:(c + 1) * rows],
                                 xs[0:rows, t * D + (4 * n + c) * P:t * D + (4 * n + c + 1) * P],
                                 ident[0:rows, 0:rows])
                    fill_end(ins, name)
            pe.wait_ge(s_bias, 16)
            fill_begin(pe, "bias")
            for m in range(16):
                ins = tr(job_bank("bias")[:, m * EXPERTS:(m + 1) * EXPERTS], braw[:, m * P:(m + 1) * P],
                         ident[0:EXPERTS, 0:EXPERTS])
            fill_end(ins, "bias")
            for t in range(3):
                wait_emptied(pe, ("xT", t, 0))
                if t < 2:
                    wait_emptied(pe, ("xT", t, 1))
            half = MID // 2
            for t, (rows, col) in enumerate(TILES[0:2]):
                name = ("mid", t)
                fill_begin(pe, name)
                for s in range(2):
                    loaded(s)
                    for c in range(CH):
                        ins = mm(job_bank(name)[:, s * half:(s + 1) * half], xnT[:, c, col:col + rows],
                                 win(s, half)[:, c, :], start=c == 0, stop=c == CH - 1)
                fill_end(ins, name)

            def meta_strips(name, width, weight):
                fill_begin(pe, name)
                chunks = CH if weight(0, 1) is not None else 1
                for c in range(chunks):
                    for j in range(4):
                        lhs = xnT[:, c, 0:META] if chunks > 1 else ckvT[:, 0:META]
                        ins = mm(job_bank(name)[32 * j:32 * j + META, 0:width], lhs, weight(j, c),
                                 start=c == 0, stop=c == chunks - 1)
                fill_end(ins, name)

            q = MID // 4
            meta_strips(("mid", 2), q, lambda j, c: win(j // 2, half)[:, c, (j % 2) * q:(j % 2 + 1) * q])
            pe.wait_ge(s_kst, 16)
            pe.wait_ge(s_mixw, 64)
            fill_begin(pe, "ukT")
            for k in range(4):
                ins = tr(job_bank("ukT")[:, k * P:(k + 1) * P], wuk[:, k * P:(k + 1) * P], ident)
            fill_end(ins, "ukT")

            def feature_major(name, s, k, cols, width):
                fill_begin(pe, name)
                loaded(s)
                for c in range(CH):
                    ins = mm(job_bank(name)[:, 0:width], win(s)[:, c, k * P:(k + 1) * P],
                             xnT[:, c, cols:cols + width], start=c == 0, stop=c == CH - 1)
                fill_end(ins, name)

            for k in range(4):
                feature_major(("ka", k), 2 + k // 2, k % 2, 0, KEYS)
            name = ("cqT", 0)
            fill_begin(pe, name)
            pe.wait_ge(s_cqn, 1)
            for c in range(2):
                for t in range(2):
                    ins = tr(job_bank(name)[:, c * SEQ + t * P:c * SEQ + (t + 1) * P],
                             mid[:, t, M_CQ + c * P:M_CQ + (c + 1) * P], ident)
            fill_end(ins, name)
            name = ("ckvT", 0)
            fill_begin(pe, name)
            pe.wait_ge(s_ckn, 1)
            for t, (rows, col) in enumerate(TILES):
                ins = tr(job_bank(name)[:, col:col + rows], mid[0:rows, t, M_CKV:M_CKV + KVRANK],
                         ident[0:rows, 0:rows])
            fill_end(ins, name)
            for k in range(4):
                feature_major(("qa", k), 4 + k // 2, k % 2, META, SEQ)
            name = ("kkT", 0)
            fill_begin(pe, name)
            pe.wait_ge(s_kk, 1)
            for t, (rows, col) in enumerate(TILES):
                ins = tr(job_bank(name)[0:QK, col:col + rows], kk[0:rows, t, :], ident[0:rows, 0:rows])
            fill_end(ins, name)
            fill_begin(pe, "FT")
            pe.wait_ge(s_logf, 1)
            lf = logf[:, 2, :].rearrange("p (t h) -> p t h", t=3)
            FT = job_bank("FT")
            for t, (rows, col) in ((2, TILES[2]), (0, TILES[0]), (1, TILES[1])):
                terms = [(lf[0:rows, t, :], ltri[0:rows, 0:rows]), (lf[0:rows, t, :], ident[0:rows, 0:rows])]
                if t < 2:
                    terms.append((lf[0:META, 2, :], ones[0:META, 0:rows]))
                if t == 1:
                    terms.append((lf[:, 0, :], ones[:, 0:rows]))
                for n, (a, b_) in enumerate(terms):
                    ins = mm(FT[0:HEADS, col:col + rows], a, b_, start=n == 0, stop=n == len(terms) - 1)
            fill_end(ins, "FT")
            wait_emptied(pe, ("cqT", 0))
            for t in range(2):
                for n in range(2):
                    name = ("q", t, n)
                    fill_begin(pe, name)
                    for c in range(2):
                        ins = mm(job_bank(name)[:], cqT[:, c, t * P:(t + 1) * P],
                                 wq[:, c, n * 512:(n + 1) * 512], start=c == 0, stop=c == 1)
                    fill_end(ins, name)
            wait_emptied(pe, ("ckvT", 0))
            wait_emptied(pe, "ukT")
            for k in range(4):
                name = ("kc", k)
                fill_begin(pe, name)
                fill_end(mm(job_bank(name)[:, 0:KEYS], ukT[:, k * P:(k + 1) * P], ckvT, start=True,
                            stop=True), name)

            def fox_values(t):
                name = ("va", t)
                rows, col = TILES[t]
                fill_begin(pe, name)
                for s in range(2):
                    loaded(6 + s)
                    for c in range(CH):
                        ins = mm(job_bank(name)[:, s * 256:(s + 1) * 256], xnT[:, c, col:col + rows],
                                 win(6 + s)[:, c, :], start=c == 0, stop=c == CH - 1)
                fill_end(ins, name)

            fox_values(0)
            pe.wait_ge(s_qr, 4)
            for t in range(2):
                name = ("qiT", t)
                fill_begin(pe, name)
                for h in range(IH):
                    ins = tr(job_bank(name)[0:ID, h * P:(h + 1) * P],
                             qtok[:, t, 768 + h * ID:768 + (h + 1) * ID], ident)
                fill_end(ins, name)
            wait_emptied(pe, ("kkT", 0))
            for t in range(2):
                wait_emptied(pe, ("qiT", t))
                for h in range(IH):
                    name = ("dots", t, h)
                    fill_begin(pe, name)
                    fill_end(mm(job_bank(name)[:, 0:WIDTH[t]], qiT[0:ID, h, t * P:(t + 1) * P],
                                kiT[0:ID, 0:WIDTH[t]], start=True, stop=True), name)
            fox_values(1)
            meta_strips(("va", 2), P, lambda j, c: win(6 + j // 2)[:, c, (j % 2) * P:(j % 2 + 1) * P])
            for t in range(2):
                for n in range(2):
                    name = ("qT", t, n)
                    fill_begin(pe, name)
                    for h in range(4):
                        ins = tr(job_bank(name)[0:QK, h * P:(h + 1) * P],
                                 qtok[:, t, (4 * n + h) * QK:(4 * n + h + 1) * QK], ident)
                    fill_end(ins, name)
            for t, (rows, col) in enumerate(TILES[0:2]):
                name = ("vb", t)
                fill_begin(pe, name)
                fill_end(mm(job_bank(name), ckvT[:, col:col + rows], wuv, start=True, stop=True), name)
            meta_strips(("vb", 2), P, lambda j, c: wuv[:, j * P:(j + 1) * P] if c == 0 else None)
            for name in [("ka", 3), ("qa", 3), "FT"] + [("kc", k) for k in range(4)] \
                    + [("va", t) for t in range(3)]:
                wait_emptied(pe, name)

            def scores(i):
                b, t, h = ITEMS[i]
                w = WIDTH[t]
                name = ("S", i)
                fill_begin(pe, name)
                dst = job_bank(name)[:, 0:w]
                if b == 0:
                    r = (h % 2) * HD
                    mm(dst, qaT[r:r + HD, h // 2, t * P:(t + 1) * P], kaT[r:r + HD, h // 2, 0:w],
                       start=True, stop=False)
                    ins = mm(dst, ident[0:HEADS, h:h + 1].broadcast_to([HEADS, P]), nF[0:HEADS, 0:w],
                             start=False, stop=True)
                else:
                    if h == 0:
                        for n in range(2):
                            wait_emptied(pe, ("qT", t, n))
                    ins = mm(dst, qcat[0:QK, h, t * P:(t + 1) * P], kcat[0:QK, h, 0:w], start=True,
                             stop=True)
                fill_end(ins, name)

            def transposed(i):
                b, t, h = ITEMS[i]
                name = ("PT", i)
                fill_begin(pe, name)
                pe.wait_ge(s_pn, i + 1)
                for k in range(t + 1):
                    tr(job_bank(name)[:, k * P:(k + 1) * P], pr[:, i % 3, META + k * P:META + (k + 1) * P],
                       ident)
                fill_end(tr(job_bank(name)[0:META, 256:384], pr[:, i % 3, 0:META], ident), name)

            def values(j):
                b, t, h = ITEMS[2 * j]
                n = 2 * b + t
                if h == 0 and n >= 2:
                    pe.wait_ge(s_on, n - 1)
                if j == 8:
                    for m in range(3):
                        wait_emptied(pe, ("vb", m))
                for u in range(2):
                    wait_emptied(pe, ("PT", 2 * j + u))
                vv = vb if b else va
                for k in list(range(t + 1)) + [2]:
                    rows = META if k == 2 else P
                    for u in range(2):
                        ins = mm(bank[6 + n % 2][u * HD:(u + 1) * HD, (h // 2) * P:(h // 2 + 1) * P],
                                 vv[0:rows, k, (h + u) * HD:(h + u + 1) * HD],
                                 pT[0:rows, (2 * j + u) % 4, k, :], start=k == 0, stop=k == 2)
                ins.then_inc(s_pv, 1)

            for i in range(len(ITEMS) + 3):
                if i < len(ITEMS):
                    scores(i)
                if i >= 4 and i % 2 == 0:
                    values(i // 2 - 2)
                if 2 <= i < len(ITEMS) + 2:
                    transposed(i - 2)
                if i % 2 == 1 and i < len(ITEMS):
                    m = i // 2
                    name = ("gate", m)
                    fill_begin(pe, name)
                    loaded(8 + m // 2)
                    for c in range(CH):
                        ins = mm(job_bank(name)[:, 0:SEQ], win(8 + m // 2)[:, c, (m % 2) * P:(m % 2 + 1) * P],
                                 xnT[:, c, META:KEYS], start=c == 0, stop=c == CH - 1)
                    fill_end(ins, name)
            for b, (kind, src, s0) in enumerate((("ba", oaT, 16), ("bb", obT, 18))):
                pe.wait_ge(s_on, 2 * b + 2)
                loaded(s0)
                loaded(s0 + 1)
                for m in range(4):
                    name = (kind, m)
                    fill_begin(pe, name)
                    for k in range(2):
                        for c in range(4):
                            w = slot(s0 + c // 2).rearrange("p (k n) -> p k n", k=2)[:, c % 2, :]
                            ins = mm(job_bank(name)[:, k * SEQ:(k + 1) * SEQ],
                                     w[:, (2 * m + k) * P:(2 * m + k + 1) * P], src[:, c, :],
                                     start=c == 0, stop=c == 3)
                    fill_end(ins, name)

            def project(t, n):
                name = ("out", t, n)
                fill_begin(pe, name)
                for c in range(CH):
                    if t == 0 and n == 0 and c % 2 == 0:
                        pe.wait_ge(s_mg, c // 2 + 1)
                        loaded(20 + c // 2)
                    w = slot(20 + c // 2).rearrange("p (k n) -> p k n", k=2)[:, c % 2, :]
                    ins = mm(job_bank(name), gaS[:, c, t * P:(t + 1) * P], w[:, n * 512:(n + 1) * 512],
                             start=c == 0, stop=c == CH - 1)
                fill_end(ins, name)

            def residual_features(t, n):
                name = ("hT", t, n)
                fill_begin(pe, name)
                wait_emptied(pe, ("out", t, n))
                for c in range(4):
                    ins = tr(job_bank(name)[:, c * P:(c + 1) * P],
                             h1[:, t * D + (4 * n + c) * P:t * D + (4 * n + c + 1) * P], ident)
                fill_end(ins, name)

            def route(t):
                name = ("router", t)
                fill_begin(pe, name)
                for n in range(2):
                    wait_emptied(pe, ("hT", t, n))
                wrv = wr[:].rearrange("p (c e) -> p c e", c=CH)
                for c in range(CH):
                    ins = mm(job_bank(name)[:, 0:EXPERTS], hT[:, c, t * P:(t + 1) * P], wrv[:, c, :],
                             start=c == 0, stop=c == CH - 1)
                fill_end(ins, name)

            project(0, 0)
            project(0, 1)
            project(1, 0)
            residual_features(0, 0)
            residual_features(0, 1)
            project(1, 1)
            pe.wait_ge(s_late, 80)
            route(0)
            residual_features(1, 0)
            residual_features(1, 1)
            route(1)
            fill_begin(pe, "rank")
            pe.wait_ge(s_mask, 2)
            mk = [rk[:, 192 + 32 * t:224 + 32 * t] for t in range(2)]
            rb = job_bank("rank")
            mm(rb[:, 0:32], ltri, mk[0], start=True, stop=True)
            mm(rb[:, 32:64], ones, mk[0], start=True, stop=False)
            mm(rb[:, 32:64], ltri, mk[1], start=False, stop=True)
            mm(rb[:, 64:96], ones, mk[0], start=True, stop=False)
            fill_end(mm(rb[:, 64:96], ones, mk[1], start=False, stop=True), "rank")

            def gather():
                for c in range(CH):
                    for t in range(2):
                        ins = mm(bank[c // 4][:, (c % 4) * P:(c % 4 + 1) * P],
                                 hs[:, t, c * P:(c + 1) * P], pick[:, t, :], start=t == 0, stop=t == 1)
                ins.then_inc(s_gath, 1)

            last_jobs = {JOB[name] % ROT: name for name in JOBS[-ROT:]}
            for n in (0, 1):
                wait_emptied(pe, last_jobs[n])
            pe.wait_ge(s_pick0, 1)
            pe.wait_ge(s_hs, 2)
            gather()
            for n in range(2, ROT):
                wait_emptied(pe, last_jobs[n])
            pe.wait_ge(s_gates, 1)
            gt3 = gates[:].rearrange("p (t e) -> p t e", t=2)
            for t in range(2):
                ins = tr(bank[2][0:EXPERTS, t * P:(t + 1) * P], gt3[:, t, 0:EXPERTS], ident)
            ins.then_inc(s_gtf, 1)
            pe.wait_ge(s_gt, 1)
            pe.wait_ge(s_bdn, 16)
            for t in range(2):
                for n in range(2):
                    ins = mm(bank[4 + 2 * t + n], gatesT[:, t * P:(t + 1) * P], bdn[:, n * 512:(n + 1) * 512],
                             start=True, stop=True)
                ins.then_inc(s_sc, 1)

            def expert_pair(turn, u):
                g = turn * UNROLL + u
                base = PAIR_LOADS * u

                def arrived(k):
                    n = place(base + k)
                    before = MIX_LOADS // NSLOT if n < NSLOT else 0
                    pe.wait_ge(slot_loaded[n], turn * (16 * USES) + 16 * (before + (base + k) // ESLOT + 1))

                def features(e):
                    pe.wait_ge(s_gl, g * 2 + (e + 1))
                    for m in range(CH):
                        ins = tr(bank[6 + m // 4][:, (m % 4) * P:(m % 4 + 1) * P],
                                 gl[:, e, m * P:(m + 1) * P], ident)
                    ins.then_inc(s_tf, 1)

                pe.wait_ge(s_xg, g + 1)
                pe.wait_ge(s_pick, g + 1)
                for t in range(2):
                    ins = tr(bank[0][:, t * P:(t + 1) * P], pickg[:, t, :], ident)
                ins.then_inc(s_pgf, 1)
                for e in range(2):
                    if e == 1:
                        pe.wait_ge(s_acc, g * 2 + 2)
                    for c in range(CH):
                        k = 8 * e + c
                        arrived(k)
                        for n in range(2):
                            for h in range(2):
                                ins = mm(bank[2 + 2 * e + n][h * CAP:(h + 1) * CAP, :],
                                         xg[:, c, e * CAP:(e + 1) * CAP],
                                         eslot(base + k)[:, h * D + n * 512:h * D + (n + 1) * 512],
                                         start=c == 0, stop=c == CH - 1)
                        used(ins, base + k)
                        if e == 1 and c == 1:
                            features(0)
                pe.wait_ge(s_pick, g + 2)
                pe.wait_ge(s_pgt, g + 1)
                gather()
                pe.wait_ge(s_act, g * 2 + 1)
                features(1)
                pe.wait_ge(s_act, g * 2 + 2)
                for c in range(CH):
                    for e in range(2):
                        if c % 2 == 0:
                            arrived(16 + 2 * (c // 2) + e)
                    for n in range(2):
                        for e in range(2):
                            k = base + 16 + 2 * (c // 2) + e
                            ins = mm(bank[2 + n][e * CAP:(e + 1) * CAP, :],
                                     act[:, e, c * CAP:(c + 1) * CAP],
                                     eslot(k)[:, (c % 2) * D + n * 512:(c % 2) * D + (n + 1) * 512],
                                     start=c == 0, stop=c == CH - 1)
                            if c % 2 and n:
                                used(ins, k)
                pe.wait_ge(s_y, g + 1)
                for t in range(2):
                    for n in range(2):
                        ins = mm(bank[4 + 2 * t + n], pickgT[:, t * P:(t + 1) * P],
                                 yr[:, n * 512:(n + 1) * 512], start=True, stop=True)
                    ins.then_inc(s_sc, 1)

            pe.wait_ge(s_np, 1)
            n_pass = pe.value_load(npi[0:1, 0:1], min_val=1, max_val=SEQ // CAP)
            with pe.Fori(0, n_pass) as b:
                with pe.Fori(0, TURNS) as j:
                    turn = pe.snap(b * TURNS + j)
                    for u in range(UNROLL):
                        expert_pair(turn, u)


_INS = ['x', 'meta_tokens', 'w_in', 'b_forget', 'w_uq', 'w_uk', 'w_uv', 'w_qidx', 'kidx_ln_g', 'kidx_ln_b',
        'w_branch_a', 'w_branch_b', 'w_out', 'norm_mix_g', 'norm_ffn_g', 'q_norm_g', 'kv_norm_g',
        'w_router', 'b_router', 'w_gate_up', 'b_gate_up', 'w_down', 'b_down', 'norm_final_g']


def _constants(np):
    k = np.zeros((P, KCOLS), np.float32)
    r = np.arange(P)
    k[:, K_ID:K_ID + P] = np.eye(P)
    k[:, K_LT:K_LT + P] = r[:, None] < r[None, :]
    k[:, K_ONE:K_ONE + P] = 1.0
    k[:, K_FM + KEYS - P:K_FM + KEYS] = np.where(r[None, :] > r[:, None], NEG, 0.0)
    k[0:64, K_CM + KEYS - 64:K_CM + KEYS] = NEG
    k[:, K_IOTA:K_IOTA + CAP] = RANK0 + np.arange(CAP)
    half = ROPE // 2
    inv = (np.float32(10000.0) ** (-np.arange(half, dtype=np.float32) / np.float32(half))).astype(np.float32)
    for t, (rows, col) in enumerate(TILES):
        ang = ((col + r).astype(np.float32)[:, None] * inv[None, :]).astype(np.float32)
        k[:, K_COS + half * t:K_COS + half * (t + 1)] = np.cos(ang.astype(np.float64))
        k[:, K_SIN + half * t:K_SIN + half * (t + 1)] = np.sin(ang.astype(np.float64))
    return k


def kernel(**inputs):
    import numpy as _np
    import concourse.bacc as _bacc
    from concourse import mybir as _mybir
    from concourse.bass_utils import run_bass_kernel_spmd as _run

    nc = _bacc.Bacc("TRN2", target_bir_lowering=False, num_devices=1)
    arrays, aps = {}, {}
    for name in _INS:
        a = _np.ascontiguousarray(inputs[name])
        arrays[f"in_{name}"] = a
        aps[name] = nc.dram_tensor(f"in_{name}", a.shape, _mybir.dt.from_np(a.dtype), kind="ExternalInput").ap()
    consts = _constants(_np)
    arrays["consts"] = consts
    aps["consts"] = nc.dram_tensor("consts", consts.shape, _mybir.dt.float32, kind="ExternalInput").ap()
    out = nc.dram_tensor("out", (1, SEQ, D), _mybir.dt.float32, kind="ExternalOutput").ap()
    a = aps
    build(nc, a['x'], a['meta_tokens'], a['w_in'], a['b_forget'], a['w_uq'], a['w_uk'], a['w_uv'],
          a['w_qidx'], a['kidx_ln_g'], a['kidx_ln_b'], a['w_branch_a'], a['w_branch_b'], a['w_out'],
          a['norm_mix_g'], a['norm_ffn_g'], a['q_norm_g'], a['kv_norm_g'], a['w_router'], a['b_router'],
          a['w_gate_up'], a['b_gate_up'], a['w_down'], a['b_down'], a['norm_final_g'], a['consts'], out)
    r = _run(nc, [arrays], core_ids=[0])
    return r.results[0]["out"]
```

```python
import concourse.bass as bass
from concourse import mybir
from contextlib import ExitStack

P = 128
D = 1024
SEQ = 256
META = 16
KEYS = META + SEQ
CH = D // P
HEADS = 8
HD = 64
NOPE, ROPE = 64, 32
QK = NOPE + ROPE
QRANK, KVRANK = 256, 128
IH, ID = 4, 64
TOPK_SEL = 64
EXPERTS, TOPK = 32, 4
ARENA = 31800
CAP = 64
PAIRS = EXPERTS // 2
RCOLS = EXPERTS + 2
EPS = 1e-6
NEG = -1e30
RANK0 = 1000.0
TAKEN = -3e38

C_QA, C_KA, C_VA, C_MID = 0, 512, 1024, 1536
MID = 8 + QRANK + KVRANK + ROPE + ID + IH
C_GA = C_MID + MID
C_GB = C_GA + D
M_F, M_CQ, M_CKV, M_KR, M_KI, M_IW = 0, 8, 264, 392, 424, 488

TILES = [(P, META), (P, META + P), (META, 0)]
WIDTH = [META + P, META + 2 * P]

K_ID, K_LT, K_ONE, K_FM, K_CM, K_IOTA, K_COS, K_SIN = 0, 128, 256, 384, 656, 928, 992, 1040
K_THR = 1088
KCOLS = 1092

SLOT = 2048
NSLOT = 8
ESLOT = 16
MIX_LOADS = 24
PAIR_LOADS = 24
UNROLL = 2
TURNS = PAIRS // UNROLL
USES = UNROLL * PAIR_LOADS // ESLOT
LAST_READ = [("mid", 2)] * 2 + [("ka", 1), ("ka", 3), ("qa", 1), ("qa", 3)] + [("va", 2)] * 2 \
    + [("gate", 2 * m + 1) for m in range(8)] + [("ba", 3)] * 2 + [("bb", 3)] * 2 \
    + [None] * 2 + [("out", 1, 1)] * 2

V_MIX, V_FFN, V_Q, V_KV, V_ROWS = 0, 8, 16, 18, 19
LATENT = 32


def mixer_jobs():
    jobs = ["vec"]
    jobs += [("xT", 0, 0), ("xT", 0, 1), ("mid", 0), ("xT", 1, 0), ("xT", 1, 1), ("mid", 1)]
    jobs += [("xT", 2, 0), ("mid", 2), "vec2"]
    jobs += [("ka", k) for k in range(4)]
    jobs += [("cqT", 0), ("ckvT", 0)]
    jobs += [("qa", k) for k in range(4)]
    jobs += ["ukT", ("kkT", 0), "FT"]
    jobs += [("q", t, n) for t in range(2) for n in range(2)]
    jobs += [("kc", k) for k in range(4)]
    jobs += [("va", 0)]
    jobs += [("qiT", t) for t in range(2)]
    jobs += [("dots", t, h) for t in range(2) for h in range(IH)]
    jobs += [("va", 1), ("va", 2)]
    jobs += [("qT", t, n) for t in range(2) for n in range(2)]
    jobs += [("vb", t) for t in range(3)]
    items = attention_items()
    for i in range(len(items) + 2):
        if i < len(items):
            jobs.append(("S", i))
        if i >= 2:
            jobs.append(("PT", i - 2))
        if i % 2 == 1 and i < len(items):
            jobs.append(("gate", i // 2))
    jobs += [("ba", m) for m in range(4)]
    jobs += [("bb", m) for m in range(4)]
    jobs += [("out", 0, 0), ("out", 0, 1), ("out", 1, 0), ("out", 1, 1)]
    jobs += [("hT", 0, 0), ("hT", 0, 1), ("hT", 1, 0), ("hT", 1, 1)]
    return jobs


def attention_items():
    return [(b, t, h) for b in range(2) for t in range(2) for h in range(HEADS)]


WARM_UP = 3
ROT = 6


def build(nc, x, meta, w_in, b_forget, w_uq, w_uk, w_uv, w_qidx, kln_g, kln_b, w_a, w_b, w_out,
          norm_mix_g, norm_ffn_g, q_norm_g, kv_norm_g, w_router, b_router, w_gu, b_gu, w_dn, b_dn,
          norm_final_g, consts, out):
    f32, i32 = mybir.dt.float32, mybir.dt.int32
    ALU, ACT, AX = mybir.AluOpType, mybir.ActivationFunctionType, mybir.AxisListType

    JOBS = mixer_jobs()
    JOB = {name: n for n, name in enumerate(JOBS)}
    ITEMS = attention_items()

    ctx = ExitStack()
    with ctx:
        def sb(name, cols, dt=f32):
            return ctx.enter_context(nc.sbuf_tensor(name, [P, cols], dt))

        def sem(name):
            return ctx.enter_context(nc.semaphore(name))

        ring = sb("ring", NSLOT * SLOT)
        kst = sb("kst", KCOLS)
        h1 = sb("h1", 2 * D)
        vraw = sb("vraw", P)
        vT = sb("vT", V_ROWS)
        biasT = sb("biasT", 16 * EXPERTS)
        wr = sb("wr", CH * EXPERTS)
        bfor = sb("bfor", HEADS)
        klng = sb("klng", ID)
        klnb = sb("klnb", ID)
        brt = sb("brt", EXPERTS)
        st = sb("st", 64)
        rk = sb("rk", 8 * EXPERTS)
        gates = sb("gates", 2 * RCOLS)
        rank = sb("rank", 2 * RCOLS)
        top8 = sb("top8", 16)
        npi = sb("npi", 1, i32)

        arena = sb("arena", ARENA)
        at = [0]

        def take(n):
            at[0] += n
            assert at[0] <= ARENA, at[0]
            return arena[:, at[0] - n:at[0]]

        xs = take(3 * D)
        qaT = xs[:, 0:HEADS * SEQ].rearrange("p (h k) -> p h k", h=HEADS)
        nF = take(KEYS)
        kiT = take(KEYS)
        isc = take(2 * KEYS)
        mid = take(3 * MID).rearrange("p (t n) -> p t n", t=3)
        qiT = take(IH * SEQ).rearrange("p (h k) -> p h k", h=IH)
        wuv = take(512)
        wuk = take(512)
        cqT = take(2 * SEQ).rearrange("p (c k) -> p c k", c=2)
        ckvT = take(KEYS)
        kk = take(3 * 96).rearrange("p (t n) -> p t n", t=3)
        sq = take(3 * 96)
        logf = take(4 * 24)
        gaS = take(CH * SEQ)
        gbS = take(CH * SEQ)
        oaT = take(4 * SEQ).rearrange("p (c k) -> p c k", c=4)
        obT = take(4 * SEQ).rearrange("p (c k) -> p c k", c=4)
        at[0] = tail = max(at[0], 15 * D)
        xnT = take(CH * KEYS).rearrange("p (c k) -> p c k", c=CH)
        qcat = take(HEADS * SEQ)
        kcat = take(HEADS * KEYS)
        va = take(3 * 512).rearrange("p (t n) -> p t n", t=3)
        vb = take(3 * 512).rearrange("p (t n) -> p t n", t=3)
        kaT = take(HEADS * KEYS).rearrange("p (h k) -> p h k", h=HEADS)
        pT = take(4 * 384)
        pr = take(3 * KEYS)
        sm = take(3 * KEYS)
        selb = take(2 * KEYS)
        wrk = take(2 * KEYS)
        ukT = take(512)
        assert at[0] - tail >= (ESLOT - NSLOT) * SLOT
        more = arena[:, tail:tail + (ESLOT - NSLOT) * SLOT]
        rel = oaT.rearrange("p c k -> p (c k)")[:, 0:3 * KEYS]
        wq = gaS.rearrange("p (c n) -> p c n", c=2)
        qtok = gbS.rearrange("p (t n) -> p t n", t=2)
        rt = xs[:, 2048:2048 + 1024]
        gaS = gaS.rearrange("p (c k) -> p c k", c=CH)
        gbS = gbS.rearrange("p (c k) -> p c k", c=CH)
        qcat = qcat.rearrange("p (h k) -> p h k", h=HEADS)
        kcat = kcat.rearrange("p (h k) -> p h k", h=HEADS)
        isc = isc.rearrange("p (t k) -> p t k", t=2)
        wrk = wrk.rearrange("p (t k) -> p t k", t=2)
        selb = selb.rearrange("p (t k) -> p t k", t=2)
        pr = pr.rearrange("p (t k) -> p t k", t=3)
        sm = sm.rearrange("p (t k) -> p t k", t=3)
        rel = rel.rearrange("p (t k) -> p t k", t=3)
        pT = pT.rearrange("p (b t k) -> p b t k", b=4, t=3)
        logf = logf.rearrange("p (a n) -> p a n", a=4)

        at[0] = 0
        hs = take(2 * D).rearrange("p (t n) -> p t n", t=2)
        hT = take(CH * SEQ).rearrange("p (c k) -> p c k", c=CH)
        xg = take(CH * P).rearrange("p (c j) -> p c j", c=CH)
        braw = arena[0:EXPERTS, at[0]:at[0] + 2 * D]
        gl = take(2 * D).rearrange("p (e n) -> p e n", e=2)
        glu = take(2 * 512).rearrange("p (e n) -> p e n", e=2)
        lin = take(2 * 512).rearrange("p (e n) -> p e n", e=2)
        sg = take(2 * 512).rearrange("p (e n) -> p e n", e=2)
        act = take(2 * 512).rearrange("p (e n) -> p e n", e=2)
        yr = take(D)
        pick = take(2 * P).rearrange("p (t j) -> p t j", t=2)
        pickg = take(2 * P).rearrange("p (t j) -> p t j", t=2)
        pickgT = take(2 * P)
        gfin = take(D)
        bdn = take(D)[0:EXPERTS, :]
        which = take(P)[0:EXPERTS, :]
        fin = gl.rearrange("p e n -> p (e n)").rearrange("p (t n) -> p t n", t=2)
        assert at[0] <= tail

        ident = kst[:, K_ID:K_ID + P]
        ltri = kst[:, K_LT:K_LT + P]
        ones = kst[:, K_ONE:K_ONE + P]
        fmask = kst[:, K_FM:K_FM + KEYS]
        cmask = kst[:, K_CM:K_CM + KEYS]
        iota = kst[:, K_IOTA:K_IOTA + CAP]
        thr = kst[:, K_THR:K_THR + SEQ // CAP]
        cos = kst[:, K_COS:K_COS + 48].rearrange("p (t n) -> p t n", t=3)
        sin = kst[:, K_SIN:K_SIN + 48].rearrange("p (t n) -> p t n", t=3)

        psum = ctx.enter_context(nc.psum_tensor("psum", [P, 8 * 512], f32))
        bank = [psum[:, n * 512:(n + 1) * 512] for n in range(8)]

        def banks(a, b):
            return psum[:, a * 512:b * 512]

        s_x = [sem(f"x_tile{t}_loaded") for t in range(3)]
        s_vec = sem("feature_vectors_loaded")
        s_vec2 = sem("latent_vectors_loaded")
        s_idn = sem("identity_loaded")
        s_kst = sem("constants_loaded")
        s_bias = sem("biases_loaded")
        s_mixw = sem("small_mixer_weights_loaded")
        s_btf = sem("biases_transposed")
        s_bT = sem("biases_in_sbuf")
        s_late = sem("late_vectors_loaded")
        s_wr = sem("router_loaded")
        s_gfin = sem("final_gain_loaded")
        slot_loaded = [sem(f"slot{n}_loaded") for n in range(ESLOT)]
        slot_used = [sem(f"slot{n}_used") for n in range(ESLOT)]
        last_half = [sem(f"last_chunk_of_expert{e}_loaded") for e in range(2)]
        filled = [sem(f"bank{n}_filled") for n in range(ROT)]
        emptied = [sem(f"bank{n}_emptied") for n in range(ROT)]
        s_clear = sem("pool_cleared")
        s_ss = sem("x_squares_summed")
        s_ms = sem("x_mean_square_ready")
        s_sd = sem("x_deviation_ready")
        s_xs = sem("x_scaled")
        s_mss = sem("mid_squares_summed")
        s_mms = sem("mid_mean_square_ready")
        s_msd = sem("mid_deviation_ready")
        s_fz = sem("forget_logit_ready")
        s_fl = sem("forget_softplus_ready")
        s_logf = sem("log_forget_ready")
        s_cqn = sem("cq_normed")
        s_ckn = sem("ckv_normed")
        s_nf = sem("forget_row_beside_keys")
        s_kk = sem("index_and_rope_keys_ready")
        s_qr = sem("queries_roped")
        s_relu = sem("index_relu_used")
        s_sel = sem("selection_ready")
        s_exp = sem("probabilities_ready")
        s_pv = sem("pair_of_heads_summed_over_values")
        s_pn = sem("probabilities_normalised")
        s_on = sem("attention_tile_in_sbuf")
        s_mg = sem("merged_ready")
        s_hss = sem("h_squares_summed")
        s_hms = sem("h_mean_square_ready")
        s_hsd = sem("h_deviation_ready")
        s_hri = sem("h_scale_ready")
        s_hs = sem("h_scaled")
        s_half = sem("first_half_of_projection_done")
        s_rt = sem("router_products_ready")
        s_rank = sem("ranks_counted")
        s_rkt = sem("rank_table_ready")
        s_dn0 = sem("first_half_of_down_rows_ready")
        s_rmx = sem("router_maximum_ready")
        s_rex = sem("router_exp_ready")
        s_mask = sem("router_mask_ready")
        s_np = sem("pass_count_ready")
        s_bdn = sem("down_biases_loaded")
        s_gl = sem("gate_up_rows_in_sbuf")
        s_tf = sem("gate_up_transposed")
        s_pick0 = sem("first_pick_ready")
        s_pick = sem("gated_pick_ready")
        s_gath = sem("pair_gathered")
        s_xg = sem("gathered_in_sbuf")
        s_pgf = sem("gated_pick_transposed")
        s_pgt = sem("gated_pick_in_sbuf")
        s_glu = sem("glu_clamped")
        s_sig = sem("sigmoid_ready")
        s_act = sem("activation_ready")
        s_y = sem("down_rows_in_sbuf")
        s_sc = sem("rows_scattered")
        s_acc = [sem(f"rows_of_tile{t}_added") for t in range(2)]
        s_fss = sem("final_squares_summed")
        s_fms = sem("final_mean_square_ready")
        s_fsd = sem("final_deviation_ready")
        s_fin = sem("output_rows_ready")
        s_out = sem("output_stored")
        s_dch = sem("vector_step")
        s_ach = sem("scalar_step")
        s_moe = sem("vector_expert_step")

        block = ctx.enter_context(nc.Block())

        def job_bank(name):
            return bank[JOB[name] % ROT]

        def fill_begin(pe, name):
            n = JOB[name]
            if n >= ROT:
                pe.wait_ge(emptied[n % ROT], n // ROT)

        def fill_end(last, name):
            last.then_inc(filled[JOB[name] % ROT], 1)

        def wait_filled(eng, name):
            eng.wait_ge(filled[JOB[name] % ROT], JOB[name] // ROT + 1)

        def empty_end(last, name):
            last.then_inc(emptied[JOB[name] % ROT], 1)

        def wait_emptied(eng, name):
            eng.wait_ge(emptied[JOB[name] % ROT], JOB[name] // ROT + 1)

        def gate_up_done(eng, turn, u, e):
            k = PAIR_LOADS * u + 8 * e + 7
            eng.wait_ge(slot_used[place(k)], turn * USES + (k // ESLOT + 1))

        def down_done(eng, turn, u):
            k = PAIR_LOADS * u + PAIR_LOADS - 1
            eng.wait_ge(slot_used[place(k)], turn * USES + (k // ESLOT + 1))

        def slot(n):
            return ring[:, (n % NSLOT) * SLOT:(n % NSLOT + 1) * SLOT]

        def place(k):
            return (k + NSLOT) % ESLOT

        def eslot(k):
            n = place(k)
            return ring[:, n * SLOT:(n + 1) * SLOT] if n < NSLOT else more[:, (n - NSLOT) * SLOT:(n - NSLOT + 1) * SLOT]

        w_in_v = w_in[0].rearrange("(c p) n -> p c n", p=P)

        def load(sp, n, dst, src):
            if n >= NSLOT:
                wait_filled(sp, LAST_READ[n - NSLOT])
            sp.dma_start(dst, src).then_inc(slot_loaded[n % NSLOT], 16)

        def in_cols(sp, n, col, width):
            load(sp, n, slot(n)[:, 0:CH * width].rearrange("p (c n) -> p c n", c=CH),
                 w_in_v[:, :, col:col + width])

        def in_rows(sp, n, w, row):
            load(sp, n, slot(n).rearrange("p (k n) -> p k n", k=2),
                 w[0, row:row + 2 * P, :].rearrange("(k p) n -> p k n", p=P))

        def vector_rows(eng, dram, row, rows, loaded):
            eng.dma_start(vraw[row:row + rows, :], dram.rearrange("a (c p) -> (a c) p", p=P)).then_inc(loaded, 16)

        @block.sync
        def _(sp):
            sp.dma_start(h1[:, 0:D], x[0, 0:P, :]).then_inc(s_x[0], 16)
            sp.dma_start(kst[:, 0:P], consts[:, 0:P]).then_inc(s_idn, 16)
            in_cols(sp, 0, C_MID, MID // 2)
            sp.dma_start(h1[:, D:2 * D], x[0, P:2 * P, :]).then_inc(s_x[1], 16)
            sp.dma_start(xs[0:META, 2 * D:3 * D], meta).then_inc(s_x[2], 16)
            in_cols(sp, 1, C_MID + MID // 2, MID // 2)
            for k in range(2):
                in_cols(sp, 2 + k, C_KA + 256 * k, 256)
            for k in range(2):
                in_cols(sp, 4 + k, C_QA + 256 * k, 256)
            for k in range(2):
                in_cols(sp, 6 + k, C_VA + 256 * k, 256)
            for k in range(4):
                in_cols(sp, 8 + k, C_GA + 256 * k, 256)
            for k in range(4):
                in_cols(sp, 12 + k, C_GB + 256 * k, 256)
            for k in range(2):
                in_rows(sp, 16 + k, w_a, 256 * k)
            for k in range(2):
                in_rows(sp, 18 + k, w_b, 256 * k)
            for k in range(4):
                in_rows(sp, 20 + k, w_out, 256 * k)

            def expert_load(j, kk):
                u, k = divmod(kk, PAIR_LOADS)
                pair = j * (2 * UNROLL) + 2 * u
                if k < 16:
                    src = w_gu[0, bass.ds(pair + k // 8, 1), (k % 8) * P:(k % 8 + 1) * P, :]
                    sp.dma_start(eslot(kk), src.rearrange("e p n -> p (e n)")).then_inc(slot_loaded[place(kk)], 16)
                elif k < PAIR_LOADS - 2:
                    r = 2 * P * ((k - 16) // 2)
                    src = w_dn[0, bass.ds(pair + k % 2, 1), r:r + 2 * P, :]
                    sp.dma_start(eslot(kk).rearrange("p (k n) -> p k n", k=2),
                                 src.rearrange("e (k p) n -> p (e k) n", p=P)).then_inc(slot_loaded[place(kk)], 16)
                elif k == PAIR_LOADS - 2:
                    for half in range(2):
                        for e in range(2):
                            r = (CH - 2 + half) * P
                            sp.dma_start(eslot(kk + e)[:, half * D:(half + 1) * D],
                                         w_dn[0, bass.ds(pair + e, 1), r:r + P, :].rearrange("e p n -> p (e n)")
                                         ).then_inc(last_half[e] if half else slot_loaded[place(kk + e)], 16)

            def rest_of_turn(turn, j):
                for kk in range(ESLOT, UNROLL * PAIR_LOADS):
                    sp.wait_ge(slot_used[place(kk)], turn * USES + kk // ESLOT)
                    if kk % PAIR_LOADS == PAIR_LOADS - 2:
                        continue
                    if kk % PAIR_LOADS == PAIR_LOADS - 1:
                        kk -= 1
                    expert_load(j, kk)

            def whole_pass(turn0):
                with sp.Fori(0, TURNS - 1) as j:
                    rest_of_turn(turn0 + j, j)
                    for kk in range(ESLOT):
                        sp.wait_ge(slot_used[place(kk)], (turn0 + j) * USES + USES)
                        expert_load(j + 1, kk)
                rest_of_turn(turn0 + (TURNS - 1), TURNS - 1)

            sp.wait_ge(s_pv, len(ITEMS) // 2)
            for kk in range(ESLOT):
                if place(kk) < NSLOT:
                    job = LAST_READ[MIX_LOADS - NSLOT + place(kk)]
                    if job is None:
                        sp.wait_ge(s_half, 1)
                    else:
                        wait_filled(sp, job)
                expert_load(0, kk)
            whole_pass(0)
            sp.wait_ge(s_np, 1)
            n_pass = sp.value_load(npi[0:1, 0:1], min_val=1, max_val=SEQ // CAP)
            with sp.If(n_pass > 1):
                with sp.Fori(1, n_pass) as b:
                    for kk in range(ESLOT):
                        sp.wait_ge(slot_used[place(kk)], b * (TURNS * USES))
                        expert_load(0, kk)
                    whole_pass(b * TURNS)
            for t in range(2):
                for n in range(2):
                    sp.wait_ge(s_fin, 2 * t + n + 1)
                    col = slice(n * 512, (n + 1) * 512)
                    sp.dma_start(out[0, t * P:(t + 1) * P, col], fin[:, t, col]).then_inc(s_out, 16)
            sp.wait_ge(s_out, 64)

        @block.gpsimd
        def _(pool):
            nc.gpsimd.memset(st[:], 1.0).then_inc(s_clear, 1)
            nc.gpsimd.memset(mid[:, 2, :], 0.0).then_inc(s_clear, 1)
            vector_rows(pool, q_norm_g, LATENT, 2, s_vec2)
            vector_rows(pool, kv_norm_g, LATENT + V_KV - V_Q, 1, s_vec2)
            for dst, src in ((bfor, b_forget), (klng, kln_g), (klnb, kln_b), (brt, b_router)):
                pool.dma_start(dst[:], src.broadcast_to([P, dst.shape[1]])).then_inc(s_late, 16)
            pool.dma_start(kst[:, P:KCOLS], consts[:, P:KCOLS]).then_inc(s_kst, 16)
            pool.dma_start(wuk.rearrange("p (k r) -> p k r", k=4),
                           w_uk[0].rearrange("(k a) n r -> (a n) k r", a=2)).then_inc(s_mixw, 16)
            pool.dma_start(wuv.rearrange("p (h v) -> p h v", h=HEADS),
                           w_uv[0].rearrange("h r v -> r h v")).then_inc(s_mixw, 16)
            pool.dma_start(wq[:, :, 0:768], w_uq[0].rearrange("(c p) n -> p c n", p=P)).then_inc(s_mixw, 16)
            pool.dma_start(wq[:, :, 768:1024], w_qidx[0].rearrange("(c p) n -> p c n", p=P)).then_inc(s_mixw, 16)
            pool.dma_start(wr[:].rearrange("p (c e) -> p c e", c=CH),
                           w_router[0].rearrange("(c p) e -> p c e", p=P)).then_inc(s_wr, 16)
            for t in range(2):
                for n in range(2):
                    wait_filled(pool, ("xT", t, n))
            nc.gpsimd.memset(qaT[HD:HD + 1, :, :], 1.0).then_inc(s_clear, 1)
            wait_emptied(pool, "FT")
            for h in range(HEADS):
                pool.dma_start(kaT[HD:HD + 1, h, :], nF[h:h + 1, :]).then_inc(s_nf, 16)

        @block.scalar
        def _(sc):
            vector_rows(sc, norm_mix_g, V_MIX, CH, s_vec)
            vector_rows(sc, norm_ffn_g, V_FFN, CH, s_vec)
            sc.wait_ge(s_clear, 1)
            sc.activation(st[:, 60:61], st[:, 61:62], ACT.Sqrt)
            for t, (rows, _) in enumerate(TILES):
                sc.wait_ge(s_x[t], 16)
                src = h1[:, t * D:(t + 1) * D] if t < 2 else xs[0:META, 2 * D:3 * D]
                sc.activation(qtok[0:rows, 0, :], src, ACT.Square, accum_out=st[0:rows, t:t + 1]).then_inc(s_ss, 1)
                sc.wait_ge(s_ms, t + 1)
                sc.activation(st[:, 3 + t:4 + t], st[:, 3 + t:4 + t], ACT.Sqrt).then_inc(s_sd, 1)

            def copy_out(name, dst, src):
                wait_filled(sc, name)
                empty_end(sc.activation(dst, src, ACT.Copy), name)

            def strips_out(name, dst, width):
                wait_filled(sc, name)
                for j in range(4):
                    ins = sc.activation(dst[0:META, 2, j * width:(j + 1) * width],
                                        job_bank(name)[32 * j:32 * j + META, 0:width], ACT.Copy)
                empty_end(ins, name)

            for t in range(2):
                copy_out(("mid", t), mid[:, t, :], job_bank(("mid", t))[:, 0:MID])
            sc.wait_ge(s_clear, 2)
            strips_out(("mid", 2), mid, MID // 4)
            sc.wait_ge(s_fz, 1)
            z, e = logf[:, 0, :], logf[:, 1, :]
            sc.activation(e, z, ACT.Abs).then_inc(s_ach, 1)
            sc.wait_ge(s_ach, 1)
            sc.activation(e, e, ACT.Exp, scale=-1.0).then_inc(s_ach, 1)
            sc.wait_ge(s_ach, 2)
            sc.activation(e, e, ACT.Ln, bias=1.0).then_inc(s_fl, 1)
            for t in range(3):
                wait_emptied(sc, ("mid", t))
            for t in range(2):
                sc.activation(rel[:, 0, 0:QRANK], mid[:, t, M_CQ:M_CQ + QRANK], ACT.Square,
                              accum_out=st[:, 8 + t:9 + t]).then_inc(s_mss, 1)
                sc.wait_ge(s_mss, t + 1)
            for t in range(3):
                sc.activation(rel[:, 0, 0:KVRANK], mid[:, t, M_CKV:M_CKV + KVRANK], ACT.Square,
                              accum_out=st[:, 10 + t:11 + t]).then_inc(s_mss, 1)
                sc.wait_ge(s_mss, t + 3)
            sc.wait_ge(s_mms, 1)
            sc.activation(st[:, 8:16], st[:, 8:16], ACT.Sqrt).then_inc(s_msd, 1)


            def two_heads_out(name, dst, k, width):
                wait_filled(sc, name)
                sc.activation(dst[0:64, 2 * k, :], job_bank(name)[0:64, 0:width], ACT.Copy)
                empty_end(sc.activation(dst[0:64, 2 * k + 1, :], job_bank(name)[64:128, 0:width], ACT.Copy), name)

            for k in range(4):
                two_heads_out(("ka", k), kaT, k, KEYS)
            for k in range(4):
                two_heads_out(("qa", k), qaT, k, SEQ)
            copy_out("ukT", ukT, job_bank("ukT")[:])
            for t in range(2):
                for n in range(2):
                    copy_out(("q", t, n), qtok[:, t, n * 512:(n + 1) * 512], job_bank(("q", t, n))[:])
            for k in range(4):
                two_heads_out(("kc", k), kcat, k, KEYS)
            copy_out(("va", 0), va[:, 0, :], job_bank(("va", 0)))
            for t in range(2):
                copy_out(("qiT", t), qiT[0:ID, :, t * P:(t + 1) * P],
                         job_bank(("qiT", t))[0:ID, :].rearrange("p (h k) -> p h k", h=IH))
            for n in range(2 * IH):
                t, h = divmod(n, IH)
                name = ("dots", t, h)
                if n >= 3:
                    sc.wait_ge(s_relu, n - 2)
                wait_filled(sc, name)
                ins = sc.activation(rel[:, n % 3, 0:WIDTH[t]], job_bank(name)[:, 0:WIDTH[t]], ACT.Relu,
                                    scale=IH ** -0.5 * ID ** -0.5)
                empty_end(ins, name)
            copy_out(("va", 1), va[:, 1, :], job_bank(("va", 1)))
            strips_out(("va", 2), va, P)
            for t in range(2):
                for n in range(2):
                    copy_out(("qT", t, n), qcat[0:QK, 4 * n:4 * n + 4, t * P:(t + 1) * P],
                             job_bank(("qT", t, n))[0:QK, :].rearrange("p (h k) -> p h k", h=4))
            for t in range(2):
                copy_out(("vb", t), vb[:, t, :], job_bank(("vb", t)))
            strips_out(("vb", 2), vb, P)
            def output_tile(n):
                sc.wait_ge(s_pv, 4 * n + 4)
                dst = (oaT if n < 2 else obT)[:, :, (n % 2) * P:(n % 2 + 1) * P]
                sc.activation(dst, bank[6 + n % 2].rearrange("p (c k) -> p c k", c=4), ACT.Copy).then_inc(s_on, 1)

            for i, (b, t, h) in enumerate(ITEMS):
                w = WIDTH[t]
                wait_emptied(sc, ("S", i))
                if i >= 3:
                    wait_filled(sc, ("PT", i - 3))
                sc.activation(pr[:, i % 3, 0:w], sm[:, i % 3, 0:w], ACT.Exp, scale=-1.0,
                              bias=st[:, 16 + i % 3:17 + i % 3],
                              accum_out=rk[:, i:i + 1]).then_inc(s_exp, 1)
                if i % 2 == 1:
                    name = ("gate", i // 2)
                    dst = (gaS if i < 16 else gbS)[:, i // 2 % CH, :]
                    wait_filled(sc, name)
                    empty_end(sc.activation(dst, job_bank(name)[:, 0:SEQ], ACT.Sigmoid), name)
                if i % 8 == 3 and i > 8:
                    output_tile(i // 8 - 1)
            output_tile(3)
            sc.dma_start(braw, b_gu[0]).then_inc(s_bias, 16)
            sc.activation(st[:, 60:61], st[:, 61:62], ACT.Sqrt)
            for t in range(2):
                for n in range(2):
                    wait_emptied(sc, ("out", t, n))
                sc.activation(sg.rearrange("p e n -> p (e n)"), h1[:, t * D:(t + 1) * D], ACT.Square,
                              accum_out=st[:, 20 + t:21 + t]).then_inc(s_hss, 1)
                sc.wait_ge(s_hms, t + 1)
                sc.activation(st[:, 22 + t:23 + t], st[:, 22 + t:23 + t], ACT.Sqrt).then_inc(s_hsd, 1)
                sc.wait_ge(s_hri, t + 1)
                sc.activation(hs[:, t, :], h1[:, t * D:(t + 1) * D], ACT.Copy,
                              scale=st[:, 22 + t:23 + t]).then_inc(s_hs, 1)
            sc.dma_start(bdn, b_dn[0]).then_inc(s_bdn, 16)
            sc.dma_start(gfin, norm_final_g.rearrange("(a n) -> a n", a=1).broadcast_to([P, D])).then_inc(s_gfin, 16)
            for t in range(2):
                sc.wait_ge(s_rmx, t + 1)
                sc.activation(rk[:, 64 + 32 * t:96 + 32 * t], rk[:, 32 * t:32 * t + 32], ACT.Exp,
                              bias=st[:, 24 + t:25 + t]).then_inc(s_rex, 1)

            sc.wait_ge(s_btf, 1)
            sc.activation(biasT[:], job_bank(("out", 1, 0)), ACT.Copy).then_inc(s_bT, 1)
            sc.wait_ge(s_np, 1)
            n_pass = sc.value_load(npi[0:1, 0:1], min_val=1, max_val=SEQ // CAP)
            with sc.Fori(0, n_pass) as b:
                with sc.Fori(0, TURNS) as j:
                    turn = sc.snap(b * TURNS + j)
                    for u in range(UNROLL):
                        g = turn * UNROLL + u
                        sc.wait_ge(s_pgf, g + 1)
                        sc.activation(pickgT, bank[0][:, 0:2 * P], ACT.Copy).then_inc(s_pgt, 1)
                        for e in range(2):
                            gate_up_done(sc, turn, u, e)
                            sc.activation(gl[:, e, :], banks(2 + 2 * e, 4 + 2 * e), ACT.Copy).then_inc(s_gl, 1)
                            sc.wait_ge(s_glu, g * 2 + (e + 1))
                            sc.activation(sg[:, e, :], glu[:, e, :], ACT.Sigmoid, scale=1.702).then_inc(s_sig, 1)
                        sc.wait_ge(s_dn0, g + 1)
                        sc.activation(yr[:, 0:512], bank[2], ACT.Copy).then_inc(s_y, 1)
                        down_done(sc, turn, u)
                        sc.activation(yr[:, 512:D], bank[3], ACT.Copy).then_inc(s_y, 1)
            sc.activation(st[:, 60:61], st[:, 61:62], ACT.Sqrt)
            for t in range(2):
                sc.wait_ge(s_acc[t], n_pass * PAIRS)
                sc.activation(hs[:, t, :], h1[:, t * D:(t + 1) * D], ACT.Square,
                              accum_out=st[:, 28 + t:29 + t]).then_inc(s_fss, 1)
            sc.wait_ge(s_fms, 1)
            sc.activation(st[:, 30:32], st[:, 30:32], ACT.Sqrt).then_inc(s_fsd, 1)

        @block.vector
        def _(dve):
            v = nc.vector
            chain = [0]

            def link(ins):
                chain[0] += 1
                ins.then_inc(s_dch, 1)
                dve.wait_ge(s_dch, chain[0])

            def scaled(dst, src, vec, cols):
                return v.tensor_tensor(dst, src, vec.unsqueeze(2).broadcast_to([P] + cols), ALU.mult)

            def rope4(dst1, dst2, x1, x2, c, s, tmp):
                a, b_, c_, d_ = tmp
                v.tensor_tensor(a, x1, c, ALU.mult)
                v.tensor_tensor(b_, x2, s, ALU.mult)
                v.tensor_tensor(c_, x1, s, ALU.mult)
                link(v.tensor_tensor(d_, x2, c, ALU.mult))
                v.tensor_tensor(dst1, a, b_, ALU.subtract)
                return v.tensor_tensor(dst2, c_, d_, ALU.add)

            def input_scale(t):
                rows = TILES[t][0]
                dve.wait_ge(s_ss, t + 1)
                v.tensor_scalar(st[:, 3 + t:4 + t], st[:, t:t + 1], 1.0 / D, EPS, ALU.mult, ALU.add).then_inc(s_ms, 1)
                dve.wait_ge(s_sd, t + 1)
                link(v.reciprocal(st[:, 3 + t:4 + t], st[:, 3 + t:4 + t]))
                src = h1[:, t * D:(t + 1) * D] if t < 2 else xs[0:META, 2 * D:3 * D]
                v.tensor_scalar(xs[0:rows, t * D:(t + 1) * D], src, st[0:rows, 3 + t:4 + t], None,
                                ALU.mult).then_inc(s_xs, 1)

            def input_features(t):
                rows, col = TILES[t]
                for n in range(2 if t < 2 else 1):
                    name = ("xT", t, n)
                    wait_filled(dve, name)
                    cs = 4 if t < 2 else CH
                    src = job_bank(name)[:, 0:cs * rows].rearrange("p (c k) -> p c k", c=cs)
                    empty_end(scaled(xnT[:, 4 * n:4 * n + cs, col:col + rows], src,
                                     vT[:, V_MIX + 4 * n:V_MIX + 4 * n + cs], [cs, rows]), name)

            dve.wait_ge(s_clear, 1)
            input_scale(0)
            wait_filled(dve, "vec")
            empty_end(v.tensor_copy(vT[:, 0:V_Q], job_bank("vec")[:, 0:V_Q]), "vec")
            wait_emptied(dve, "vec")
            input_features(0)
            for t in (1, 2):
                input_scale(t)
                input_features(t)
            dve.wait_ge(s_late, 64)
            for t in range(3):
                wait_emptied(dve, ("mid", t))
            z = logf[:, 0, :].rearrange("p (t h) -> p t h", t=3)
            v.tensor_tensor(z, mid[:, :, M_F:M_F + HEADS], bfor[:].unsqueeze(1).broadcast_to([P, 3, HEADS]),
                            ALU.add).then_inc(s_fz, 1)
            wait_filled(dve, "vec2")
            empty_end(v.tensor_copy(vT[:, V_Q:V_ROWS], job_bank("vec2")[:, 0:V_ROWS - V_Q]), "vec2")
            wait_emptied(dve, "vec2")
            ki = mid[:, :, M_KI:M_KI + ID]
            kc = kk[:, :, 0:ID]
            link(v.tensor_reduce(st[:, 32:35], ki, AX.X, ALU.add))
            link(v.tensor_scalar(st[:, 32:35], st[:, 32:35], 1.0 / ID, None, ALU.mult))
            link(v.tensor_tensor(kc, ki, st[:, 32:35].unsqueeze(2).broadcast_to([P, 3, ID]), ALU.subtract))
            sqv = sq[:, 0:3 * ID].rearrange("p (t n) -> p t n", t=3)
            link(v.tensor_tensor(sqv, kc, kc, ALU.mult))
            link(v.tensor_reduce(st[:, 13:16], sqv, AX.X, ALU.add))
            dve.wait_ge(s_mss, 5)
            v.tensor_scalar(st[:, 8:10], st[:, 8:10], 1.0 / QRANK, EPS, ALU.mult, ALU.add)
            v.tensor_scalar(st[:, 10:13], st[:, 10:13], 1.0 / KVRANK, EPS, ALU.mult, ALU.add)
            v.tensor_scalar(st[:, 13:16], st[:, 13:16], 1.0 / ID, EPS, ALU.mult, ALU.add).then_inc(s_mms, 1)
            dve.wait_ge(s_fl, 1)
            v.scalar_tensor_tensor(logf[:, 2, :], logf[:, 0, :], 0.0, logf[:, 1, :], ALU.min,
                                   ALU.subtract).then_inc(s_logf, 1)
            dve.wait_ge(s_msd, 1)
            link(v.reciprocal(st[:, 8:16], st[:, 8:16]))
            for t in range(2):
                ins = v.tensor_scalar(mid[:, t, M_CQ:M_CQ + QRANK], mid[:, t, M_CQ:M_CQ + QRANK],
                                      st[:, 8 + t:9 + t], None, ALU.mult)
            ins.then_inc(s_cqn, 1)
            for t in range(3):
                ins = v.tensor_scalar(mid[:, t, M_CKV:M_CKV + KVRANK], mid[:, t, M_CKV:M_CKV + KVRANK],
                                      st[:, 10 + t:11 + t], None, ALU.mult)
            ins.then_inc(s_ckn, 1)
            link(v.tensor_tensor(kc, kc, st[:, 13:16].unsqueeze(2).broadcast_to([P, 3, ID]), ALU.mult))
            link(v.tensor_tensor(kc, kc, klng[:].unsqueeze(1).broadcast_to([P, 3, ID]), ALU.mult))
            link(v.tensor_tensor(kc, kc, klnb[:].unsqueeze(1).broadcast_to([P, 3, ID]), ALU.add))
            link(v.tensor_copy(kk[:, :, ID:ID + ROPE], mid[:, :, M_KR:M_KR + ROPE]))
            dve.wait_ge(s_kst, 16)
            tmp3 = [rt[:, 48 * n:48 * n + 48].rearrange("p (t n) -> p t n", t=3) for n in range(8)]
            for n, o in enumerate((0, ID)):
                last = rope4(kk[:, :, o:o + 16], kk[:, :, o + 16:o + 32], kk[:, :, o:o + 16],
                             kk[:, :, o + 16:o + 32], cos, sin, tmp3[4 * n:4 * n + 4])
            last.then_inc(s_kk, 1)
            wait_filled(dve, ("cqT", 0))
            empty_end(scaled(cqT, job_bank(("cqT", 0))[:].rearrange("p (c k) -> p c k", c=2),
                             vT[:, V_Q:V_Q + 2], [2, SEQ]), ("cqT", 0))
            wait_filled(dve, ("ckvT", 0))
            empty_end(v.tensor_scalar(ckvT, job_bank(("ckvT", 0))[:, 0:KEYS], vT[:, V_KV:V_KV + 1], None,
                                      ALU.mult), ("ckvT", 0))
            wait_filled(dve, ("kkT", 0))
            v.tensor_copy(kiT[0:ID, :], job_bank(("kkT", 0))[0:ID, 0:KEYS])
            empty_end(v.tensor_copy(kcat[NOPE:QK, :, :],
                                    job_bank(("kkT", 0))[ID:ID + ROPE, 0:KEYS].unsqueeze(1)
                                    .broadcast_to([ROPE, HEADS, KEYS])), ("kkT", 0))
            wait_filled(dve, "FT")
            empty_end(v.tensor_scalar(nF[0:HEADS, :], job_bank("FT")[0:HEADS, 0:KEYS], -(HD ** 0.5), None,
                                      ALU.mult), "FT")
            for t in range(2):
                for n in range(2):
                    wait_emptied(dve, ("q", t, n))
                for n, (o, heads, per, off) in enumerate(((768, IH, ID, 0), (0, HEADS, QK, NOPE))):
                    grp = qtok[:, t, o:o + heads * per].rearrange("p (h n) -> p h n", h=heads)
                    x1, x2 = grp[:, :, off:off + 16], grp[:, :, off + 16:off + 32]
                    cs_ = cos[:, t, :].unsqueeze(1).broadcast_to([P, heads, 16])
                    sn_ = sin[:, t, :].unsqueeze(1).broadcast_to([P, heads, 16])
                    tmp = [rt[:, 512 * n + 128 * m:512 * n + 128 * m + 16 * heads]
                           .rearrange("p (h n) -> p h n", h=heads) for m in range(4)]
                    ins = rope4(x1, x2, x1, x2, cs_, sn_, tmp)
                    ins.then_inc(s_qr, 1)
                    dve.wait_ge(s_qr, 2 * t + n + 1)
            for n in range(2 * IH):
                t, h = divmod(n, IH)
                w = WIDTH[t]
                wait_emptied(dve, ("dots", t, h))
                base = cmask[:, KEYS - w:KEYS] if h == 0 else isc[:, t, 0:w]
                ins = v.scalar_tensor_tensor(isc[:, t, 0:w], rel[:, n % 3, 0:w],
                                             mid[:, t, M_IW + h:M_IW + h + 1], base, ALU.mult, ALU.add)
                ins.then_inc(s_relu, 1)
                dve.wait_ge(s_relu, n + 1)
            for t in range(2):
                w = WIDTH[t]
                for r in range(TOPK_SEL // 8):
                    src = isc[:, t, 0:w] if r == 0 else wrk[:, t, 0:w]
                    link(v.max(top8[:, 8 * t:8 * t + 8], src))
                    link(v.match_replace(wrk[:, t, 0:w], top8[:, 8 * t:8 * t + 8], src, TAKEN))
                v.tensor_scalar(selb[:, t, 0:w], wrk[:, t, 0:w], TAKEN / 2, NEG, ALU.is_gt,
                                ALU.mult).then_inc(s_sel, 1)
            dve.wait_ge(s_sel, 2)
            for i in range(len(ITEMS) + 2):
                if i < len(ITEMS):
                    b, t, h = ITEMS[i]
                    w = WIDTH[t]
                    mask = selb[:, t, 0:w] if b else fmask[:, KEYS - w:KEYS]
                    scale = (QK if b else HD) ** -0.5
                    if i >= 3:
                        dve.wait_ge(s_exp, i - 2)
                    wait_filled(dve, ("S", i))
                    ins = v.tensor_tensor_reduce(out=sm[:, i % 3, 0:w], in0=job_bank(("S", i))[:, 0:w],
                                                 in1=mask, scale=-scale, scalar=3e38, op0=ALU.add,
                                                 op1=ALU.min, accum_out=st[:, 16 + i % 3:17 + i % 3])
                    empty_end(ins, ("S", i))
                if 1 <= i <= len(ITEMS):
                    k = i - 1
                    w = WIDTH[ITEMS[k][1]]
                    dve.wait_ge(s_exp, k + 1)
                    link(v.reciprocal(rk[:, 32 + k:33 + k], rk[:, k:k + 1]))
                    v.tensor_scalar(pr[:, k % 3, 0:w], pr[:, k % 3, 0:w], rk[:, 32 + k:33 + k], None,
                                    ALU.mult).then_inc(s_pn, 1)
                if i >= 2:
                    k = i - 2
                    t = ITEMS[k][1]
                    if k >= 4:
                        dve.wait_ge(s_pv, (k - 4) // 2 + 1)
                    wait_filled(dve, ("PT", k))
                    src = job_bank(("PT", k))
                    v.tensor_copy(pT[0:META, k % 4, 2, :], src[0:META, 256:384])
                    empty_end(v.tensor_copy(pT[:, k % 4, 0:t + 1, :],
                                            src[:, 0:(t + 1) * P].rearrange("p (t k) -> p t k", t=t + 1)),
                              ("PT", k))
            for m in range(4):
                name = ("ba", m)
                wait_filled(dve, name)
                for k in range(2):
                    wait_emptied(dve, ("gate", 2 * m + k))
                dst = gaS[:, 2 * m:2 * m + 2, :].rearrange("p c k -> p (c k)")
                empty_end(v.tensor_tensor(dst, dst, job_bank(name)[:], ALU.mult), name)
            for m in range(4):
                name = ("bb", m)
                wait_filled(dve, name)
                for k in range(2):
                    wait_emptied(dve, ("gate", CH + 2 * m + k))
                a = gaS[:, 2 * m:2 * m + 2, :].rearrange("p c k -> p (c k)")
                b_ = gbS[:, 2 * m:2 * m + 2, :].rearrange("p c k -> p (c k)")
                ins = v.tensor_tensor(b_, b_, job_bank(name)[:], ALU.mult)
                empty_end(ins, name)
                wait_emptied(dve, name)
                v.tensor_tensor(a, a, b_, ALU.add).then_inc(s_mg, 1)
            rk3 = rank[:].rearrange("p (t e) -> p t e", t=2)
            gt3 = gates[:].rearrange("p (t e) -> p t e", t=2)

            def pick_tile(t, col):
                return v.tensor_tensor(pick[:, t, :].rearrange("p (e j) -> p e j", e=2),
                                       iota.unsqueeze(1).broadcast_to([P, 2, CAP]),
                                       rk3[:, t, col].unsqueeze(2).broadcast_to([P, 2, CAP]), ALU.is_equal)

            def pick_pair(col):
                pick_tile(0, col)
                return pick_tile(1, col)

            def gate_pair(col):
                for t in range(2):
                    ins = v.tensor_tensor(pickg[:, t, :].rearrange("p (e j) -> p e j", e=2),
                                          pick[:, t, :].rearrange("p (e j) -> p e j", e=2),
                                          gt3[:, t, col].unsqueeze(2).broadcast_to([P, 2, CAP]), ALU.mult)
                return ins

            def gathered(n):
                for k in range(2):
                    dve.wait_ge(s_gath, n * 2 + (k + 1))
                    scaled(xg[:, 4 * k:4 * k + 4, :], bank[k].rearrange("p (c j) -> p c j", c=4),
                           vT[:, V_FFN + 4 * k:V_FFN + 4 * k + 4], [4, P]).then_inc(s_xg, 1)

            def add_rows(n):
                for t in range(2):
                    dve.wait_ge(s_sc, n * 2 + (t + 1))
                    half = h1[:, t * D:(t + 1) * D]
                    v.tensor_tensor(half, half, banks(4 + 2 * t, 6 + 2 * t), ALU.add).then_inc(s_acc[t], 1)

            lg = rk[:, 0:64].rearrange("p (t e) -> p t e", t=2)
            ex = rk[:, 64:128]
            wk = rk[:, 128:192]
            msk = rk[:, 192:256]

            def add_projected(t, n):
                name = ("out", t, n)
                wait_filled(dve, name)
                dst = h1[:, t * D + 512 * n:t * D + 512 * (n + 1)]
                empty_end(v.tensor_tensor(dst, dst, job_bank(name), ALU.add), name)

            def features_out(t, n):
                name = ("hT", t, n)
                wait_filled(dve, name)
                src = job_bank(name).rearrange("p (c k) -> p c k", c=4)
                empty_end(scaled(hT[:, 4 * n:4 * n + 4, t * P:(t + 1) * P], src,
                                 vT[:, V_FFN + 4 * n:V_FFN + 4 * n + 4], [4, P]), name)

            def row_scale(t):
                dve.wait_ge(s_hss, t + 1)
                v.tensor_scalar(st[:, 22 + t:23 + t], st[:, 20 + t:21 + t], 1.0 / D, EPS, ALU.mult,
                                ALU.add).then_inc(s_hms, 1)
                dve.wait_ge(s_hsd, t + 1)
                v.reciprocal(st[:, 22 + t:23 + t], st[:, 22 + t:23 + t]).then_inc(s_hri, 1)
                dve.wait_ge(s_hri, t + 1)

            def choose(t):
                dve.wait_ge(s_rt, t + 1)
                link(v.scalar_tensor_tensor(lg[:, t, :], bank[7 - t][:, 0:EXPERTS], st[:, 22 + t:23 + t],
                                            brt[:], ALU.mult, ALU.add))
                m8 = top8[:, 8 * t:8 * t + 8]
                link(v.max(m8, lg[:, t, :]))
                v.tensor_scalar(st[:, 24 + t:25 + t], m8[:, 0:1], -1.0, None, ALU.mult).then_inc(s_rmx, 1)
                link(v.memset(m8[:, 4:8], 3e38))
                link(v.match_replace(wk[:, 32 * t:32 * t + 32], m8, lg[:, t, :], TAKEN))
                v.tensor_scalar(msk[:, 32 * t:32 * t + 32], wk[:, 32 * t:32 * t + 32], TAKEN / 2, None,
                                ALU.is_lt).then_inc(s_mask, 1)
                dve.wait_ge(s_mask, t + 1)

            def rank_tile(t):
                dve.wait_ge(s_rank, t + 1)
                v.scalar_tensor_tensor(rk3[:, t, 0:EXPERTS], bank[7][:, 64 + 32 * t:96 + 32 * t], RANK0,
                                       msk[:, 32 * t:32 * t + 32], ALU.add, ALU.mult).then_inc(s_rkt, 1)
                dve.wait_ge(s_rkt, t + 1)
                pick_tile(t, slice(0, 2)).then_inc(s_pick0, 1)

            add_projected(0, 0)
            add_projected(0, 1)
            features_out(0, 0)
            add_projected(1, 0)
            features_out(0, 1)
            row_scale(0)
            features_out(1, 0)
            choose(0)
            add_projected(1, 1)
            rank_tile(0)
            features_out(1, 1)
            row_scale(1)
            choose(1)
            rank_tile(1)
            link(v.tensor_reduce(st[:, 48:49], bank[7][:, 128:160], AX.X, ALU.max))
            link(v.tensor_tensor(st[:, 52:56], thr, st[:, 48:49].broadcast_to([P, SEQ // CAP]), ALU.is_lt))
            link(v.tensor_reduce(st[:, 49:50], st[:, 52:56], AX.X, ALU.add))
            v.tensor_copy(npi[:], st[:, 49:50]).then_inc(s_np, 1)
            gathered(0)
            dve.wait_ge(s_rex, 2)
            link(v.tensor_tensor(ex, ex, msk, ALU.mult))
            link(v.tensor_reduce(st[:, 26:28], ex.rearrange("p (t e) -> p t e", t=2), AX.X, ALU.add))
            link(v.reciprocal(st[:, 26:28], st[:, 26:28]))
            link(v.tensor_tensor(gt3[:, :, 0:EXPERTS], ex.rearrange("p (t e) -> p t e", t=2),
                                 st[:, 26:28].unsqueeze(2).broadcast_to([P, 2, EXPERTS]), ALU.mult))
            dve.wait_ge(s_pick0, 2)
            gate_pair(slice(0, 2)).then_inc(s_pick, 1)
            link(v.tensor_copy(gt3[:, :, EXPERTS:RCOLS], gt3[:, :, 0:2]))
            link(v.tensor_scalar(rk3[:, :, EXPERTS:RCOLS], rk3[:, :, 0:2], -float(CAP), None, ALU.add))
            dve.wait_ge(s_np, 1)
            n_pass = dve.value_load(npi[0:1, 0:1], min_val=1, max_val=SEQ // CAP)
            dve.wait_ge(s_bT, 1)
            bias = biasT[:].rearrange("p (m e) -> p m e", e=EXPERTS)

            STEPS = 9
            with dve.Fori(0, n_pass) as b:
                with dve.Fori(0, TURNS) as j:
                    turn = dve.snap(b * TURNS + j)
                    first = dve.snap(turn * (UNROLL * STEPS) + b)
                    step = [0]

                    def mlink(ins):
                        step[0] += 1
                        ins.then_inc(s_moe, 1)
                        dve.wait_ge(s_moe, first + step[0])

                    for u in range(UNROLL):
                        g = turn * UNROLL + u
                        pair = j * (2 * UNROLL) + 2 * u
                        dve.wait_ge(s_pgf, g + 1)
                        v.tensor_copy(which.rearrange("p (e j) -> p e j", e=2),
                                      ident[0:EXPERTS, bass.ds(pair, 2)].unsqueeze(2)
                                      .broadcast_to([EXPERTS, 2, CAP]))
                        mlink(pick_pair(bass.ds(pair + 2, 2)))
                        gate_pair(bass.ds(pair + 2, 2)).then_inc(s_pick, 1)
                        for e in range(2):
                            rows = banks(6, 8).rearrange("p (m j) -> p m j", m=8)

                            def with_bias(dst, src, m):
                                return v.tensor_tensor(
                                    dst.rearrange("p (m j) -> p m j", m=8), src,
                                    bias[:, m:m + 8, bass.ds(pair + e, 1)].broadcast_to([P, 8, CAP]), ALU.add)
                            dve.wait_ge(s_tf, g * 2 + (e + 1))
                            mlink(with_bias(glu[:, e, :], rows[:, :, 0:CAP], 0))
                            v.tensor_scalar(glu[:, e, :], glu[:, e, :], 7.0, None, ALU.min).then_inc(s_glu, 1)
                            mlink(with_bias(lin[:, e, :], rows[:, :, CAP:2 * CAP], 8))
                            mlink(v.tensor_scalar(lin[:, e, :], lin[:, e, :], 7.0, -7.0, ALU.min, ALU.max))
                            dve.wait_ge(s_sig, g * 2 + (e + 1))
                            mlink(v.scalar_tensor_tensor(lin[:, e, :], lin[:, e, :], 1.0, glu[:, e, :],
                                                         ALU.add, ALU.mult))
                            v.tensor_tensor(act[:, e, :], lin[:, e, :], sg[:, e, :], ALU.mult).then_inc(s_act, 1)
                        gathered(g + 1)
                        add_rows(g)
                        for t in range(2):
                            dve.wait_ge(s_acc[t], g + 1)
                    assert step[0] == UNROLL * STEPS
                v.tensor_scalar(rank[:], rank[:], -float(CAP), None, ALU.add).then_inc(s_moe, 1)
                dve.wait_ge(s_moe, (b * TURNS + TURNS) * (UNROLL * STEPS) + (b + 1))

            dve.wait_ge(s_gfin, 16)
            dve.wait_ge(s_fss, 2)
            v.tensor_scalar(st[:, 30:32], st[:, 28:30], 1.0 / D, EPS, ALU.mult, ALU.add).then_inc(s_fms, 1)
            dve.wait_ge(s_fsd, 1)
            link(v.reciprocal(st[:, 30:32], st[:, 30:32]))
            for t in range(2):
                for n in range(2):
                    col = slice(n * 512, (n + 1) * 512)
                    v.scalar_tensor_tensor(fin[:, t, col], h1[:, t * D + n * 512:t * D + (n + 1) * 512],
                                           st[:, 30 + t:31 + t], gfin[:, col], ALU.mult,
                                           ALU.mult).then_inc(s_fin, 1)

        @block.tensor
        def _(pe):
            mm = nc.tensor.matmul
            tr = nc.tensor.transpose
            def loaded(n):
                pe.wait_ge(slot_loaded[n % NSLOT], 16 * (n // NSLOT + 1))

            def used(last, n):
                last.then_inc(slot_used[place(n)], 1)

            def win(n, width=256):
                return slot(n)[:, 0:CH * width].rearrange("p (c n) -> p c n", c=CH)

            pe.wait_ge(s_clear, 2)
            for _ in range(WARM_UP):
                mm(bank[7][:, 0:MID], mid[:, 2, 0:P], mid[:, 2, :], start=True, stop=True)
            pe.wait_ge(s_idn, 16)
            pe.wait_ge(s_vec, 32)
            fill_end(tr(job_bank("vec")[:, 0:V_Q], vraw[0:V_Q, :], ident[0:V_Q, 0:V_Q]), "vec")

            def input_rows(t):
                rows = TILES[t][0]
                pe.wait_ge(s_xs, t + 1)
                for n in range(2 if t < 2 else 1):
                    name = ("xT", t, n)
                    fill_begin(pe, name)
                    for c in range(4 if t < 2 else CH):
                        ins = tr(job_bank(name)[:, c * rows:(c + 1) * rows],
                                 xs[0:rows, t * D + (4 * n + c) * P:t * D + (4 * n + c + 1) * P],
                                 ident[0:rows, 0:rows])
                    fill_end(ins, name)

            half = MID // 2

            def mid_block(t, s):
                rows, col = TILES[t]
                name = ("mid", t)
                if s == 0:
                    for n in range(2):
                        wait_emptied(pe, ("xT", t, n))
                    fill_begin(pe, name)
                loaded(s)
                for c in range(CH):
                    ins = mm(job_bank(name)[:, s * half:(s + 1) * half], xnT[:, c, col:col + rows],
                             win(s, half)[:, c, :], start=c == 0, stop=c == CH - 1)
                if s == 1:
                    fill_end(ins, name)

            input_rows(0)
            mid_block(0, 0)
            input_rows(1)
            mid_block(0, 1)
            mid_block(1, 0)
            input_rows(2)
            mid_block(1, 1)

            def meta_strips(name, width, weight):
                fill_begin(pe, name)
                chunks = CH if weight(0, 1) is not None else 1
                for c in range(chunks):
                    for j in range(4):
                        lhs = xnT[:, c, 0:META] if chunks > 1 else ckvT[:, 0:META]
                        ins = mm(job_bank(name)[32 * j:32 * j + META, 0:width], lhs, weight(j, c),
                                 start=c == 0, stop=c == chunks - 1)
                fill_end(ins, name)

            q = MID // 4
            wait_emptied(pe, ("xT", 2, 0))
            meta_strips(("mid", 2), q, lambda j, c: win(j // 2, half)[:, c, (j % 2) * q:(j % 2 + 1) * q])

            n = V_ROWS - V_Q
            pe.wait_ge(s_vec2, 32)
            fill_begin(pe, "vec2")
            fill_end(tr(job_bank("vec2")[:, 0:n], vraw[LATENT:LATENT + n, :],
                        ident[LATENT:LATENT + n, LATENT:LATENT + n]), "vec2")

            def feature_major(name, s, k, cols, width):
                fill_begin(pe, name)
                loaded(s)
                for c in range(CH):
                    ins = mm(job_bank(name)[:, 0:width], win(s)[:, c, k * P:(k + 1) * P],
                             xnT[:, c, cols:cols + width], start=c == 0, stop=c == CH - 1)
                fill_end(ins, name)

            for k in range(4):
                feature_major(("ka", k), 2 + k // 2, k % 2, 0, KEYS)
            name = ("cqT", 0)
            fill_begin(pe, name)
            pe.wait_ge(s_cqn, 1)
            for c in range(2):
                for t in range(2):
                    ins = tr(job_bank(name)[:, c * SEQ + t * P:c * SEQ + (t + 1) * P],
                             mid[:, t, M_CQ + c * P:M_CQ + (c + 1) * P], ident)
            fill_end(ins, name)
            name = ("ckvT", 0)
            fill_begin(pe, name)
            pe.wait_ge(s_ckn, 1)
            for t, (rows, col) in enumerate(TILES):
                ins = tr(job_bank(name)[:, col:col + rows], mid[0:rows, t, M_CKV:M_CKV + KVRANK],
                         ident[0:rows, 0:rows])
            fill_end(ins, name)
            for k in range(4):
                feature_major(("qa", k), 4 + k // 2, k % 2, META, SEQ)
            pe.wait_ge(s_kst, 16)
            pe.wait_ge(s_mixw, 64)
            fill_begin(pe, "ukT")
            for k in range(4):
                ins = tr(job_bank("ukT")[:, k * P:(k + 1) * P], wuk[:, k * P:(k + 1) * P], ident)
            fill_end(ins, "ukT")
            name = ("kkT", 0)
            fill_begin(pe, name)
            pe.wait_ge(s_kk, 1)
            for t, (rows, col) in enumerate(TILES):
                ins = tr(job_bank(name)[0:QK, col:col + rows], kk[0:rows, t, :], ident[0:rows, 0:rows])
            fill_end(ins, name)
            fill_begin(pe, "FT")
            pe.wait_ge(s_logf, 1)
            lf = logf[:, 2, :].rearrange("p (t h) -> p t h", t=3)
            FT = job_bank("FT")
            for t, (rows, col) in ((2, TILES[2]), (0, TILES[0]), (1, TILES[1])):
                terms = [(lf[0:rows, t, :], ltri[0:rows, 0:rows]), (lf[0:rows, t, :], ident[0:rows, 0:rows])]
                if t < 2:
                    terms.append((lf[0:META, 2, :], ones[0:META, 0:rows]))
                if t == 1:
                    terms.append((lf[:, 0, :], ones[:, 0:rows]))
                for n, (a, b_) in enumerate(terms):
                    ins = mm(FT[0:HEADS, col:col + rows], a, b_, start=n == 0, stop=n == len(terms) - 1)
            fill_end(ins, "FT")
            wait_emptied(pe, ("cqT", 0))
            for t in range(2):
                for n in range(2):
                    name = ("q", t, n)
                    fill_begin(pe, name)
                    for c in range(2):
                        ins = mm(job_bank(name)[:], cqT[:, c, t * P:(t + 1) * P],
                                 wq[:, c, n * 512:(n + 1) * 512], start=c == 0, stop=c == 1)
                    fill_end(ins, name)
            wait_emptied(pe, ("ckvT", 0))
            wait_emptied(pe, "ukT")
            for k in range(4):
                name = ("kc", k)
                fill_begin(pe, name)
                fill_end(mm(job_bank(name)[:, 0:KEYS], ukT[:, k * P:(k + 1) * P], ckvT, start=True,
                            stop=True), name)

            def fox_values(t):
                name = ("va", t)
                rows, col = TILES[t]
                fill_begin(pe, name)
                for s in range(2):
                    loaded(6 + s)
                    for c in range(CH):
                        ins = mm(job_bank(name)[:, s * 256:(s + 1) * 256], xnT[:, c, col:col + rows],
                                 win(6 + s)[:, c, :], start=c == 0, stop=c == CH - 1)
                fill_end(ins, name)

            fox_values(0)
            pe.wait_ge(s_qr, 4)
            for t in range(2):
                name = ("qiT", t)
                fill_begin(pe, name)
                for h in range(IH):
                    ins = tr(job_bank(name)[0:ID, h * P:(h + 1) * P],
                             qtok[:, t, 768 + h * ID:768 + (h + 1) * ID], ident)
                fill_end(ins, name)
            wait_emptied(pe, ("kkT", 0))
            for t in range(2):
                wait_emptied(pe, ("qiT", t))
                for h in range(IH):
                    name = ("dots", t, h)
                    fill_begin(pe, name)
                    fill_end(mm(job_bank(name)[:, 0:WIDTH[t]], qiT[0:ID, h, t * P:(t + 1) * P],
                                kiT[0:ID, 0:WIDTH[t]], start=True, stop=True), name)
            fox_values(1)
            meta_strips(("va", 2), P, lambda j, c: win(6 + j // 2)[:, c, (j % 2) * P:(j % 2 + 1) * P])
            for t in range(2):
                for n in range(2):
                    name = ("qT", t, n)
                    fill_begin(pe, name)
                    for h in range(4):
                        ins = tr(job_bank(name)[0:QK, h * P:(h + 1) * P],
                                 qtok[:, t, (4 * n + h) * QK:(4 * n + h + 1) * QK], ident)
                    fill_end(ins, name)
            for t, (rows, col) in enumerate(TILES[0:2]):
                name = ("vb", t)
                fill_begin(pe, name)
                fill_end(mm(job_bank(name), ckvT[:, col:col + rows], wuv, start=True, stop=True), name)
            meta_strips(("vb", 2), P, lambda j, c: wuv[:, j * P:(j + 1) * P] if c == 0 else None)
            pe.wait_ge(s_nf, 16 * HEADS)
            pe.wait_ge(s_clear, 3)
            for name in [("ka", 3), ("qa", 3)] + [("kc", k) for k in range(4)] \
                    + [("va", t) for t in range(3)]:
                wait_emptied(pe, name)

            def scores(i):
                b, t, h = ITEMS[i]
                w = WIDTH[t]
                name = ("S", i)
                fill_begin(pe, name)
                dst = job_bank(name)[:, 0:w]
                if b == 0:
                    ins = mm(dst, qaT[0:HD + 1, h, t * P:(t + 1) * P], kaT[0:HD + 1, h, 0:w], start=True,
                             stop=True)
                else:
                    if h == 0:
                        for n in range(2):
                            wait_emptied(pe, ("qT", t, n))
                    ins = mm(dst, qcat[0:QK, h, t * P:(t + 1) * P], kcat[0:QK, h, 0:w], start=True,
                             stop=True)
                fill_end(ins, name)

            def transposed(i):
                b, t, h = ITEMS[i]
                name = ("PT", i)
                fill_begin(pe, name)
                pe.wait_ge(s_pn, i + 1)
                for k in range(t + 1):
                    tr(job_bank(name)[:, k * P:(k + 1) * P], pr[:, i % 3, META + k * P:META + (k + 1) * P],
                       ident)
                fill_end(tr(job_bank(name)[0:META, 256:384], pr[:, i % 3, 0:META], ident), name)

            def values(j):
                b, t, h = ITEMS[2 * j]
                n = 2 * b + t
                if h == 0 and n >= 2:
                    pe.wait_ge(s_on, n - 1)
                if j == 8:
                    for m in range(3):
                        wait_emptied(pe, ("vb", m))
                for u in range(2):
                    wait_emptied(pe, ("PT", 2 * j + u))
                vv = vb if b else va
                for k in list(range(t + 1)) + [2]:
                    rows = META if k == 2 else P
                    for u in range(2):
                        ins = mm(bank[6 + n % 2][u * HD:(u + 1) * HD, (h // 2) * P:(h // 2 + 1) * P],
                                 vv[0:rows, k, (h + u) * HD:(h + u + 1) * HD],
                                 pT[0:rows, (2 * j + u) % 4, k, :], start=k == 0, stop=k == 2)
                ins.then_inc(s_pv, 1)

            def branch_block(kind, m):
                b, src, s0 = (0, oaT, 16) if kind == "ba" else (1, obT, 18)
                name = (kind, m)
                fill_begin(pe, name)
                pe.wait_ge(s_on, 2 * b + 2)
                for k in range(2):
                    for c in range(4):
                        if c % 2 == 0:
                            loaded(s0 + c // 2)
                        w = slot(s0 + c // 2).rearrange("p (k n) -> p k n", k=2)[:, c % 2, :]
                        ins = mm(job_bank(name)[:, k * SEQ:(k + 1) * SEQ],
                                 w[:, (2 * m + k) * P:(2 * m + k + 1) * P], src[:, c, :],
                                 start=c == 0, stop=c == 3)
                fill_end(ins, name)

            for i in range(len(ITEMS) + 3):
                if i < len(ITEMS):
                    scores(i)
                if i >= 4 and i % 2 == 0:
                    if i == len(ITEMS) + 2:
                        branch_block("ba", 0)
                    values(i // 2 - 2)
                if 2 <= i < len(ITEMS) + 2:
                    transposed(i - 2)
                if i % 2 == 1 and i < len(ITEMS):
                    m = i // 2
                    name = ("gate", m)
                    fill_begin(pe, name)
                    loaded(8 + m // 2)
                    for c in range(CH):
                        ins = mm(job_bank(name)[:, 0:SEQ], win(8 + m // 2)[:, c, (m % 2) * P:(m % 2 + 1) * P],
                                 xnT[:, c, META:KEYS], start=c == 0, stop=c == CH - 1)
                    fill_end(ins, name)
            for m in range(1, 4):
                branch_block("ba", m)
            for m in range(4):
                branch_block("bb", m)

            def project(t, n, c0, c1):
                name = ("out", t, n)
                if c0 == 0:
                    fill_begin(pe, name)
                for c in range(c0, c1):
                    if t == 0 and n == 0 and c % 2 == 0:
                        pe.wait_ge(s_mg, c // 2 + 1)
                        loaded(20 + c // 2)
                    w = slot(20 + c // 2).rearrange("p (k n) -> p k n", k=2)[:, c % 2, :]
                    ins = mm(job_bank(name), gaS[:, c, t * P:(t + 1) * P], w[:, n * 512:(n + 1) * 512],
                             start=c == 0, stop=c == CH - 1)
                if c1 == CH:
                    fill_end(ins, name)
                return ins

            def residual_features(t, n):
                name = ("hT", t, n)
                fill_begin(pe, name)
                wait_emptied(pe, ("out", t, n))
                for c in range(4):
                    ins = tr(job_bank(name)[:, c * P:(c + 1) * P],
                             h1[:, t * D + (4 * n + c) * P:t * D + (4 * n + c + 1) * P], ident)
                fill_end(ins, name)

            def route(t, n):
                wait_emptied(pe, ("hT", t, n))
                wrv = wr[:].rearrange("p (c e) -> p c e", c=CH)
                for c in range(4 * n, 4 * n + 4):
                    ins = mm(bank[7 - t][:, 0:EXPERTS], hT[:, c, t * P:(t + 1) * P], wrv[:, c, :],
                             start=c == 0, stop=c == CH - 1)
                if n == 1:
                    ins.then_inc(s_rt, 1)

            def gather(k):
                for c in range(4):
                    for t in range(2):
                        ins = mm(bank[k][:, c * P:(c + 1) * P], hs[:, t, (4 * k + c) * P:(4 * k + c + 1) * P],
                                 pick[:, t, :], start=t == 0, stop=t == 1)
                ins.then_inc(s_gath, 1)

            def gather_first(t, k):
                for c in range(4):
                    ins = mm(bank[k][:, c * P:(c + 1) * P], hs[:, t, (4 * k + c) * P:(4 * k + c + 1) * P],
                             pick[:, t, :], start=t == 0 and c == 0, stop=t == 1 and c == 3)
                if t == 1:
                    ins.then_inc(s_gath, 1)

            for t in range(2):
                for n in range(2):
                    ins = project(t, n, 0, 4)
            ins.then_inc(s_half, 1)
            project(0, 0, 4, 8)
            project(0, 1, 4, 6)
            residual_features(0, 0)
            project(0, 1, 6, 8)
            project(1, 0, 4, 6)
            residual_features(0, 1)
            project(1, 0, 6, 8)
            project(1, 1, 4, 6)
            pe.wait_ge(s_wr, 16)
            route(0, 0)
            route(0, 1)
            residual_features(1, 0)
            project(1, 1, 6, 8)
            def bias_features(m0):
                for m in range(m0, m0 + 8):
                    ins = tr(job_bank(("out", 1, 0))[:, m * EXPERTS:(m + 1) * EXPERTS], braw[:, m * P:(m + 1) * P],
                             ident[0:EXPERTS, 0:EXPERTS])
                return ins

            last_jobs = {JOB[name] % ROT: name for name in JOBS[-ROT:]}
            pe.wait_ge(s_bias, 16)
            wait_emptied(pe, ("out", 1, 0))
            bias_features(0)
            pe.wait_ge(s_mask, 1)
            mk = [rk[:, 192 + 32 * t:224 + 32 * t] for t in range(2)]
            rb = bank[7]
            mm(rb[:, 64:96], ltri, mk[0], start=True, stop=True)
            mm(rb[:, 96:160], ones, mk[0].unsqueeze(1).broadcast_to([P, 2, EXPERTS]), start=True,
               stop=False).then_inc(s_rank, 1)
            route(1, 0)
            residual_features(1, 1)
            pe.wait_ge(s_pick0, 1)
            pe.wait_ge(s_hs, 1)
            wait_emptied(pe, last_jobs[0])
            gather_first(0, 0)
            wait_emptied(pe, last_jobs[1])
            route(1, 1)
            gather_first(0, 1)
            pe.wait_ge(s_mask, 2)
            mm(rb[:, 96:128], ltri, mk[1], start=False, stop=False)
            mm(rb[:, 128:160], ones, mk[1], start=False, stop=True).then_inc(s_rank, 1)
            bias_features(8).then_inc(s_btf, 1)
            pe.wait_ge(s_pick0, 2)
            pe.wait_ge(s_hs, 2)
            gather_first(1, 0)
            pe.wait_ge(s_np, 1)
            n_pass = pe.value_load(npi[0:1, 0:1], min_val=1, max_val=SEQ // CAP)
            gather_first(1, 1)
            for n in range(2, ROT):
                wait_emptied(pe, last_jobs[n])

            def expert_pair(turn, u):
                g = turn * UNROLL + u
                base = PAIR_LOADS * u

                def arrived(k):
                    n = place(base + k)
                    before = MIX_LOADS // NSLOT if n < NSLOT else 0
                    pe.wait_ge(slot_loaded[n], turn * (16 * USES) + 16 * (before + (base + k) // ESLOT + 1))

                def features(e):
                    pe.wait_ge(s_gl, g * 2 + (e + 1))
                    for m in range(CH):
                        ins = tr(bank[6 + m // 4][:, (m % 4) * P:(m % 4 + 1) * P],
                                 gl[:, e, m * P:(m + 1) * P], ident)
                    ins.then_inc(s_tf, 1)

                for e in range(2):
                    for c in range(CH):
                        if e == 0 and c % 4 == 0:
                            pe.wait_ge(s_xg, g * 2 + (c // 4 + 1))
                        if e == 0 and c == 2:
                            pe.wait_ge(s_pick, g + 1)
                            for t in range(2):
                                ins = tr(bank[0][:, t * P:(t + 1) * P], pickg[:, t, :], ident)
                            ins.then_inc(s_pgf, 1)
                        if e == 1 and c == 0:
                            pe.wait_ge(s_pick, g + 2)
                        k = 8 * e + c
                        arrived(k)
                        for n in range(2):
                            for h in range(2):
                                ins = mm(bank[2 + 2 * e + n][h * CAP:(h + 1) * CAP, :],
                                         xg[:, c, e * CAP:(e + 1) * CAP],
                                         eslot(base + k)[:, h * D + n * 512:h * D + (n + 1) * 512],
                                         start=c == 0, stop=c == CH - 1)
                        used(ins, base + k)
                        if e == 1 and c == 1:
                            features(0)
                        if e == 1 and c == 2:
                            for n in range(2):
                                for h in range(2):
                                    mm(bank[2 + n][h * CAP:(h + 1) * CAP, :],
                                       which[:, h * CAP:(h + 1) * CAP],
                                       bdn[:, n * 512:(n + 1) * 512], start=True, stop=False)
                pe.wait_ge(s_pgt, g + 1)
                gather(0)
                pe.wait_ge(s_act, g * 2 + 1)
                features(1)
                gather(1)
                pe.wait_ge(s_act, g * 2 + 2)
                for c, n in [(c, n) for c in range(CH) for n in range(2)]:
                    for e in range(2):
                        k = 16 + 2 * (c // 2) + e
                        if c % 2 == 0 and n == 0:
                            arrived(k)
                        if c == CH - 1 and n == 0:
                            pe.wait_ge(last_half[e], g * 16 + 16)
                        ins = mm(bank[2 + n][e * CAP:(e + 1) * CAP, :], act[:, e, c * CAP:(c + 1) * CAP],
                                 eslot(base + k)[:, (c % 2) * D + n * 512:(c % 2) * D + (n + 1) * 512],
                                 start=False, stop=c == CH - 1)
                        if c % 2 and n:
                            used(ins, base + k)
                    if c == CH - 1 and n == 0:
                        ins.then_inc(s_dn0, 1)
                for t in range(2):
                    for n in range(2):
                        pe.wait_ge(s_y, g * 2 + (n + 1))
                        ins = mm(bank[4 + 2 * t + n], pickgT[:, t * P:(t + 1) * P],
                                 yr[:, n * 512:(n + 1) * 512], start=True, stop=True)
                    ins.then_inc(s_sc, 1)

            pe.wait_ge(s_bT, 1)
            pe.wait_ge(s_bdn, 16)
            with pe.Fori(0, n_pass) as b:
                with pe.Fori(0, TURNS) as j:
                    turn = pe.snap(b * TURNS + j)
                    for u in range(UNROLL):
                        expert_pair(turn, u)


_INS = ['x', 'meta_tokens', 'w_in', 'b_forget', 'w_uq', 'w_uk', 'w_uv', 'w_qidx', 'kidx_ln_g', 'kidx_ln_b',
        'w_branch_a', 'w_branch_b', 'w_out', 'norm_mix_g', 'norm_ffn_g', 'q_norm_g', 'kv_norm_g',
        'w_router', 'b_router', 'w_gate_up', 'b_gate_up', 'w_down', 'b_down', 'norm_final_g']


def _constants(np):
    k = np.zeros((P, KCOLS), np.float32)
    r = np.arange(P)
    k[:, K_ID:K_ID + P] = np.eye(P)
    k[:, K_LT:K_LT + P] = r[:, None] < r[None, :]
    k[:, K_ONE:K_ONE + P] = 1.0
    k[:, K_FM + KEYS - P:K_FM + KEYS] = np.where(r[None, :] > r[:, None], NEG, 0.0)
    k[0:64, K_CM + KEYS - 64:K_CM + KEYS] = NEG
    k[:, K_IOTA:K_IOTA + CAP] = RANK0 + np.arange(CAP)
    k[:, K_THR:K_THR + SEQ // CAP] = CAP * np.arange(SEQ // CAP) - (np.arange(SEQ // CAP) == 0)
    half = ROPE // 2
    inv = (np.float32(10000.0) ** (-np.arange(half, dtype=np.float32) / np.float32(half))).astype(np.float32)
    for t, (rows, col) in enumerate(TILES):
        ang = ((col + r).astype(np.float32)[:, None] * inv[None, :]).astype(np.float32)
        k[:, K_COS + half * t:K_COS + half * (t + 1)] = np.cos(ang.astype(np.float64))
        k[:, K_SIN + half * t:K_SIN + half * (t + 1)] = np.sin(ang.astype(np.float64))
    return k


def kernel(**inputs):
    import numpy as _np
    import concourse.bacc as _bacc
    from concourse import mybir as _mybir
    from concourse.bass_utils import run_bass_kernel_spmd as _run

    nc = _bacc.Bacc("TRN2", target_bir_lowering=False, num_devices=1)
    arrays, aps = {}, {}
    for name in _INS:
        a = _np.ascontiguousarray(inputs[name])
        arrays[f"in_{name}"] = a
        aps[name] = nc.dram_tensor(f"in_{name}", a.shape, _mybir.dt.from_np(a.dtype), kind="ExternalInput").ap()
    consts = _constants(_np)
    arrays["consts"] = consts
    aps["consts"] = nc.dram_tensor("consts", consts.shape, _mybir.dt.float32, kind="ExternalInput").ap()
    out = nc.dram_tensor("out", (1, SEQ, D), _mybir.dt.float32, kind="ExternalOutput").ap()
    a = aps
    build(nc, a['x'], a['meta_tokens'], a['w_in'], a['b_forget'], a['w_uq'], a['w_uk'], a['w_uv'],
          a['w_qidx'], a['kidx_ln_g'], a['kidx_ln_b'], a['w_branch_a'], a['w_branch_b'], a['w_out'],
          a['norm_mix_g'], a['norm_ffn_g'], a['q_norm_g'], a['kv_norm_g'], a['w_router'], a['b_router'],
          a['w_gate_up'], a['b_gate_up'], a['w_down'], a['b_down'], a['norm_final_g'], a['consts'], out)
    r = _run(nc, [arrays], core_ids=[0])
    return r.results[0]["out"]
```
